# Optimizing a Trainium2 kernel written in Bass

```python
import jax
import jax.numpy as jnp
from jax import lax
import numpy as np

D_MODEL = 1024
BATCH = 1
SEQ = 256
DEPTH = 1

CTX_LEN = 256
GRID_W = 64

POOL_GROUPS = 4
POOL_GROUP_DIM = D_MODEL // 16
POOL_WIDTH = POOL_GROUPS * POOL_GROUP_DIM
POOL_WINDOWS = (2, 4, 8, 16)

MLSTM_HEADS = 4
MLSTM_HEAD_DIM = D_MODEL // 8
MLSTM_WIDTH = MLSTM_HEADS * MLSTM_HEAD_DIM
MLSTM_CHUNK = 128
QK_CONV_WIDTH = 3

SGU_GROUPS = 4
SGU_GROUP_DIM = D_MODEL // 16
SGU_WIDTH = SGU_GROUPS * SGU_GROUP_DIM
SGU_CHUNK = 128

N_BRANCH = 3
IN_SPLIT_SIZES = (POOL_WIDTH, 2 * MLSTM_WIDTH, MLSTM_WIDTH, MLSTM_WIDTH, 4 * MLSTM_HEADS, 2 * SGU_WIDTH, N_BRANCH * D_MODEL)
IN_COLS = sum(IN_SPLIT_SIZES)
MLSTM_GATE_OFF = POOL_WIDTH + 4 * MLSTM_WIDTH

N_EXPERTS = 32
TOP_K = 4
D_FF = D_MODEL
SWIGLU_LIMIT = 7.0
SWIGLU_ALPHA = 1.702

LN_EPS = 1e-5
HEAD_NORM_EPS = 1e-6
DEEPNORM_ALPHA = (2 * DEPTH) ** 0.25
DEEPNORM_BETA = (8 * DEPTH) ** -0.25


def layer_norm_plain(x):
    xf = x.astype(jnp.float32)
    mu = xf.mean(-1, keepdims=True)
    var = jnp.square(xf - mu).mean(-1, keepdims=True)
    return ((xf - mu) * lax.rsqrt(var + LN_EPS)).astype(x.dtype)

def layer_norm(x, g, b):
    return layer_norm_plain(x) * g + b

def modulate(h, shift, scale):
    return h * (1 + scale) + shift

def split_in(z):
    idx = [int(s) for s in np.cumsum(IN_SPLIT_SIZES)[:-1]]
    return jnp.split(z, idx, axis=-1)

def centred_box_mean(x, window):
    length = x.shape[-2]
    xf = x.astype(jnp.float32)
    prefix = jnp.concatenate([jnp.zeros_like(xf[..., :1, :]), jnp.cumsum(xf, axis=-2)], axis=-2)
    t = jnp.arange(length)
    lo = jnp.clip(t - window // 2, 0, length)
    hi = jnp.clip(t + window // 2, 0, length)
    s = jnp.take(prefix, hi, axis=-2) - jnp.take(prefix, lo, axis=-2)
    cnt = (hi - lo).astype(jnp.float32)[:, None]
    return (s / cnt).astype(x.dtype)

def pool_mixer(xp, w_lin, scale):
    grp = xp.reshape(xp.shape[:-1] + (POOL_GROUPS, POOL_GROUP_DIM))
    pooled = jnp.stack([centred_box_mean(grp[..., g, :], w) for g, w in enumerate(POOL_WINDOWS)], axis=-2)
    y = jnp.einsum('...lgc,gcd->...lgd', pooled - grp, w_lin)
    return y.reshape(xp.shape) * scale

def dwconv_centred(x, w, b):
    k = w.shape[0]
    length = x.shape[1]
    left = k // 2
    xp = jnp.pad(x, ((0, 0), (left, k - 1 - left), (0, 0)))
    y = b
    for j in range(k):
        y = y + xp[:, j:j + length, :] * w[j]
    return y

def mlstm_prepare(qk, v, gates, conv_w, conv_b):
    qk = jax.nn.silu(dwconv_centred(qk, conv_w, conv_b))
    q, k = jnp.split(qk, 2, axis=-1)
    b, length, _ = v.shape

    def heads(a):
        return a.reshape(b, length, MLSTM_HEADS, MLSTM_HEAD_DIM).transpose(0, 2, 1, 3).astype(jnp.float32)

    g = gates.astype(jnp.float32).reshape(b, length, 4, MLSTM_HEADS).transpose(2, 0, 3, 1)
    return heads(q), heads(k) * MLSTM_HEAD_DIM ** -0.5, heads(v), g

def mlstm_chunk_scan(q, k, v, log_i, log_f, state):
    b, h, length, dh = q.shape
    nc = length // MLSTM_CHUNK
    lower = jnp.tril(jnp.ones((MLSTM_CHUNK, MLSTM_CHUNK), dtype=bool))

    def chunks(a):
        return jnp.moveaxis(a.reshape((b, h, nc, MLSTM_CHUNK) + a.shape[3:]), 2, 0)

    def step(carry, xs):
        c_mat, n_vec, m = carry
        qc, kc, vc, ic, fc = xs
        bcum = jnp.cumsum(fc, axis=-1)
        dmat = jnp.where(lower, bcum[..., :, None] - bcum[..., None, :] + ic[..., None, :], -jnp.inf)
        inter = bcum + m[..., None]
        m_t = jnp.maximum(inter, dmat.max(-1))
        decay = jnp.exp(inter - m_t)
        scores = jnp.einsum('bhtd,bhsd->bhts', qc, kc) * jnp.exp(dmat - m_t[..., None])
        num = decay[..., None] * jnp.einsum('bhvk,bhtk->bhtv', c_mat, qc) + jnp.einsum('bhts,bhsv->bhtv', scores, vc)
        den = decay * jnp.einsum('bhk,bhtk->bht', n_vec, qc) + scores.sum(-1)
        out = num / jnp.maximum(jnp.abs(den), jnp.exp(-m_t))[..., None]
        total = bcum[..., -1]
        wlog = total[..., None] - bcum + ic
        m_new = jnp.maximum(total + m, wlog.max(-1))
        a = jnp.exp(total + m - m_new)
        wk = jnp.exp(wlog - m_new[..., None])
        c_new = a[..., None, None] * c_mat + jnp.einsum('bhsv,bhsk->bhvk', vc * wk[..., None], kc)
        n_new = a[..., None] * n_vec + jnp.einsum('bhs,bhsk->bhk', wk, kc)
        return (c_new, n_new, m_new), out

    state, hs = lax.scan(step, state, tuple(chunks(a) for a in (q, k, v, log_i, log_f)))
    return jnp.moveaxis(hs, 0, 2).reshape(b, h, length, dh), state

def mlstm_bidirectional(ctx_in, lat_in):
    qc, kc, vc, gc = ctx_in
    ql, kl, vl, gl = lat_in
    b = qc.shape[0]
    zero = (jnp.zeros((b, MLSTM_HEADS, MLSTM_HEAD_DIM, MLSTM_HEAD_DIM), jnp.float32),
            jnp.zeros((b, MLSTM_HEADS, MLSTM_HEAD_DIM), jnp.float32),
            jnp.zeros((b, MLSTM_HEADS), jnp.float32))
    ls = jax.nn.log_sigmoid
    hc_f, st_f = mlstm_chunk_scan(qc, kc, vc, gc[0], ls(gc[1]), zero)
    hl_f, _ = mlstm_chunk_scan(ql, kl, vl, gl[0], ls(gl[1]), st_f)
    fs = lambda a: jnp.flip(a, axis=2)
    fg = lambda a: jnp.flip(a, axis=-1)
    hc_b, st_b = mlstm_chunk_scan(fs(qc), fs(kc), fs(vc), fg(gc[2]), ls(fg(gc[3])), zero)
    hl_b, _ = mlstm_chunk_scan(fs(ql), fs(kl), fs(vl), fg(gl[2]), ls(fg(gl[3])), st_b)
    return hc_f + fs(hc_b), hl_f + fs(hl_b)

def mlstm_output(h, o, norm_g):
    b, _, length, _ = h.shape
    mu = h.mean(-1, keepdims=True)
    var = jnp.square(h - mu).mean(-1, keepdims=True)
    hn = ((h - mu) * lax.rsqrt(var + HEAD_NORM_EPS)).transpose(0, 2, 1, 3).reshape(b, length, MLSTM_WIDTH)
    return (hn * norm_g * jax.nn.sigmoid(o.astype(jnp.float32))).astype(o.dtype)

def sgu_mixer(uv, ln_g, ln_b, w_s, b_s):
    u, v = jnp.split(jax.nn.gelu(uv, approximate=False), 2, axis=-1)
    v = layer_norm(v, ln_g, ln_b)
    b, length, _ = v.shape
    vc = v.reshape(b, length // SGU_CHUNK, SGU_CHUNK, SGU_GROUPS, SGU_GROUP_DIM)
    mixed = jnp.einsum('gts,bnsgc->bntgc', w_s, vc) + b_s.T[:, :, None]
    return u * mixed.reshape(b, length, SGU_WIDTH)

def branch_merge(pool_o, mlstm_o, sgu_o, gate_pre, w_bp, w_bm, w_bs, w_o):
    g = jax.nn.sigmoid(gate_pre.astype(jnp.float32)).astype(pool_o.dtype)
    g_p, g_m, g_s = jnp.split(g, N_BRANCH, axis=-1)
    y = g_p * (pool_o @ w_bp) + g_m * (mlstm_o @ w_bm) + g_s * (sgu_o @ w_bs)
    return y @ w_o

def moe_ffn(h, w_router, b_router, w_gate_up, b_gate_up, w_down, b_down):
    logits = (h @ w_router + b_router).astype(jnp.float32)
    top_val, top_idx = lax.top_k(logits, TOP_K)
    probs = jax.nn.softmax(top_val, axis=-1)
    combine = jnp.einsum('nk,nke->en', probs, jax.nn.one_hot(top_idx, N_EXPERTS, dtype=jnp.float32)).astype(h.dtype)

    def expert(acc, xs):
        wgu, bgu, wd, bd, cw = xs
        gate, up = jnp.split(h @ wgu + bgu, 2, axis=-1)
        gate = jnp.minimum(gate, SWIGLU_LIMIT)
        up = jnp.clip(up, -SWIGLU_LIMIT, SWIGLU_LIMIT)
        glu = gate * jax.nn.sigmoid(SWIGLU_ALPHA * gate)
        y = ((up + 1) * glu) @ wd + bd
        return acc + cw[:, None] * y, None

    out, _ = lax.scan(expert, jnp.zeros_like(h), (w_gate_up, b_gate_up, w_down, b_down, combine))
    return out

def first_inputs(seed: int = 0) -> dict:
    key = jax.random.key(seed)
    ks = iter(jax.random.split(key, 40))

    def nrm(shape, scale):
        return scale * jax.random.normal(next(ks), shape, jnp.float32)

    L, D, E, F = DEPTH, D_MODEL, N_EXPERTS, D_FF
    f_bias = jnp.linspace(3.0, 6.0, MLSTM_HEADS, dtype=jnp.float32)
    b_in = nrm((L, IN_COLS), 0.02)
    b_in = b_in.at[:, MLSTM_GATE_OFF + MLSTM_HEADS:MLSTM_GATE_OFF + 2 * MLSTM_HEADS].add(f_bias)
    b_in = b_in.at[:, MLSTM_GATE_OFF + 3 * MLSTM_HEADS:MLSTM_GATE_OFF + 4 * MLSTM_HEADS].add(f_bias)
    return {
        'x': nrm((BATCH, SEQ, D), 1.0),
        'c': nrm((BATCH, D), 1.0),
        'ctx': nrm((BATCH, CTX_LEN, D), 1.0),
        'c_ctx': nrm((D,), 1.0),
        'w_ada': nrm((L, D, 6 * D), 0.5 * D ** -0.5),
        'b_ada': nrm((L, 6 * D), 0.02),
        'w_in': nrm((L, D, IN_COLS), D ** -0.5),
        'b_in': b_in,
        'pool_w': nrm((L, POOL_GROUPS, POOL_GROUP_DIM, POOL_GROUP_DIM), POOL_GROUP_DIM ** -0.5),
        'pool_scale': 1.0 + nrm((L, POOL_WIDTH), 0.02),
        'qk_conv_w': nrm((L, QK_CONV_WIDTH, 2 * MLSTM_WIDTH), QK_CONV_WIDTH ** -0.5),
        'qk_conv_b': nrm((L, 2 * MLSTM_WIDTH), 0.02),
        'mlstm_norm_g': 1.0 + nrm((L, MLSTM_WIDTH), 0.02),
        'sgu_ln_g': 1.0 + nrm((L, SGU_WIDTH), 0.02),
        'sgu_ln_b': nrm((L, SGU_WIDTH), 0.02),
        'sgu_w': nrm((L, SGU_GROUPS, SGU_CHUNK, SGU_CHUNK), SGU_CHUNK ** -0.5),
        'sgu_b': 1.0 + nrm((L, SGU_GROUPS, SGU_CHUNK), 0.02),
        'w_br_pool': nrm((L, POOL_WIDTH, D), POOL_WIDTH ** -0.5),
        'w_br_mlstm': nrm((L, MLSTM_WIDTH, D), MLSTM_WIDTH ** -0.5),
        'w_br_sgu': nrm((L, SGU_WIDTH, D), SGU_WIDTH ** -0.5),
        'w_out': nrm((L, D, D), DEEPNORM_BETA * D ** -0.5),
        'ln1_g': 1.0 + nrm((L, D), 0.02),
        'ln1_b': nrm((L, D), 0.02),
        'w_router': nrm((L, D, E), D ** -0.5),
        'b_router': nrm((L, E), 0.01),
        'w_gate_up': nrm((L, E, D, 2 * F), D ** -0.5),
        'b_gate_up': nrm((L, E, 2 * F), 0.02),
        'w_down': nrm((L, E, F, D), DEEPNORM_BETA * F ** -0.5),
        'b_down': nrm((L, E, D), 0.02),
        'ln2_g': 1.0 + nrm((L, D), 0.02),
        'ln2_b': nrm((L, D), 0.02),
    }

def first_block(x, c, ctx, c_ctx, w_ada, b_ada, w_in, b_in, pool_w, pool_scale, qk_conv_w, qk_conv_b,
              mlstm_norm_g, sgu_ln_g, sgu_ln_b, sgu_w, sgu_b, w_br_pool, w_br_mlstm, w_br_sgu, w_out,
              ln1_g, ln1_b, w_router, b_router, w_gate_up, b_gate_up, w_down, b_down, ln2_g, ln2_b):
    B, S, D = x.shape
    rows = S // GRID_W
    xl, xc = x, ctx
    for i in range(DEPTH):
        last = i == DEPTH - 1
        sh1_l, sc1_l, g1_l, sh2_l, sc2_l, g2_l = [
            m[:, None, :] for m in jnp.split(jax.nn.silu(c) @ w_ada[i] + b_ada[i], 6, axis=-1)]
        sh1_c, sc1_c, g1_c, sh2_c, sc2_c, g2_c = jnp.split(jax.nn.silu(c_ctx) @ w_ada[i] + b_ada[i], 6, axis=-1)

        z_l = modulate(layer_norm_plain(xl), sh1_l, sc1_l) @ w_in[i] + b_in[i]
        z_c = modulate(layer_norm_plain(xc), sh1_c, sc1_c) @ w_in[i] + b_in[i]
        p_l, qk_l, v_l, o_l, gt_l, uv_l, mg_l = split_in(z_l)
        p_c, qk_c, v_c, o_c, gt_c, uv_c, mg_c = split_in(z_c)

        hm_c, hm_l = mlstm_bidirectional(
            mlstm_prepare(qk_c, v_c, gt_c, qk_conv_w[i], qk_conv_b[i]),
            mlstm_prepare(qk_l, v_l, gt_l, qk_conv_w[i], qk_conv_b[i]))
        merge_w = (w_br_pool[i], w_br_mlstm[i], w_br_sgu[i], w_out[i])
        moe_w = (w_router[i], b_router[i], w_gate_up[i], b_gate_up[i], w_down[i], b_down[i])

        y_l = branch_merge(
            pool_mixer(p_l.reshape(B, rows, GRID_W, POOL_WIDTH), pool_w[i], pool_scale[i]).reshape(B, S, POOL_WIDTH),
            mlstm_output(hm_l, o_l, mlstm_norm_g[i]),
            sgu_mixer(uv_l, sgu_ln_g[i], sgu_ln_b[i], sgu_w[i], sgu_b[i]),
            mg_l, *merge_w)
        xl = layer_norm(DEEPNORM_ALPHA * xl + g1_l * y_l, ln1_g[i], ln1_b[i])
        h_l = modulate(layer_norm_plain(xl), sh2_l, sc2_l).reshape(B * S, D)

        if last:
            f_l = moe_ffn(h_l, *moe_w)
        else:
            y_c = branch_merge(
                pool_mixer(p_c, pool_w[i], pool_scale[i]),
                mlstm_output(hm_c, o_c, mlstm_norm_g[i]),
                sgu_mixer(uv_c, sgu_ln_g[i], sgu_ln_b[i], sgu_w[i], sgu_b[i]),
                mg_c, *merge_w)
            xc = layer_norm(DEEPNORM_ALPHA * xc + g1_c * y_c, ln1_g[i], ln1_b[i])
            h_c = modulate(layer_norm_plain(xc), sh2_c, sc2_c).reshape(-1, D)
            f_all = moe_ffn(jnp.concatenate([h_l, h_c], axis=0), *moe_w)
            f_l, f_c = f_all[:B * S], f_all[B * S:]
            xc = layer_norm(DEEPNORM_ALPHA * xc + g2_c * f_c.reshape(xc.shape), ln2_g[i], ln2_b[i])
        xl = layer_norm(DEEPNORM_ALPHA * xl + g2_l * f_l.reshape(B, S, D), ln2_g[i], ln2_b[i])
    return xl


_first_inputs = first_inputs


def first_inputs(seed=0):
    import zlib

    import numpy as np

    out = dict(_first_inputs(seed))
    spreads = {}
    factors = {'ctx': 5.889,
     'c_ctx': 3.459,
     'b_ada': 3.993,
     'pool_scale': 42.378,
     'qk_conv_w': 3.312,
     'qk_conv_b': 64.0,
     'mlstm_norm_g': 64.0,
     'sgu_ln_g': 51.91,
     'sgu_ln_b': 58.725,
     'sgu_b': 54.137,
     'b_router': 8.0,
     'b_gate_up': 26.172,
     'b_down': 8.0,
     'ln2_g': 8.672,
     'ln2_b': 8.105}
    for name, (base, spread) in spreads.items():
        noise = np.random.default_rng([zlib.crc32(name.encode()), seed]).standard_normal(out[name].shape)
        drawn = base * np.exp(spread * noise) if base else spread * noise
        out[name] = jnp.asarray(drawn.astype(out[name].dtype))
    for name, factor in factors.items():
        out[name] = (out[name] * factor).astype(out[name].dtype)
    return out


_narrow_inputs = first_inputs


def first_inputs(seed=0):

    out = dict(_narrow_inputs(seed))
    wider = {'pool_scale': 4.71,
     'mlstm_norm_g': 4.8,
     'sgu_ln_g': 4.97,
     'sgu_ln_b': 5.23,
     'sgu_b': 5.49,
     'ln2_g': 3.37,
     'ln2_b': 3.33}
    for name, times in wider.items():
        mean = out[name].mean()
        out[name] = (mean + times * (out[name] - mean)).astype(out[name].dtype)
    return out


DEPTH_2 = 2

CHUNK = 64
Q_BLOCK = 128
MEM_LEN = 256

MLA_HEADS = 8
QK_NOPE_DIM = 64
QK_ROPE_DIM = 32
V_HEAD_DIM = 64
Q_LORA_RANK = 256
KV_LORA_RANK = 256
MLA_WIDTH = MLA_HEADS * V_HEAD_DIM
CONV_WIDTH = D_MODEL - MLA_WIDTH
CONV_TAPS = 31
IN_COLS_2 = Q_LORA_RANK + KV_LORA_RANK + QK_ROPE_DIM + 2 * CONV_WIDTH

XA_HEADS = 4
XA_HEAD_DIM = D_MODEL // XA_HEADS

FFN_HIDDEN = ((8 * D_MODEL + 3 * 256 - 1) // (3 * 256)) * 256

ALPHA = (2.0 * DEPTH_2) ** 0.25
BETA = (8.0 * DEPTH_2) ** -0.25

ROPE_BASE = 10000.0
RMS_EPS = 1e-6


def layer_norm_2(x, g, b):
    xf = x.astype(jnp.float32)
    mu = jnp.mean(xf, axis=-1, keepdims=True)
    var = jnp.mean(jnp.square(xf - mu), axis=-1, keepdims=True)
    y = (xf - mu) * lax.rsqrt(var + LN_EPS)
    return (y * g.astype(jnp.float32) + b.astype(jnp.float32)).astype(x.dtype)

def rms_norm(x, g):
    xf = x.astype(jnp.float32)
    y = xf * lax.rsqrt(jnp.mean(jnp.square(xf), axis=-1, keepdims=True) + RMS_EPS)
    return (y * g.astype(jnp.float32)).astype(x.dtype)

def rope_cos_sin(positions, dim):
    inv_freq = ROPE_BASE ** (-jnp.arange(0, dim, 2, dtype=jnp.float32) / dim)
    ang = positions.astype(jnp.float32)[..., None] * inv_freq
    return jnp.cos(ang), jnp.sin(ang)

def apply_rope(x, cos, sin):
    half = x.shape[-1] // 2
    x1 = x[..., :half].astype(jnp.float32)
    x2 = x[..., half:].astype(jnp.float32)
    return jnp.concatenate([x1 * cos - x2 * sin, x1 * sin + x2 * cos], axis=-1).astype(x.dtype)

def mla_group(c_q, c_kv, k_r, cos, sin, q_norm_g, w_uq, kv_norm_g, w_ukv):
    B, S, _ = c_q.shape
    q = (rms_norm(c_q, q_norm_g) @ w_uq).reshape(B, S, MLA_HEADS, QK_NOPE_DIM + QK_ROPE_DIM)
    q_nope, q_rope = q[..., :QK_NOPE_DIM], q[..., QK_NOPE_DIM:]
    q_rope = apply_rope(q_rope, cos[:, :, None, :], sin[:, :, None, :])
    kv = (rms_norm(c_kv, kv_norm_g) @ w_ukv).reshape(B, S, MLA_HEADS, QK_NOPE_DIM + V_HEAD_DIM)
    k_nope, v = kv[..., :QK_NOPE_DIM], kv[..., QK_NOPE_DIM:]
    k_rope = apply_rope(k_r, cos, sin)
    scale = (QK_NOPE_DIM + QK_ROPE_DIM) ** -0.5
    outs = []
    for start in range(0, S, Q_BLOCK):
        end = start + Q_BLOCK
        s = (jnp.einsum('bqhd,bkhd->bhqk', q_nope[:, start:end], k_nope[:, :end])
             + jnp.einsum('bqhr,bkr->bhqk', q_rope[:, start:end], k_rope[:, :end]))
        q_chunk = jnp.arange(start, end) // CHUNK
        k_chunk = jnp.arange(end) // CHUNK
        mask = k_chunk[None, :] <= q_chunk[:, None]
        s = jnp.where(mask[None, None], s.astype(jnp.float32) * scale, -jnp.inf)
        p = jax.nn.softmax(s, axis=-1).astype(v.dtype)
        outs.append(jnp.einsum('bhqk,bkhd->bqhd', p, v[:, :end]))
    o = jnp.concatenate(outs, axis=1)
    return o.reshape(B, S, MLA_WIDTH)

def conformer_conv_group(u, dw_w, dw_b, norm_g, norm_b):
    a, g = jnp.split(u, 2, axis=-1)
    h = a * jax.nn.sigmoid(g)
    h = jnp.pad(h, ((0, 0), (CONV_TAPS - 1, 0), (0, 0)))
    h = lax.conv_general_dilated(
        h, dw_w[:, None, :], window_strides=(1,), padding='VALID',
        dimension_numbers=('NWC', 'WIO', 'NWC'), feature_group_count=CONV_WIDTH) + dw_b
    h = layer_norm_2(h, norm_g, norm_b)
    return jax.nn.silu(h)

def hybrid_mixer(x, cos, sin, w_in, b_in, q_norm_g, w_uq, kv_norm_g, w_ukv,
                 dw_w, dw_b, cn_g, cn_b, w_o):
    proj = x @ w_in + b_in
    o1 = Q_LORA_RANK
    o2 = o1 + KV_LORA_RANK
    o3 = o2 + QK_ROPE_DIM
    c_q, c_kv, k_r, u = proj[..., :o1], proj[..., o1:o2], proj[..., o2:o3], proj[..., o3:]
    y_att = mla_group(c_q, c_kv, k_r, cos, sin, q_norm_g, w_uq, kv_norm_g, w_ukv)
    y_conv = conformer_conv_group(u, dw_w, dw_b, cn_g, cn_b)
    return jnp.concatenate([y_att, y_conv], axis=-1) @ w_o

def memory_cross_attention(x, mem, w_q, w_kv, w_o):
    B, S, D = x.shape
    M = mem.shape[1]
    q = (x @ w_q).reshape(B, S, XA_HEADS, XA_HEAD_DIM)
    kv = (mem @ w_kv).reshape(B, M, 2, XA_HEADS, XA_HEAD_DIM)
    k, v = kv[:, :, 0], kv[:, :, 1]
    s = jnp.einsum('bshd,bmhd->bhsm', q, k).astype(jnp.float32) * (XA_HEAD_DIM ** -0.5)
    p = jax.nn.softmax(s, axis=-1).astype(v.dtype)
    o = jnp.einsum('bhsm,bmhd->bshd', p, v).reshape(B, S, D)
    return o @ w_o

def swiglu_ffn(x, w_in, w_down):
    gu = x @ w_in
    g, up = gu[..., :FFN_HIDDEN], gu[..., FFN_HIDDEN:]
    return (jax.nn.silu(g) * up) @ w_down

def second_inputs(seed: int = 0) -> dict:
    key = jax.random.key(seed)
    ks = jax.random.split(key, 32)
    L, D = DEPTH_2, D_MODEL

    def normal(k, shape, fan_in, scale=1.0):
        return jax.random.normal(k, shape, jnp.float32) * (scale * fan_in ** -0.5)

    def gain(k, shape):
        return 1.0 + 0.02 * jax.random.normal(k, shape, jnp.float32)

    def small(k, shape):
        return 0.02 * jax.random.normal(k, shape, jnp.float32)

    x = jax.random.normal(ks[0], (BATCH, SEQ, D), jnp.float32)
    mem = jax.random.normal(ks[1], (BATCH, MEM_LEN, D), jnp.float32)
    offset = jax.random.randint(ks[2], (BATCH, 1), 0, 4096, dtype=jnp.int32)
    positions = offset + jnp.arange(SEQ, dtype=jnp.int32)[None, :]

    w_uk = normal(ks[7], (L, KV_LORA_RANK, MLA_HEADS, QK_NOPE_DIM), KV_LORA_RANK)
    w_uv = normal(ks[8], (L, KV_LORA_RANK, MLA_HEADS, V_HEAD_DIM), KV_LORA_RANK, BETA)
    mla_w_ukv = jnp.concatenate([w_uk, w_uv], axis=-1).reshape(
        L, KV_LORA_RANK, MLA_HEADS * (QK_NOPE_DIM + V_HEAD_DIM))
    xa_w_k = normal(ks[18], (L, D, D), D)
    xa_w_v = normal(ks[19], (L, D, D), D, BETA)
    xa_w_kv = jnp.concatenate([xa_w_k, xa_w_v], axis=-1)

    return {
        "x": x,
        "mem": mem,
        "positions": positions,
        "mix_w_in": normal(ks[3], (L, D, IN_COLS_2), D),
        "mix_b_in": small(ks[4], (L, IN_COLS_2)),
        "mla_q_norm": gain(ks[5], (L, Q_LORA_RANK)),
        "mla_w_uq": normal(ks[6], (L, Q_LORA_RANK, MLA_HEADS * (QK_NOPE_DIM + QK_ROPE_DIM)), Q_LORA_RANK),
        "mla_kv_norm": gain(ks[9], (L, KV_LORA_RANK)),
        "mla_w_ukv": mla_w_ukv,
        "conv_dw_w": normal(ks[10], (L, CONV_TAPS, CONV_WIDTH), CONV_TAPS),
        "conv_dw_b": small(ks[11], (L, CONV_WIDTH)),
        "conv_norm_g": gain(ks[12], (L, CONV_WIDTH)),
        "conv_norm_b": small(ks[13], (L, CONV_WIDTH)),
        "mix_w_o": normal(ks[14], (L, D, D), D, BETA),
        "ln1_g": gain(ks[15], (L, D)),
        "ln1_b": small(ks[16], (L, D)),
        "xa_w_q": normal(ks[17], (L, D, D), D),
        "xa_w_kv": xa_w_kv,
        "xa_w_o": normal(ks[20], (L, D, D), D, BETA),
        "ln2_g": gain(ks[21], (L, D)),
        "ln2_b": small(ks[22], (L, D)),
        "ffn_w_in": normal(ks[23], (L, D, 2 * FFN_HIDDEN), D),
        "ffn_w_down": normal(ks[24], (L, FFN_HIDDEN, D), FFN_HIDDEN, BETA),
        "ln3_g": gain(ks[25], (L, D)),
        "ln3_b": small(ks[26], (L, D)),
    }

def second_block(x, mem, positions, mix_w_in, mix_b_in, mla_q_norm, mla_w_uq, mla_kv_norm,
              mla_w_ukv, conv_dw_w, conv_dw_b, conv_norm_g, conv_norm_b, mix_w_o,
              ln1_g, ln1_b, xa_w_q, xa_w_kv, xa_w_o, ln2_g, ln2_b,
              ffn_w_in, ffn_w_down, ln3_g, ln3_b):
    cos, sin = rope_cos_sin(positions, QK_ROPE_DIM)
    for l in range(DEPTH_2):
        y = hybrid_mixer(x, cos, sin, mix_w_in[l], mix_b_in[l], mla_q_norm[l], mla_w_uq[l],
                         mla_kv_norm[l], mla_w_ukv[l], conv_dw_w[l], conv_dw_b[l],
                         conv_norm_g[l], conv_norm_b[l], mix_w_o[l])
        x = layer_norm_2(ALPHA * x + y, ln1_g[l], ln1_b[l])
        y = memory_cross_attention(x, mem, xa_w_q[l], xa_w_kv[l], xa_w_o[l])
        x = layer_norm_2(ALPHA * x + y, ln2_g[l], ln2_b[l])
        y = swiglu_ffn(x, ffn_w_in[l], ffn_w_down[l])
        x = layer_norm_2(ALPHA * x + y, ln3_g[l], ln3_b[l])
    return x


def setup_inputs(seed=0):
    out = dict(first_inputs(seed))
    for name, value in second_inputs(seed + 1).items():
        if name != "x":
            out[name + "_2"] = value
    return out


def reference(
    x, c, ctx, c_ctx, w_ada, b_ada, w_in, b_in, pool_w, pool_scale, qk_conv_w, qk_conv_b,
    mlstm_norm_g, sgu_ln_g, sgu_ln_b, sgu_w, sgu_b, w_br_pool, w_br_mlstm, w_br_sgu, w_out,
    ln1_g, ln1_b, w_router, b_router, w_gate_up, b_gate_up, w_down, b_down, ln2_g, ln2_b, mem_2,
    positions_2, mix_w_in_2, mix_b_in_2, mla_q_norm_2, mla_w_uq_2, mla_kv_norm_2, mla_w_ukv_2,
    conv_dw_w_2, conv_dw_b_2, conv_norm_g_2, conv_norm_b_2, mix_w_o_2, ln1_g_2, ln1_b_2,
    xa_w_q_2, xa_w_kv_2, xa_w_o_2, ln2_g_2, ln2_b_2, ffn_w_in_2, ffn_w_down_2, ln3_g_2, ln3_b_2,
):
    x = first_block(
        x, c, ctx, c_ctx, w_ada, b_ada, w_in, b_in, pool_w, pool_scale, qk_conv_w, qk_conv_b,
        mlstm_norm_g, sgu_ln_g, sgu_ln_b, sgu_w, sgu_b, w_br_pool, w_br_mlstm, w_br_sgu, w_out,
        ln1_g, ln1_b, w_router, b_router, w_gate_up, b_gate_up, w_down, b_down, ln2_g, ln2_b,
    )
    return second_block(
        x, mem_2, positions_2, mix_w_in_2, mix_b_in_2, mla_q_norm_2, mla_w_uq_2, mla_kv_norm_2,
        mla_w_ukv_2, conv_dw_w_2, conv_dw_b_2, conv_norm_g_2, conv_norm_b_2, mix_w_o_2, ln1_g_2,
        ln1_b_2, xa_w_q_2, xa_w_kv_2, xa_w_o_2, ln2_g_2, ln2_b_2, ffn_w_in_2, ffn_w_down_2,
        ln3_g_2, ln3_b_2,
    )


_drawn_inputs = setup_inputs


def setup_inputs(seed=0):
    import zlib

    import numpy as np

    out = dict(_drawn_inputs(seed))
    spreads = {}
    factors = {'mix_b_in_2': 8.0,
     'mla_q_norm_2': 8.0,
     'mla_w_uq_2': 3.424,
     'mla_kv_norm_2': 8.0,
     'conv_dw_b_2': 7.849,
     'conv_norm_g_2': 8.0,
     'conv_norm_b_2': 8.0}
    for name, (base, spread) in spreads.items():
        noise = np.random.default_rng([zlib.crc32(name.encode()), seed]).standard_normal(out[name].shape)
        drawn = base * np.exp(spread * noise) if base else spread * noise
        out[name] = jnp.asarray(drawn.astype(out[name].dtype))
    for name, factor in factors.items():
        out[name] = (out[name] * factor).astype(out[name].dtype)
    return out
```

```python
from contextlib import ExitStack

import numpy as np

import concourse.bass as bass
from concourse import mybir

F32 = mybir.dt.float32
I32 = mybir.dt.int32
ALU = mybir.AluOpType
ACT = mybir.ActivationFunctionType
AX = mybir.AxisListType
ALPHA1 = 2.0 ** 0.25
ALPHA2 = 4.0 ** 0.25
NEG = -1e30
NSLOT = 5
STEM = 640

CONST = {}
_at = 0
for _name, _w in (("ident", 128), ("maskf", 128), ("maskb", 128), ("zero", 128), ("maskc", 128), ("pool", 512), ("rot", 96),
                  ("freq", 1), ("sel", 1024), ("mean", 128), ("ones", 128), ("nhalf", 8)):
    CONST[_name] = (_at, _w)
    _at += _w
NCONST = _at


def constants():
    c = np.zeros((128, NCONST), np.float32)
    p = np.arange(128)

    def put(name, a):
        o, w = CONST[name]
        c[:a.shape[0], o:o + w] = a

    put("ident", np.eye(128))
    put("maskf", np.where(p[:, None] <= p[None, :], 0.0, NEG))
    put("maskb", np.where(p[:, None] >= p[None, :], 0.0, NEG))
    put("maskc", np.where((p[:, None] < 64) & (p[None, :] >= 64), NEG, 0.0))
    pool = np.zeros((128, 4, 128))
    for g, w in enumerate((2, 4, 8, 16)):
        for t in range(128):
            base, tt = t // 64 * 64, t % 64
            lo, hi = max(tt - w // 2, 0), min(tt + w // 2, 64)
            pool[base + lo:base + hi, g, t] += 1.0 / (hi - lo)
            pool[t, g, t] -= 1.0
    put("pool", pool.reshape(128, 512))
    rot = np.zeros((96, 96))
    freq = np.zeros((96, 1), np.float32)
    for i in range(16):
        rot[80 + i, 64 + i] = -1.0
        rot[64 + i, 80 + i] = 1.0
    inv = np.float32(10000.0) ** (-np.arange(0, 32, 2, dtype=np.float32) / np.float32(32))
    freq[64:80, 0] = inv
    freq[80:96, 0] = inv
    put("rot", rot)
    put("freq", freq)
    sel = np.zeros((64, 8, 128))
    for r in range(8):
        sel[32 * (r // 4) + r % 4, r, :] = 1.0
    put("sel", sel.reshape(64, 1024))
    put("mean", np.full((128, 128), 1.0 / 512))
    put("ones", np.ones((128, 128)))
    put("nhalf", np.full((128, 8), -0.5))
    return c


class Queue:

    def __init__(self, sems, serial=False):
        self.serial = serial
        self.sems, self.n, self.count, self.items = sems, 0, 0, []

    def __call__(self, fn, *args, w=(), inc=True, **kw):
        if self.serial and self.count:
            w = tuple(w) + (self.last(),)
        if self.count >= 1000:
            self.n += 1
            self.count = 0
        sem = self.sems[self.n] if inc else None
        self.items.append((w, fn, args, kw, sem, 1))
        if inc:
            self.count += 1
            return (sem, self.count)
        return None

    def last(self):
        return (self.sems[self.n], self.count)


def emit(eng, items):
    seen = {}

    def wait(w):
        if w is None:
            return
        if isinstance(w, list):
            for x in w:
                wait(x)
            return
        sem, value = w
        if seen.get(id(sem), 0) < value:
            eng.wait_ge(sem, value)
            seen[id(sem)] = value

    for w, fn, args, kw, sem, by in items:
        for x in w:
            wait(x)
        if fn is None:
            continue
        ins = fn(*args, **kw)
        if sem is not None:
            ins.then_inc(sem, by)


class Box:

    def __init__(self, t, sem=None):
        self.t, self.sem, self.n, self.free, self.ready = t, sem, 0, [], None
        self.pin, self.w = False, []


def build(nc, T, out):
    ctx = ExitStack()
    with ctx:
        def sb(name, shape, dt=F32):
            return ctx.enter_context(nc.sbuf_tensor(name, shape, dt))

        def sem(name):
            return ctx.enter_context(nc.semaphore(name))

        PE = Queue([sem(f"s_pe{i}") for i in range(6)])
        V = Queue([sem(f"s_v{i}") for i in range(8)])
        A = Queue([sem(f"s_a{i}") for i in range(6)])
        G = Queue([sem(f"s_g{i}") for i in range(4)], serial=True)
        SP = Queue([])
        ve, ae, ge, pe = nc.vector, nc.scalar, nc.gpsimd, nc.tensor

        cst = sb("cst", [128, NCONST])

        def C(name, rows=128):
            o, w = CONST[name]
            return cst[0:rows, o:o + w]

        slots = [Box(sb(f"slot{i}", [128, 4096]), sem(f"s_w{i}")) for i in range(NSLOT)]
        rows = [Box(sb(f"rows{i}", [128, 2048]), sem(f"s_r{i}")) for i in range(2)]
        banks = [Box(ctx.enter_context(nc.psum_tensor(f"ps{i}", [128, 512], F32))) for i in range(8)]
        small_sems = [sem(f"s_c{i}") for i in range(26)]
        state = {"slot": 0, "row": 0, "bank": 0, "small": 0}

        def load_into(box, parts):
            free = box.free
            assert free is not None
            box.free = None
            for dst, src in parts:
                SP.items.append(([free], nc.sync.dma_start, (dst, src), {}, box.sem, 16))
            box.n += 16 * len(parts)
            box.ready = (box.sem, box.n)
            return box

        def slot():
            b = slots[state["slot"] % NSLOT]
            state["slot"] += 1
            return b

        def load(shape, parts):
            b = slot()
            n = int(np.prod(shape))
            view = b.t[:, 0:n]
            if len(shape) == 2:
                view = view.rearrange("p (a b) -> p a b", a=shape[0])
            elif len(shape) == 3:
                view = view.rearrange("p (a b c) -> p a b c", a=shape[0], b=shape[1])
            load_into(b, [(f(view), src) for f, src in parts])
            b.v = view
            return b

        def load_rows(vectors):
            b = rows[state["row"] % 2]
            state["row"] += 1
            parts, at = [], 0
            for v in vectors:
                n = v.shape[1]
                parts.append((b.t[:, at:at + n], v.broadcast_to((128, n))))
                at += n
            return load_into(b, parts)

        def small(parts, w=(), q=None):
            eng = nc.sync if q is None else nc.gpsimd
            s = small_sems[state["small"]]
            state["small"] += 1
            for dst, src in parts:
                (q or SP).items.append((list(w), eng.dma_start, (dst, src), {}, s, 16))
            return (s, 16 * len(parts))

        def bank():
            while banks[state["bank"] % 8].pin:
                state["bank"] += 1
            b = banks[state["bank"] % 8]
            state["bank"] += 1
            assert b.free is not None
            b.w, b.free = b.free, None
            return b

        def mm(o, l, r, start, stop, w=(), inc=False, tp=None):
            if tp is None:
                return PE(pe.matmul, o, l, r, w=w, inc=inc, start=start, stop=stop)
            return PE(pe.matmul, o, l, r, w=w, inc=inc, start=start, stop=stop, tile_position=tp)

        def tr(o, i, w=(), inc=False, k=128):
            return PE(pe.transpose, o, i, C("ident", k)[:, 0:k], w=w, inc=inc)

        def barrier():
            toks = [q.last() for q in (PE, V, A, G) if q.count]
            for q in (PE, V, A, G):
                q.items.append((list(toks), None, (), {}, None, 0))

        def row(v, a=None, b=None):
            v = v.rearrange("(o n) -> o n", o=1)
            return v if a is None else v[:, a:b]

        xtok = sb("xtok", [128, 2, 1024])
        XT = sb("XT", [128, 8, 256])
        st6 = sb("st6", [128, 16, 6])
        mv = sb("mv", [128, 16, 2])
        rstd = sb("rstd", [128, 16])
        wrt = sb("wrt", [128, 8, 32])
        AR = sb("AR", [128, 17020])
        ar = {"at": 0}

        def arena(*shape, p=128, reset=None):
            if reset is not None:
                ar["at"] = reset
            n = int(np.prod(shape))
            v = AR[0:p, ar["at"]:ar["at"] + n]
            ar["at"] += n
            assert ar["at"] <= 17020, ar["at"]
            if len(shape) == 2:
                v = v.rearrange("p (a b) -> p a b", a=shape[0])
            if len(shape) == 3:
                v = v.rearrange("p (a b c) -> p a b c", a=shape[0], b=shape[1])
            return v

        def rows128(v):
            return v.rearrange("(r c) -> r c", c=128)

        def columns(parts, dst, i, w=()):
            n = sum(s.shape[0] for _, s in parts)
            t = small([(stage[i][a:a + s.shape[0], :], s) for a, s in parts])
            b = bank()
            tk = tr(b.t[:, 0:n], stage[i][0:n, :], w=(t, t_const, b.w), inc=True, k=n)
            tv = V(ve.tensor_copy, dst, b.t[:, 0:n], w=(tk,) + tuple(w))
            b.free = [tv]
            return tk, tv

        def stats(srcs, eps, base, w=()):
            n = len(srcs)
            for i, s in enumerate(srcs):
                f = s.shape[1]
                if f > 512:
                    for k in range(2):
                        t = V(ve.bn_stats, st6[:, 2 * i + k + base, :], s[:, k * 512:(k + 1) * 512], w=w)
                else:
                    t = V(ve.bn_stats, st6[:, i + base, :], s, w=w)
            for i, s in enumerate(srcs):
                if s.shape[1] > 512:
                    src = st6[:, base + 2 * i:base + 2 * i + 2, :]
                else:
                    src = st6[:, base + i, :]
                t2 = V(ve.bn_aggr, mv[:, base + i, :], src, w=(t,))
            t3 = V(ve.tensor_scalar, rstd[:, base:base + n], mv[:, base:base + n, 1], eps, None, ALU.add, w=(t2,))
            return G(ge.tensor_tensor, rstd[:, base:base + n], rstd[:, base:base + n],
                     C("nhalf")[:, 0:n], ALU.pow, w=(t3, t_const))

        def normal(dst, src, i, w=()):
            return V(ve.tensor_scalar, dst, src, mv[:, i, 0:1], rstd[:, i:i + 1], ALU.subtract, ALU.mult, w=w)

        def turn(dst, src, w, scale=None, bias=None, chunks=8):
            last = None
            for k0 in range(0, chunks, 2):
                b = bank()
                for k in (k0, k0 + 1):
                    for tt in range(2):
                        j = (k - k0) * 2 + tt
                        t = tr(b.t[:, j * 128:(j + 1) * 128], src[:, tt, k * 128:(k + 1) * 128],
                               w=(b.w, w), inc=(j == 3))
                for k in (k0, k0 + 1):
                    src_ = b.t[:, (k - k0) * 256:(k - k0 + 1) * 256]
                    eng = A if k0 % 4 else V
                    if eng is A:
                        last = A(ae.activation, dst[:, k, :], src_, ACT.Identity,
                                 bias=(0.0 if bias is None else bias[:, k:k + 1]),
                                 scale=(1.0 if scale is None else scale[:, k:k + 1]), w=(t,))
                        la = last
                    else:
                        if scale is None:
                            last = V(ve.tensor_copy, dst[:, k, :], src_, w=(t,))
                        else:
                            last = V(ve.tensor_scalar, dst[:, k, :], src_, scale[:, k:k + 1],
                                     0.0 if bias is None else bias[:, k:k + 1], ALU.mult, ALU.add, w=(t,))
                        lv = last
                b.free = [last]
            return [la, lv] if chunks > 2 else [lv]

        def feature(wcols, xT, w, n=256, kk=8):
            b = bank()
            for k in range(kk):
                l = wcols(k)
                t = mm(b.t[0:l.shape[1], 0:n], l, xT(k), k == 0, k == kk - 1, w=(b.w, w), inc=(k == kk - 1))
            b.tk = t
            return b

        def token(xT, wcols, n, w, kk=8, b=None, first=True, last=True):
            b = b or bank()
            for k in range(kk):
                t = mm(b.t[:, 0:n], xT(k), wcols(k), first and k == 0, last and k == kk - 1,
                       w=(b.w, w) if first else (w,), inc=(k == kk - 1))
            b.tk = t
            return b

        stage = [AR[:, 7168 + 128 * i:7296 + 128 * i] for i in range(10)]
        t_const = small([(cst[:, :], T["const"])])
        xc = arena(2, 1024)
        t_x = small([(xtok[:, tt, :], T["x"][0, tt * 128:(tt + 1) * 128, :]) for tt in range(2)])
        t_c = small([(xc[:, tt, :], T["ctx"][0, tt * 128:(tt + 1) * 128, :]) for tt in range(2)])
        b_in = T["b_in"][0]
        colA = sb("colA", [128, 128])
        colB = sb("colB", [128, 32])
        b_ada = T["b_ada"][0]
        _, t_cA = columns([(0, rows128(T["c"][0])), (8, rows128(T["c_ctx"])), (16, rows128(b_ada)),
                           (64, rows128(b_in[256:1280])), (72, rows128(b_in[1792:2304])),
                           (76, rows128(b_in[2320:2576])), (78, rows128(b_in[2832:5904])),
                           (102, rows128(T["pool_scale"][0])),
                           (104, T["qk_conv_w"][0].rearrange("j (r c) -> (j r) c", c=128))], colA[:, :], 0)
        _, t_cB = columns([(0, rows128(T["qk_conv_b"][0])), (8, rows128(T["mlstm_norm_g"][0]))], colB[:, 0:12], 1)
        rowb = load_rows([row(b_in, 0, 256), row(b_in, 1280, 1792), row(b_in, 2576, 2832),
                          row(T["sgu_ln_g"][0]), row(T["sgu_ln_b"][0]),
                          T["sgu_b"][0].rearrange("g (o t) -> o (g t)", o=1)])
        bgu = sb("bgu", [128, 512])
        gsrc = T["b_gate_up"][0].rearrange("e (r c) -> (e r) c", c=128)
        for q in range(4):
            _, t_bgu = columns([(0, gsrc[q * 128:(q + 1) * 128, :])], bgu[:, q * 128:(q + 1) * 128], 2 + q)
        colL = [sb(f"colL{l}", [128, 152]) for l in range(2)]
        t_cL = []
        for l in range(2):
            columns([(0, T["conv_dw_w_2"][l].rearrange("j (r c) -> (j r) c", c=128))], colL[l][:, 0:124], 6 + 2 * l)
            t_cL.append(columns([(0, rows128(T["mix_b_in_2"][l][544:1568])), (8, rows128(T["mla_q_norm_2"][l])),
                                 (10, rows128(T["mla_kv_norm_2"][l])), (12, rows128(T["conv_dw_b_2"][l])),
                                 (16, rows128(T["conv_norm_g_2"][l])), (20, rows128(T["conv_norm_b_2"][l]))],
                                colL[l][:, 124:148], 7 + 2 * l)[1])
        poolw = sb("poolw", [128, 2, 128])
        sguw = sb("sguw", [128, 4, 128])
        gb = sb("gb", [64, 2])
        tz = [G(ge.memset, poolw[:, :, :], 0.0), G(ge.memset, gb[:, :], 0.0)]
        gsem = small_sems[state["small"]]
        state["small"] += 1
        gl = [(poolw[(g % 2) * 64:(g % 2) * 64 + 64, g // 2, (g % 2) * 64:(g % 2) * 64 + 64], T["pool_w"][0, g])
              for g in range(4)]
        for kind in range(4):
            o = 2304 + 4 * kind
            p0 = 32 * (kind // 2)
            gl.append((gb[p0:p0 + 4, kind % 2:kind % 2 + 1], b_in[o:o + 4].rearrange("(a o) -> a o", o=1)))
        gl.append((sguw[:, :, :], T["sgu_w"][0].rearrange("g t s -> t g s")))
        for d, s in gl:
            SP.items.append(([tz], nc.sync.dma_start, (d, s), {}, gsem, 16))
        t_gl = (gsem, 16 * len(gl))

        w_ada = T["w_ada"][0].rearrange("(k p) n -> p k n", p=128)
        scT = sb("scT", [128, 2, 8])
        t_sc = A(ae.activation, scT[:, :, :].rearrange("p a b -> p (a b)"), colA[:, 0:16], ACT.Silu, w=(t_cA,))
        scB = arena(8, 128)
        for k in range(8):
            t_scb = V(ve.tensor_scalar, scB[:, k, :], C("ones"), scT[:, 0, k:k + 1], None, ALU.mult, w=(t_sc, t_const))
        modT = sb("modT", [128, 6, 8, 2])
        gB = sb("gB", [128, 2, 1024])
        rowg = load_rows([row(b_ada, 2048, 3072), row(b_ada, 5120, 6144)])

        def ada_cols(part):
            for h in range(2):
                s = load((8, 512), [(lambda v: v, w_ada[:, :, part * 1024 + h * 512:part * 1024 + (h + 1) * 512])])
                b = bank()
                for f in range(4):
                    for k in range(8):
                        t = mm(b.t[:, f * 2:f * 2 + 2], s.v[:, k, f * 128:(f + 1) * 128], scT[:, :, k],
                               k == 0, k == 7, w=(b.w, s.ready, t_sc), inc=(f == 3 and k == 7))
                s.free = [t]
                f0 = 16 + part * 8 + h * 4
                for src in range(2):
                    tv = V(ve.tensor_tensor, modT[:, part, h * 4:h * 4 + 4, src],
                           b.t[:, 0:8].rearrange("p (f s) -> p f s", s=2)[:, :, src], colA[:, f0:f0 + 4],
                           ALU.add, w=(t, t_cA))
                if part in (1, 4):
                    tv = V(ve.tensor_scalar, modT[:, part, h * 4:h * 4 + 4, :], modT[:, part, h * 4:h * 4 + 4, :],
                           1.0, None, ALU.add, w=(tv,))
                b.free = [tv]
            return tv

        def ada_rows(part, g):
            for h in range(2):
                s = load((8, 512), [(lambda v: v, w_ada[:, :, part * 1024 + h * 512:part * 1024 + (h + 1) * 512])])
                b = token(lambda k: scB[:, k, :], lambda k: s.v[:, k, :], 512, [s.ready, t_scb])
                s.free = [b.tk]
                o = g * 1024 + h * 512
                tv = V(ve.tensor_tensor, gB[:, g, h * 512:(h + 1) * 512], b.t[:, :], rowg.t[:, o:o + 512], ALU.add,
                       w=(b.tk, rowg.ready))
                b.free = [tv]
            return tv

        ada_cols(0)
        t_m1 = ada_cols(1)

        ts = stats([xtok[:, 0, :], xtok[:, 1, :], xc[:, 0, :], xc[:, 1, :]], 1e-5, 0, w=(t_x, t_c))
        xn = arena(2, 1024)
        for tt in range(2):
            tn = normal(xn[:, tt, :], xtok[:, tt, :], tt, w=(ts,))
            tnc = normal(xc[:, tt, :], xc[:, tt, :], 2 + tt, w=(ts,))
        XC = arena(8, 256, reset=5120)
        t_XT = turn(XT, xn, [tn], modT[:, 1, :, 0], modT[:, 0, :, 0])
        t_XC = turn(XC, xc, [tnc], modT[:, 1, :, 1], modT[:, 0, :, 1])
        ada_cols(3)
        t_m4 = ada_cols(4)
        ada_rows(2, 0)
        t_gB = ada_rows(5, 1)
        rowg.free = [t_gB]
        barrier()

        w_in = T["w_in"][0].rearrange("(k p) n -> p k n", p=128)
        X = lambda k: XT[:, k, :]
        XCk = lambda k: XC[:, k, :]
        zpad = arena(2, 258, reset=7168)
        cva = arena(256)
        cvb = arena(256)
        qkT = arena(12, 256)
        vaug = arena(4, 4, 129)
        kN = arena(4, 4, 128)
        bo = 0
        ptok = arena(2, 256, reset=0)
        vs = arena(2, 256)
        uT = arena(2, 256)
        soT = arena(4, 256)
        poolT = arena(2, 256)
        sguT = arena(2, 256)
        dT = arena(2, 256)
        assert ar["at"] <= 5120
        KS = 128.0 ** -0.5

        tz0 = V(ve.memset, zpad[:, :, 0:1], 0.0)
        tz1 = V(ve.memset, zpad[:, :, 257:258], 0.0, w=(tz0,))
        tz2 = V(ve.memset, vaug[:, :, :, 128:129], 1.0)

        s = load((8, 256), [(lambda v: v, w_in[:, :, 0:256])])
        for tt in range(2):
            b = token(lambda k: XT[:, k, tt * 128:(tt + 1) * 128], lambda k: s.v[:, k, :], 256, [s.ready] + t_XT)
            t_p = V(ve.tensor_tensor, ptok[:, tt, :], b.t[:, 0:256], rowb.t[:, 0:256], ALU.add, w=(b.tk, rowb.ready))
            b.free = [t_p]
        s.free = [b.tk]

        conv = {"i": 0, "tok": [tz1, tz1], "a": []}

        def qk(f, xT, dst):
            i = conv["i"] % 2
            conv["i"] += 1
            b = feature(lambda k: s.v[:, k, (f % 4) * 128:(f % 4 + 1) * 128], xT, [s.ready] + t_XT + t_XC)
            z = zpad[:, i, :]
            ta = A(ae.activation, z[:, 1:257], b.t[:, 0:256], ACT.Identity, bias=colA[:, 64 + f:65 + f], scale=1.0,
                   w=(b.tk, conv["tok"][i], t_cA))
            b.free = [ta]
            y = cva if i == 0 else cvb
            t = V(ve.tensor_scalar, y, z[:, 0:256], colA[:, 104 + f:105 + f], colB[:, f:f + 1], ALU.mult, ALU.add,
                  w=(ta, t_cB, conv["a"][-2:-1]))
            for j in (1, 2):
                t = V(ve.scalar_tensor_tensor, y, z[:, j:j + 256], colA[:, 104 + 8 * j + f:105 + 8 * j + f], y,
                      ALU.mult, ALU.add, w=(t,))
            conv["tok"][i] = t
            ta = A(ae.activation, dst, y, ACT.Silu, w=(t,))
            conv["a"].append(ta)
            if f >= 4:
                ta = V(ve.tensor_scalar, dst, dst, KS, None, ALU.mult, w=(ta,))
            return ta, b.tk

        for half in range(2):
            s = load((8, 512), [(lambda v: v, w_in[:, :, 256 + half * 512:768 + half * 512])])
            for f in range(4 * half, 4 * half + 4):
                t_qk, tk = qk(f, X, qkT[:, f, :])
                if half:
                    t_qk, tk = qk(f, XCk, qkT[:, f + 4, :])
            s.free = [tk]
        t_q = [V.last(), A.last()]

        s = load((8, 512), [(lambda v: v, w_in[:, :, 1280:1792])])
        for c in range(4):
            src = (XC if c < 2 else XT)
            b = token(lambda k: src[:, k, (c % 2) * 128:(c % 2 + 1) * 128], lambda k: s.v[:, k, :], 512, [s.ready])
            t_v = V(ve.tensor_tensor, vaug[:, c, :, 0:128], b.t[:, :].rearrange("p (h d) -> p h d", h=4),
                    rowb.t[:, 256:768].rearrange("p (h d) -> p h d", h=4), ALU.add, w=(b.tk, tz2, rowb.ready))
            b.free = [t_v]
        s.free = [b.tk]

        s = load((8, 512), [(lambda v: v, w_in[:, :, 1792:2304])])
        for f in range(4):
            b = feature(lambda k: s.v[:, k, f * 128:(f + 1) * 128], X, [s.ready])
            t_so = A(ae.activation, soT[:, f, :], b.t[:, 0:256], ACT.Sigmoid, bias=colA[:, 72 + f:73 + f], scale=1.0,
                     w=(b.tk,))
            b.free = [t_so]
        s.free = [b.tk]

        s = load((8, 16 + 496), [(lambda v: v, w_in[:, :, 2304:2816])])
        s2 = load((8, 16), [(lambda v: v, w_in[:, :, 2816:2832])])
        wg = AR[:, 15380:16404].rearrange("p (k i m) -> p k i m", k=8, i=2)
        tg = G(ge.memset, wg[:, :, :, :], 0.0)
        for kind in range(4):
            p0 = 32 * (kind // 2)
            tg = G(ge.tensor_copy, wg[:, :, kind % 2, p0:p0 + 4], s.v[:, :, 4 * kind:4 * kind + 4],
                   w=(tg, s.ready))
        rI = arena(512, p=64, reset=4096)
        rF = arena(512, p=64)
        bc = arena(512, p=64, reset=5120)
        uR = arena(512, p=64)
        MR = arena(512, p=64)
        assert ar["at"] <= 17020
        for i, dst in ((0, rI), (1, rF)):
            b = bank()
            for k in range(8):
                mm(b.t[0:64, 0:256], wg[:, k, i, :], XC[:, k, :], k == 0, k == 7, w=(b.w, tg))
            for k in range(8):
                t = mm(b.t[0:64, 256:512], wg[:, k, i, :], XT[:, k, :], k == 0, k == 7, inc=(k == 7))
            t_if = A(ae.activation, dst, b.t[0:64, :], ACT.Identity, bias=gb[:, i:i + 1], scale=1.0, w=(t, t_gl))
            b.free = [t_if]
        for f in range(2):
            b = feature(lambda k: s.v[:, k, 16 + f * 128:144 + f * 128], X, [s.ready])
            t_u = A(ae.activation, uT[:, f, :], b.t[:, 0:256], ACT.Gelu, bias=colA[:, 76 + f:77 + f], scale=1.0,
                    w=(b.tk,))
            b.free = [t_u]
        for tt in range(2):
            b = bank()
            for k in range(8):
                mm(b.t[:, 0:240], XT[:, k, tt * 128:(tt + 1) * 128], s.v[:, k, 272:512], k == 0, k == 7,
                   w=(b.w, s.ready))
            for k in range(8):
                t = mm(b.t[:, 240:256], XT[:, k, tt * 128:(tt + 1) * 128], s2.v[:, k, :], k == 0, k == 7,
                       w=(s2.ready,), inc=(k == 7))
            tv = V(ve.tensor_tensor, vs[:, tt, :], b.t[:, 0:256], rowb.t[:, 768:1024], ALU.add, w=(t,))
            b.free = [tv]
            ta = A(ae.activation, vs[:, tt, :], vs[:, tt, :], ACT.Gelu, w=(tv,))
        s.free = [t, tg]
        s2.free = [t]

        ts = stats([vs[:, 0, :], vs[:, 1, :]], 1e-5, 0, w=(ta,))
        for tt in range(2):
            t = normal(vs[:, tt, :], vs[:, tt, :], tt, w=(ts,))
            t = V(ve.tensor_tensor, vs[:, tt, :], vs[:, tt, :], rowb.t[:, 1024:1280], ALU.mult, w=(t,))
            t_vs = V(ve.tensor_tensor, vs[:, tt, :], vs[:, tt, :], rowb.t[:, 1280:1536], ALU.add, w=(t,))
        wsT = AR[:, 16412:16924].rearrange("p (g t) -> p g t", g=4)
        b = bank()
        for g in range(4):
            t = tr(b.t[:, g * 128:(g + 1) * 128], sguw[:, g, :], w=(b.w, t_gl), inc=(g == 3))
        t_ws = V(ve.tensor_copy, wsT[:, :, :].rearrange("p g t -> p (g t)"), b.t[:, :], w=(t,))
        b.free = [t_ws]
        for g in range(4):
            b = bank()
            for n in range(2):
                t = mm(b.t[:, n * 128:(n + 1) * 128], vs[:, n, (g // 2) * 128:(g // 2 + 1) * 128], wsT[:, g, :],
                       True, True, w=(b.w, t_vs, t_ws), inc=(n == 1))
            q0 = (g % 2) * 64
            for n in range(2):
                tv = V(ve.tensor_tensor, sguT[q0:q0 + 64, g // 2, n * 128:(n + 1) * 128],
                       b.t[q0:q0 + 64, n * 128:(n + 1) * 128],
                       rowb.t[q0:q0 + 64, 1536 + g * 128:1536 + (g + 1) * 128], ALU.add, w=(t,))
            b.free = [tv]
            t_sgu = V(ve.tensor_tensor, sguT[q0:q0 + 64, g // 2, :], sguT[q0:q0 + 64, g // 2, :],
                      uT[q0:q0 + 64, g // 2, :], ALU.mult, w=(tv, t_u))
        rowb.free = [t_sgu]

        for g in range(4):
            b = bank()
            for n in range(2):
                t = mm(b.t[:, n * 128:(n + 1) * 128], ptok[:, n, (g // 2) * 128:(g // 2 + 1) * 128],
                       C("pool")[:, g * 128:(g + 1) * 128], True, True, w=(b.w, t_p), inc=(n == 1))
            q0 = (g % 2) * 64
            t_d = V(ve.tensor_copy, dT[q0:q0 + 64, g // 2, :], b.t[q0:q0 + 64, 0:256], w=(t,))
            b.free = [t_d]
        for j in range(2):
            b = bank()
            t = mm(b.t[:, 0:256], poolw[:, j, :], dT[:, j, :], True, True, w=(b.w, t_d, t_gl), inc=True)
            t_pool = V(ve.tensor_scalar, poolT[:, j, :], b.t[:, 0:256], colA[:, 102 + j:103 + j], None, ALU.mult,
                       w=(t,))
            b.free = [t_pool]

        tmpR = arena(512, p=64)
        assert ar["at"] == 7168
        te = V(ve.scalar_tensor_tensor, tmpR, rF, -1.0, rF, ALU.mult, ALU.max, w=(t_if,))
        te = A(ae.activation, tmpR, tmpR, ACT.Exp, scale=-1.0, w=(te,))
        te = A(ae.activation, tmpR, tmpR, ACT.Ln, bias=1.0, w=(te,))
        te = V(ve.scalar_tensor_tensor, rF, rF, 0.0, tmpR, ALU.min, ALU.subtract, w=(te,))
        tzr = V(ve.memset, tmpR, 0.0, w=(te,))
        tzb = V(ve.memset, bc, 0.0, w=(te,))
        tzm = V(ve.memset, MR, 0.0, w=(te,))
        mst = sb("mst", [64, 8])
        mls = sb("mls", [64, 8])
        tzs = V(ve.memset, mst[:, :], 0.0)
        tzl = V(ve.memset, mls[:, :], 0.0)
        ORD = ((0, 1, 2, 3), (1, 0, 3, 2))
        for d in range(2):
            p0 = 32 * d
            for c in range(4):
                a, e = c * 128, (c + 1) * 128
                cut = slice(a, e) if d == 0 else slice(e - 1, a - 1 if a else None, -1)
                t = V(ve.tensor_tensor_scan, bc[p0:p0 + 4, cut], rF[p0:p0 + 4, cut], tmpR[p0:p0 + 4, cut],
                      0.0, ALU.add, ALU.add, w=(te, tzr, tzb))
        t = V(ve.tensor_tensor, uR, rI, bc, ALU.subtract, w=(t,))
        for st in range(4):
            for d in range(2):
                p0 = 32 * d
                c = ORD[d][st]
                a, e = c * 128, (c + 1) * 128
                cut = slice(a, e) if d == 0 else slice(e - 1, a - 1 if a else None, -1)
                end = e - 1 if d == 0 else a
                tm = V(ve.tensor_tensor_scan, MR[p0:p0 + 4, cut], uR[p0:p0 + 4, cut], uR[p0:p0 + 4, cut],
                       mst[p0:p0 + 4, st:st + 1], ALU.max, ALU.max, w=(t, tzs, tzm, tzl))
                tm2 = V(ve.tensor_tensor, mst[p0:p0 + 4, st + 1:st + 2], MR[p0:p0 + 4, end:end + 1],
                        bc[p0:p0 + 4, end:end + 1], ALU.add, w=(tm,))
                tm3 = V(ve.tensor_scalar, mls[p0:p0 + 4, st:st + 1], MR[p0:p0 + 4, end:end + 1], -1.0, None,
                        ALU.mult, w=(tm,))
            t = tm2
        t = V(ve.tensor_tensor, mls[:, 4:8], mst[:, 0:4], mls[:, 0:4], ALU.add, w=(tm2, tm3))
        t_a = A(ae.activation, mls[:, 4:8], mls[:, 4:8], ACT.Exp, w=(t,))
        t = V(ve.tensor_tensor, bc, bc, MR, ALU.add, w=(tm2,))
        t_em = A(ae.activation, bc, bc, ACT.Exp, scale=-1.0, w=(t,))
        for d in range(2):
            p0 = 32 * d
            for st in range(4):
                c = ORD[d][st]
                a, e = c * 128, (c + 1) * 128
                t_wk = A(ae.activation, rI[p0:p0 + 32, a:e], uR[p0:p0 + 32, a:e], ACT.Exp,
                         bias=mls[p0:p0 + 32, st:st + 1], scale=1.0, w=(tm3,))
                t_dc = A(ae.activation, rF[p0:p0 + 32, a:e], MR[p0:p0 + 32, a:e], ACT.Exp,
                         bias=mst[p0:p0 + 32, st:st + 1], scale=-1.0, w=(tm2, te))
        t_nm = V(ve.tensor_scalar, MR, MR, -1.0, None, ALU.mult, w=(t_dc, t_em))
        cols = AR[:, 0:768].rearrange("p (a b) -> p a b", a=12)
        lst = [(uR, c) for c in range(4)] + [(rI, c) for c in range(4)] + [(rF, 2), (rF, 3), (bc, 2), (bc, 3)]
        for h in range(2):
            b = bank()
            for i in range(6):
                r, c = lst[h * 6 + i]
                t = tr(b.t[:, i * 64:(i + 1) * 64], r[:, c * 128:(c + 1) * 128], w=(b.w, t_wk, t_dc, t_em),
                       inc=(i == 5), k=64)
            t_cols = V(ve.tensor_copy, cols[:, h * 6:h * 6 + 6, :].rearrange("p a b -> p (a b)"), b.t[:, 0:384],
                       w=(t, t_d, t_sgu))
            b.free = [t_cols]
        aB = sb("aB", [128, 8, 4])
        b = bank()
        sel = C("sel", 64).rearrange("p (r m) -> p r m", r=8)
        for r in range(8):
            t = mm(b.t[:, r * 4:r * 4 + 4], sel[:, r, :], mls[:, 4:8], True, True, w=(b.w, t_a), inc=(r == 7))
        t_aB = V(ve.tensor_copy, aB[:, :, :].rearrange("p a b -> p (a b)"), b.t[:, 0:32], w=(t,))
        b.free = [t_aB]
        for c in range(4):
            b = bank()
            for h in range(4):
                src = qkT[:, (8 if c < 2 else 4) + h, (c % 2) * 128:(c % 2 + 1) * 128]
                t = tr(b.t[:, h * 128:(h + 1) * 128], src, w=(b.w, t_q), inc=(h == 3))
            t_kN = V(ve.tensor_copy, kN[:, c, :, :].rearrange("p a b -> p (a b)"), b.t[:, :], w=(t,))
            b.free = [t_kN]

        barrier()
        CT = arena(8, 129, reset=15380)
        Et = [arena(128, reset=7168), arena(128)]
        SC = [arena(128), arena(128)]
        vw = [arena(129) for _ in range(2)]
        nd = [arena(129) for _ in range(2)]
        assert ar["at"] <= 8196
        tmpI = [arena(129, reset=3584), arena(129)]
        hsum = arena(2, 4, 128, reset=4096)
        dn = sb("dn", [128, 32])
        vw_free = [None, None]
        ct_tok = [None] * 8
        ct_use = [None] * 8
        et_free = [None, None]
        sc_free = [None, None]
        nd_tok = [None, None]
        ti_free = [None, None]
        cnt = {"u": 0, "o": 0}
        hs_tok = {}

        def col(kind, r):
            j = 32 * (r // 4) + r % 4
            return cols[:, kind, j:j + 1]

        def update(r, st):
            d, h = r // 4, r % 4
            c = ORD[d][st]
            i = cnt["u"] % 2
            cnt["u"] += 1
            tw = A(ae.activation, vw[i], vaug[:, c, h, :], ACT.Copy, scale=col(4 + c, r), w=(vw_free[i], t_v, t_cols))
            b = bank()
            t = mm(b.t[:, 0:129], kN[:, c, h, :], vw[i], True, True, w=(b.w, tw, t_kN), inc=True)
            vw_free[i] = t
            if st == 0:
                tv = V(ve.tensor_copy, CT[:, r, :], b.t[:, 0:129], w=(t,))
            else:
                tv = V(ve.scalar_tensor_tensor, CT[:, r, :], CT[:, r, :], aB[:, r, st:st + 1], b.t[:, 0:129],
                       ALU.mult, ALU.add, w=(t, ct_tok[r], ct_use[r], t_aB))
            b.free = [tv]
            ct_tok[r] = tv

        def output(r, st):
            d, h = r // 4, r % 4
            c = ORD[d][st]
            n = c - 2
            i = cnt["o"] % 2
            j = cnt["o"]
            cnt["o"] += 1
            tc = slice(n * 128, (n + 1) * 128)
            bD = bank()
            mm(bD.t[:, 0:128], sel[:, r, :], MR[:, c * 128:(c + 1) * 128], True, False, w=(bD.w, t_nm))
            t = mm(bD.t[:, 0:128], C("ident"), C("maskf" if d == 0 else "maskb"), False, True, inc=True)
            tE = A(ae.activation, Et[i], bD.t[:, 0:128], ACT.Exp, bias=col(c, r), scale=1.0, w=(t, et_free[i]))
            bD.free = [tE]
            bS = bank()
            t = mm(bS.t[:, 0:128], qkT[:, 4 + h, tc], qkT[:, h, tc], True, True, w=(bS.w, t_q), inc=True)
            tS = V(ve.tensor_tensor, SC[i], bS.t[:, 0:128], Et[i], ALU.mult, w=(t, tE, sc_free[i]))
            bS.free = [tS]
            et_free[i] = tS
            bI = bank()
            t = mm(bI.t[:, 0:129], qkT[:, h, tc], CT[:, r, :], True, True, w=(bI.w, ct_tok[r]), inc=True)
            ct_use[r] = t
            tI = A(ae.activation, tmpI[i], bI.t[:, 0:129], ACT.Copy, scale=col(8 + n, r), w=(t, ti_free[i]))
            bI.free = [tI]
            bN = bank()
            t = mm(bN.t[:, 0:129], SC[i], vaug[:, c, h, :], True, True, w=(bN.w, tS), inc=True)
            sc_free[i] = t
            t = V(ve.tensor_tensor, nd[i], bN.t[:, 0:129], tmpI[i], ALU.add, w=(t, tI, nd_tok[i]))
            bN.free = [t]
            ti_free[i] = t
            den = nd[i][:, 128:129]
            t = V(ve.scalar_tensor_tensor, dn[:, j:j + 1], den, -1.0, den, ALU.mult, ALU.max, w=(t,))
            t = V(ve.tensor_tensor, dn[:, j:j + 1], dn[:, j:j + 1], col(10 + n, r), ALU.max, w=(t,))
            t = V(ve.reciprocal, dn[:, j:j + 1], dn[:, j:j + 1], w=(t,))
            if (h, n) not in hs_tok:
                t = V(ve.tensor_scalar, hsum[:, n, h, :], nd[i][:, 0:128], dn[:, j:j + 1], None, ALU.mult, w=(t,))
            else:
                t = V(ve.scalar_tensor_tensor, hsum[:, n, h, :], nd[i][:, 0:128], dn[:, j:j + 1], hsum[:, n, h, :],
                      ALU.mult, ALU.add, w=(t, hs_tok[(h, n)]))
            hs_tok[(h, n)] = t
            nd_tok[i] = t

        for st in range(4):
            for r in range(8):
                if st >= 2:
                    output(r, st)
                if st < 3:
                    update(r, st)
        t_hs = V.last()
        mlT = arena(4, 256, reset=0)
        ts = stats([hsum[:, n, h, :] for n in range(2) for h in range(4)], 1e-6, 0, w=(t_hs,))
        for n in range(2):
            for h in range(4):
                t = normal(hsum[:, n, h, :], hsum[:, n, h, :], n * 4 + h, w=(ts,))
        barrier()
        for h in range(4):
            b = bank()
            for n in range(2):
                tk = tr(b.t[:, n * 128:(n + 1) * 128], hsum[:, n, h, :], w=(b.w, t), inc=(n == 1))
            t_ml = V(ve.scalar_tensor_tensor, mlT[:, h, :], b.t[:, 0:256], colB[:, 8 + h:9 + h], soT[:, h, :],
                     ALU.mult, ALU.mult, w=(tk, t_so, t_cB))
            b.free = [t_ml]
        barrier()

        sig = arena(24, 256, reset=8196)
        yT = arena(8, 256)
        for q in range(6):
            s = load((8, 512), [(lambda v: v, w_in[:, :, 2832 + q * 512:2832 + (q + 1) * 512])])
            for f in range(4):
                j = q * 4 + f
                b = feature(lambda k: s.v[:, k, f * 128:(f + 1) * 128], X, [s.ready])
                ts = A(ae.activation, sig[:, j, :], b.t[:, 0:256], ACT.Sigmoid, bias=colA[:, 78 + j:79 + j],
                       scale=1.0, w=(b.tk,))
                b.free = [ts]
            s.free = [b.tk]
        wb = [T[n][0].rearrange("(k p) n -> p k n", p=128) for n in ("w_br_pool", "w_br_mlstm", "w_br_sgu")]
        yt = [arena(256, reset=5120), arena(256)]
        ty = [None, None]
        for half in range(2):
            cs = slice(half * 512, (half + 1) * 512)
            s = load((8, 512), [(lambda v: v[:, 0:2, :], wb[0][:, :, cs]), (lambda v: v[:, 2:6, :], wb[1][:, :, cs]),
                                (lambda v: v[:, 6:8, :], wb[2][:, :, cs])])
            for f in range(4):
                j = half * 4 + f
                tprev = None
                for br, (k0, kn, src) in enumerate(((0, 2, poolT), (2, 4, mlT), (6, 2, sguT))):
                    b = feature(lambda k: s.v[:, k0 + k, f * 128:(f + 1) * 128], lambda k: src[:, k, :],
                                [s.ready, t_ml, t_pool, t_sgu], kk=kn)
                    if br == 0:
                        tprev = V(ve.tensor_tensor, yT[:, j, :], b.t[:, 0:256], sig[:, j, :], ALU.mult, w=(b.tk, ts))
                        b.free = [tprev]
                    else:
                        i = br - 1
                        t = V(ve.tensor_tensor, yt[i], b.t[:, 0:256], sig[:, 8 * br + j, :], ALU.mult,
                              w=(b.tk, ts, ty[i]))
                        b.free = [t]
                        tprev = G(ge.tensor_tensor, yT[:, j, :], yT[:, j, :], yt[i], ALU.add, w=(t, tprev))
                        ty[i] = tprev
            s.free = [b.tk]
        t_y = tprev
        w_out = T["w_out"][0].rearrange("(k p) n -> p k n", p=128)

        rtmp = arena(2, 1024, reset=0)
        xtmp = arena(2, 1024)

        def residual(alpha, banks4, gate, w):
            for tt, h, b in banks4:
                cs = slice(h * 512, (h + 1) * 512)
                if gate is None:
                    t = V(ve.scalar_tensor_tensor, xtok[:, tt, cs], xtok[:, tt, cs], alpha, b.t[:, :], ALU.mult,
                          ALU.add, w=(b.tk, w))
                    b.free = [t]
                else:
                    t = V(ve.tensor_tensor, rtmp[:, tt, cs], b.t[:, :], gate[:, cs], ALU.mult, w=(b.tk, w))
                    b.free = [t]
                    t = V(ve.scalar_tensor_tensor, xtok[:, tt, cs], xtok[:, tt, cs], alpha, rtmp[:, tt, cs],
                          ALU.mult, ALU.add, w=(t,))
            return t

        def ln_affine(g, bvec, w):
            r = load_rows([row(g), row(bvec)])
            ts = stats([xtok[:, 0, :], xtok[:, 1, :]], 1e-5, 0, w=(w,))
            out_ = []
            for tt in range(2):
                t = normal(xtok[:, tt, :], xtok[:, tt, :], tt, w=(ts,))
                t = V(ve.tensor_tensor, xtok[:, tt, :], xtok[:, tt, :], r.t[:, 0:1024], ALU.mult, w=(t, r.ready))
                t = G(ge.tensor_tensor, xtok[:, tt, :], xtok[:, tt, :], r.t[:, 1024:2048], ALU.add, w=(t, r.ready))
                out_.append(t)
            r.free = list(out_)
            return out_

        def dense(xT, wsrc, w, kk=8):
            got = []
            for h in range(2):
                s = load((8, 512), [(lambda v: v, wsrc[:, :, h * 512:(h + 1) * 512])])
                for tt in range(2):
                    b = token(lambda k: xT[:, k, tt * 128:(tt + 1) * 128], lambda k: s.v[:, k, :], 512,
                              [s.ready, w])
                    got.append((tt, h, b))
                s.free = [b.tk]
            return got

        bs = dense(yT, w_out, t_y)
        t = residual(ALPHA1, bs, gB[:, 0, :], t_gB)
        tl = ln_affine(T["ln1_g"][0], T["ln1_b"][0], t)
        ts = stats([xtok[:, 0, :], xtok[:, 1, :]], 1e-5, 4, w=(tl,))
        for tt in range(2):
            t = normal(xtmp[:, tt, :], xtok[:, tt, :], 4 + tt, w=(ts,))
        t_h = turn(XT, xtmp, [t], modT[:, 4, :, 0], modT[:, 3, :, 0])

        t_wr = small([(wrt[:, :, :], T["w_router"][0].rearrange("(k p) n -> p k n", p=128))])
        rowr = load_rows([row(T["b_router"][0])])
        barrier()
        cw = arena(2, 32, reset=0)
        cwT = arena(256, p=32)
        lg = arena(2, 32)
        lg2 = arena(2, 32)
        top = arena(2, 8)
        eq = arena(2, 32)
        cs = arena(2, 32)
        zr = arena(2, 32)
        tzz = V(ve.memset, zr, 0.0)
        sm = arena(2, 4)
        bdn = arena(1024, p=32)
        t_bd = small([(bdn, T["b_down"][0])], q=G)
        acc = arena(2, 1024)
        hid = arena(8, 256)
        gt = [arena(256) for _ in range(2)]
        sg = [arena(256) for _ in range(2)]
        up = [arena(256) for _ in range(2)]
        for tt in range(2):
            b = token(lambda k: XT[:, k, tt * 128:(tt + 1) * 128], lambda k: wrt[:, k, :], 32, [t_wr, t_h])
            t = V(ve.tensor_tensor, lg[:, tt, :], b.t[:, 0:32], rowr.t[:, 0:32], ALU.add, w=(b.tk, rowr.ready))
            b.free = [t]
            rowr.free = [t]
            t0 = V(ve.max, top[:, tt, :], lg[:, tt, :], w=(t,))
            v4 = top[:, tt, 3:4]
            tg = V(ve.tensor_scalar, lg2[:, tt, :], lg[:, tt, :], v4, None, ALU.is_gt, w=(t0,))
            tn = V(ve.tensor_reduce, sm[:, tt, 3:4], lg2[:, tt, :], AX.X, ALU.add, w=(tg,))
            tq = V(ve.tensor_scalar, eq[:, tt, :], lg[:, tt, :], v4, None, ALU.is_equal, w=(t0,))
            tc_ = V(ve.tensor_tensor_scan, cs[:, tt, :], eq[:, tt, :], zr[:, tt, :], 0.0, ALU.add, ALU.add,
                    w=(tq, tzz))
            tc_ = V(ve.tensor_scalar, cs[:, tt, :], cs[:, tt, :], sm[:, tt, 3:4], 4.5, ALU.add, ALU.is_lt,
                    w=(tc_, tn))
            tc_ = V(ve.tensor_tensor, eq[:, tt, :], eq[:, tt, :], cs[:, tt, :], ALU.mult, w=(tc_,))
            te2 = V(ve.tensor_tensor, lg2[:, tt, :], lg2[:, tt, :], eq[:, tt, :], ALU.add, w=(tc_,))
            t = V(ve.tensor_scalar, sm[:, tt, 0:1], top[:, tt, 0:1], -1.0, None, ALU.mult, w=(t0,))
            te = A(ae.activation, lg[:, tt, :], lg[:, tt, :], ACT.Exp, bias=sm[:, tt, 0:1], scale=1.0, w=(t, te2))
            t = V(ve.tensor_tensor, cw[:, tt, :], lg[:, tt, :], lg2[:, tt, :], ALU.mult, w=(te, te2))
            t = V(ve.tensor_reduce, sm[:, tt, 1:2], cw[:, tt, :], AX.X, ALU.add, w=(t,))
            t = V(ve.reciprocal, sm[:, tt, 2:3], sm[:, tt, 1:2], w=(t,))
            t_cw = V(ve.tensor_scalar, cw[:, tt, :], cw[:, tt, :], sm[:, tt, 2:3], None, ALU.mult, w=(t,))
        b = bank()
        for tt in range(2):
            tk = tr(b.t[0:32, tt * 128:(tt + 1) * 128], cw[:, tt, :], w=(b.w, t_cw), inc=(tt == 1))
        t_cwT = V(ve.tensor_copy, cwT, b.t[0:32, 0:256], w=(tk,))
        b.free = [t_cwT]
        for tt in range(2):
            for h in range(2):
                b = bank()
                tk = mm(b.t[:, :], cwT[:, tt * 128:(tt + 1) * 128], bdn[:, h * 512:(h + 1) * 512], True, True,
                        w=(b.w, t_cwT, t_bd), inc=True)
                t_acc = V(ve.tensor_copy, acc[:, tt, h * 512:(h + 1) * 512], b.t[:, :], w=(tk,))
                b.free = [t_acc]

        gf = [None, None]
        hid_free = None
        acc_tok = {(tt, h): t_acc for tt in range(2) for h in range(2)}
        for e in range(32):
            wgu = T["w_gate_up"][0, e].rearrange("(k p) n -> p k n", p=128)
            wdn = T["w_down"][0, e].rearrange("(k p) n -> p k n", p=128)
            for q in range(4):
                s = load((2, 8, 256), [(lambda v: v[:, 0], wgu[:, :, q * 256:(q + 1) * 256]),
                                       (lambda v: v[:, 1], wgu[:, :, 1024 + q * 256:1024 + (q + 1) * 256])])
                for ff in range(2):
                    f = 2 * q + ff
                    i = f % 2
                    bg = feature(lambda k: s.v[:, 0, k, ff * 128:(ff + 1) * 128], X, [s.ready, t_h])
                    bu = feature(lambda k: s.v[:, 1, k, ff * 128:(ff + 1) * 128], X, [s.ready])
                    t = V(ve.tensor_scalar, gt[i], bg.t[:, 0:256], bgu[:, e * 16 + f:e * 16 + f + 1], 7.0, ALU.add,
                          ALU.min, w=(bg.tk, t_bgu, gf[i]))
                    bg.free = [t]
                    ta = A(ae.activation, sg[i], gt[i], ACT.Sigmoid, scale=1.702, w=(t, gf[i]))
                    t2 = V(ve.tensor_scalar, up[i], bu.t[:, 0:256], bgu[:, e * 16 + 8 + f:e * 16 + 9 + f], 7.0,
                           ALU.add, ALU.min, w=(bu.tk, gf[i]))
                    bu.free = [t2]
                    t2 = V(ve.tensor_scalar, up[i], up[i], -7.0, 1.0, ALU.max, ALU.add, w=(t2,))
                    t3 = G(ge.tensor_tensor, gt[i], gt[i], sg[i], ALU.mult, w=(ta,))
                    t_hid = V(ve.tensor_tensor, hid[:, f, :], gt[i], up[i], ALU.mult, w=(t3, t2, hid_free))
                    gf[i] = t_hid
                s.free = [bu.tk]
            for h in range(2):
                s = load((8, 512), [(lambda v: v, wdn[:, :, h * 512:(h + 1) * 512])])
                for tt in range(2):
                    b = token(lambda k: hid[:, k, tt * 128:(tt + 1) * 128], lambda k: s.v[:, k, :], 512,
                              [s.ready, t_hid])
                    a = acc[:, tt, h * 512:(h + 1) * 512]
                    t = V(ve.scalar_tensor_tensor, a, b.t[:, :], cw[:, tt, e:e + 1], a, ALU.mult, ALU.add,
                          w=(b.tk, acc_tok[(tt, h)]))
                    acc_tok[(tt, h)] = t
                    b.free = [t]
                s.free = [b.tk]
            hid_free = b.tk
        for tt in range(2):
            t = V(ve.tensor_tensor, acc[:, tt, :], acc[:, tt, :], gB[:, 1, :], ALU.mult, w=(V.last(),))
            t = V(ve.scalar_tensor_tensor, xtok[:, tt, :], xtok[:, tt, :], ALPHA1, acc[:, tt, :], ALU.mult, ALU.add,
                  w=(t,))
        tl = ln_affine(T["ln2_g"][0], T["ln2_b"][0], t)
        barrier()
        memT = arena(8, 256, reset=0)
        RC = arena(256, p=96)
        RS = arena(256, p=96)
        base = ar["at"]
        mtok = arena(2, 1024)
        t_mem = small([(mtok[:, tt, :], T["mem_2"][0, tt * 128:(tt + 1) * 128, :]) for tt in range(2)],
                      w=(PE.last(), V.last(), A.last(), G.last()))
        posi = sb("posi", [96, 256], I32)
        t_pos = small([(posi[:, :], T["positions_2"].broadcast_to((96, 256)))])
        t_mT = turn(memT, mtok, [t_mem])
        an = arena(256, p=96)
        kk_ = arena(256, p=96)
        t = V(ve.tensor_copy, an, posi[:, :], w=(t_pos,))
        t = V(ve.tensor_scalar, an, an, C("freq", 96), None, ALU.mult, w=(t,))
        t = V(ve.tensor_scalar, kk_, an, 1.0 / (2 * np.pi), None, ALU.mult, w=(t,))
        t = V(ve.tensor_scalar, kk_, kk_, 12582912.0, None, ALU.add, w=(t,))
        t = V(ve.tensor_scalar, kk_, kk_, -12582912.0, None, ALU.add, w=(t,))
        rest = 2 * np.pi
        for bits in (5, 13, 21, None):
            part = float(np.float32(rest)) if bits is None else np.floor(rest * 2.0 ** bits) / 2.0 ** bits
            rest -= part
            t = V(ve.scalar_tensor_tensor, an, kk_, -part, an, ALU.mult, ALU.add, w=(t,))
        t = V(ve.tensor_scalar, RS, an, 3.1415925, -3.1415925, ALU.min, ALU.max, w=(t,))
        t_rs = A(ae.activation, RS, RS, ACT.Sin, w=(t,))
        t = V(ve.tensor_scalar, an, an, np.pi / 2, None, ALU.add, w=(t,))
        t = V(ve.tensor_scalar, kk_, an, 3.1415927, -2 * np.pi, ALU.is_gt, ALU.mult, w=(t,))
        t = V(ve.tensor_tensor, an, an, kk_, ALU.add, w=(t,))
        t = V(ve.tensor_scalar, RC, an, 3.1415925, -3.1415925, ALU.min, ALU.max, w=(t,))
        t_rc = A(ae.activation, RC, RC, ACT.Sin, w=(t,))
        krb = sb("krb", [96, 2])
        tkb = G(ge.memset, krb[:, :], 0.0)
        t_krb = small([(krb[64:96, l:l + 1], T["mix_b_in_2"][l][512:544].rearrange("(a o) -> a o", o=1))
                       for l in range(2)], w=(tkb,))
        rq = sb("rq", [128, 8])
        sums = sb("sums", [128, 2, 24])
        t_x = tl

        def softmax(b, n, width, dst, scale, w):
            t = V(ve.tensor_reduce, sums[:, 0, n:n + 1], b.t[:, 0:width], AX.X, ALU.max, w=(b.tk, w))
            t = V(ve.tensor_scalar, sums[:, 0, n:n + 1], sums[:, 0, n:n + 1], -scale, None, ALU.mult, w=(t,))
            t = A(ae.activation, dst, b.t[:, 0:width], ACT.Exp, bias=sums[:, 0, n:n + 1], scale=scale,
                  accum_out=sums[:, 1, n:n + 1], w=(t, w))
            b.free = [t]
            t2 = V(ve.reciprocal, sums[:, 1, n:n + 1], sums[:, 1, n:n + 1], w=(t,))
            return t, t2

        for l in range(2):
            cL = colL[l]
            w_mix = T["mix_w_in_2"][l].rearrange("(k p) n -> p k n", p=128)
            barrier()
            t_XT = turn(XT, xtok, [t_x])
            cq = arena(2, 2, 256, reset=base)
            cT = arena(2, 2, 256)
            qh = arena(8, 256, p=96)
            Kh = arena(8, 256, p=96)
            va = arena(2, 512)
            hp = arena(4, 286)
            yc = arena(4, 256)
            cat = arena(8, 256)
            otk = AR[:, base:base + 1024].rearrange("p (a b) -> p a b", a=2)
            krw = arena(8, 96)
            tq_ = [arena(2, 256, p=96) for _ in range(1)]
            pr = [arena(256) for _ in range(3)]
            pT = [arena(256) for _ in range(3)]
            sgc = arena(256)
            rowm = load_rows([row(T["mix_b_in_2"][l], 0, 512)])
            s = load((8, 512), [(lambda v: v, w_mix[:, :, 0:512])])
            tcq = []
            for tt in range(2):
                b = token(lambda k: XT[:, k, tt * 128:(tt + 1) * 128], lambda k: s.v[:, k, :], 512,
                          [s.ready] + t_XT)
                t = V(ve.tensor_tensor, cq[:, tt, :, :].rearrange("p a b -> p (a b)"), b.t[:, :], rowm.t[:, 0:512],
                      ALU.add, w=(b.tk, rowm.ready))
                b.free = [t]
                for a in range(2):
                    tcq.append(A(ae.activation, sgc, cq[:, tt, a, :], ACT.Square,
                                 accum_out=rq[:, tt * 2 + a:tt * 2 + a + 1], w=(t, tcq[-1] if tcq else None)))
            rowm.free = [t]
            s.free = [b.tk]
            t = V(ve.tensor_scalar, rq[:, 0:4], rq[:, 0:4], 1.0 / 256, 1e-6, ALU.mult, ALU.add, w=(tcq,))
            t = G(ge.tensor_tensor, rq[:, 0:4], rq[:, 0:4], C("nhalf")[:, 0:4], ALU.pow, w=(t,))
            for tt in range(2):
                for a in range(2):
                    t2 = V(ve.tensor_scalar, cq[:, tt, a, :], cq[:, tt, a, :], rq[:, tt * 2 + a:tt * 2 + a + 1],
                           None, ALU.mult, w=(t,))
            t_cT = []
            for a in range(2):
                t_cT += turn(cT[:, a], cq[:, :, a, :], [t2], cL[:, 132 + 2 * a:134 + 2 * a], None, chunks=2)
            tkz = G(ge.memset, krw, 0.0)
            t_kr = small([(krw[:, :, 64:96], w_mix[:, :, 512:544])], w=(tkz,))
            b = feature(lambda k: krw[:, k, :], X, [t_kr])
            krr = tq_[0]
            t = A(ae.activation, krr[:, 0, :], b.t[0:96, 0:256], ACT.Identity, bias=krb[:, l:l + 1], scale=1.0,
                  w=(b.tk, t_krb))
            b.free = [t]
            b = bank()
            tk = mm(b.t[0:96, 0:256], C("rot", 96), krr[:, 0, :], True, True, w=(b.w, t), inc=True)
            t2 = V(ve.tensor_tensor, krr[:, 1, :], b.t[0:96, 0:256], RS, ALU.mult, w=(tk, t_rs))
            b.free = [t2]
            t3 = V(ve.tensor_tensor, krr[:, 0, :], krr[:, 0, :], RC, ALU.mult, w=(tk, t_rc))
            t3 = V(ve.tensor_tensor, krr[:, 0, :], krr[:, 0, :], krr[:, 1, :], ALU.add, w=(t3, t2))
            for h in range(8):
                t_kh = G(ge.tensor_copy, Kh[64:96, h, :], krr[64:96, 0, :], w=(t3,))
            sa = load((8, 512), [(lambda v: v, w_mix[:, :, 544:1056])])
            sg_ = load((8, 512), [(lambda v: v, w_mix[:, :, 1056:1568])])
            t_hz = G(ge.memset, hp[:, :, 0:30], 0.0)
            t_h = []
            tsg = None
            for f in range(4):
                ba = feature(lambda k: sa.v[:, k, f * 128:(f + 1) * 128], X, [sa.ready])
                bg = feature(lambda k: sg_.v[:, k, f * 128:(f + 1) * 128], X, [sg_.ready])
                t = A(ae.activation, sgc, bg.t[:, 0:256], ACT.Sigmoid, bias=cL[:, 128 + f:129 + f], scale=1.0,
                      w=(bg.tk, tsg, t_cL[l], tcq))
                bg.free = [t]
                t = V(ve.scalar_tensor_tensor, hp[:, f, 30:286], ba.t[:, 0:256], cL[:, 124 + f:125 + f], sgc,
                      ALU.add, ALU.mult, w=(t, ba.tk))
                ba.free = [t]
                tsg = t
                t_h.append(t)
            sa.free = [ba.tk]
            sg_.free = [bg.tk]
            su = load((3584,), [(lambda v: v[:, 0:1536].rearrange("p (k n) -> p k n", k=2),
                                 T["mla_w_uq_2"][l].rearrange("(k p) n -> p k n", p=128)),
                                (lambda v: v[:, 1536:3584].rearrange("p (k n) -> p k n", k=2),
                                 T["mla_w_ukv_2"][l].rearrange("(k p) n -> p k n", p=128))])
            wuq = su.v[:, 0:1536].rearrange("p (k n) -> p k n", k=2)
            wukv = su.v[:, 1536:3584].rearrange("p (k h n) -> p k h n", k=2, h=8)
            for hh in range(4):
                b = bank()
                for i in range(2):
                    h = 2 * hh + i
                    for k in range(2):
                        tk = mm(b.t[0:64, i * 256:(i + 1) * 256], wukv[:, k, h, 0:64], cT[:, 1, k, :], k == 0,
                                k == 1, w=(b.w, su.ready, t_cT), inc=(i == 1 and k == 1))
                t_kh2 = A(ae.activation, Kh[0:64, 2 * hh:2 * hh + 2, :],
                          b.t[0:64, :].rearrange("p (a b) -> p a b", a=2), ACT.Copy, w=(tk,))
                b.free = [t_kh2]
            for tt in range(2):
                b = bank()
                for k in range(2):
                    tk = mm(b.t[:, :].rearrange("p (h n) -> p h n", h=8), cT[:, 1, k, tt * 128:(tt + 1) * 128],
                            wukv[:, k, :, 64:128], k == 0, k == 1, w=(b.w, su.ready, t_cT), inc=(k == 1))
                t_va = A(ae.activation, va[:, tt, :], b.t[:, :], ACT.Copy, w=(tk,))
                b.free = [t_va]
            t_q = t3
            for hh in range(4):
                b = bank()
                for i in range(2):
                    h = 2 * hh + i
                    for k in range(2):
                        tk = mm(b.t[0:96, i * 256:(i + 1) * 256], wuq[:, k, h * 96:(h + 1) * 96], cT[:, 0, k, :],
                                k == 0, k == 1, w=(b.w, su.ready, t_cT), inc=(i == 1 and k == 1))
                qv = qh[:, 2 * hh:2 * hh + 2, :]
                t = A(ae.activation, qv, b.t[0:96, :].rearrange("p (a b) -> p a b", a=2), ACT.Copy, w=(tk,))
                b.free = [t]
                b = bank()
                tk = mm(b.t[0:96, :], C("rot", 96), qv.rearrange("p a b -> p (a b)"), True, True, w=(b.w, t),
                        inc=True)
                for i in range(2):
                    t2 = V(ve.tensor_tensor, tq_[0][:, i, :], b.t[0:96, i * 256:(i + 1) * 256], RS, ALU.mult,
                           w=(tk, t_rs, t_q, t_kh))
                    t3 = V(ve.tensor_tensor, qv[:, i, :], qv[:, i, :], RC, ALU.mult, w=(tk, t_rc))
                b.free = [t2]
                t_q = V(ve.tensor_tensor, qv, qv, tq_[0], ALU.add, w=(t3, t2))
            su.free = [tk]
            SCL = 96.0 ** -0.5
            t_o = []
            n_ = 0
            prf = [None] * 3
            ptf = [None] * 3
            for j in range(2):
                kn = 128 * (j + 1)
                bo_ = bank()
                bo_.pin = True
                pend = {}
                for step in range(8 + 2):
                    if step < 8:
                        h = step
                        i = n_ % 3
                        b = bank()
                        mm(b.t[:, 0:kn], qh[:, h, j * 128:(j + 1) * 128], Kh[:, h, 0:kn], True, False,
                           w=(b.w, t_q, t_kh, t_kh2))
                        zo = CONST["zero"][0] + 128 * (1 - j)
                        b.tk = mm(b.t[:, 0:kn], C("ident"), cst[:, zo:zo + kn], False, True, inc=True)
                        te, tr_ = softmax(b, j * 8 + h, kn, pr[i][:, 0:kn], SCL, [prf[i]])
                        pend[h] = (i, te, tr_)
                        n_ += 1
                    if 1 <= step < 9:
                        h = step - 1
                        i, te, tr_ = pend[h]
                        b = bank()
                        for m in range(j + 1):
                            tk = tr(b.t[:, m * 128:(m + 1) * 128], pr[i][:, m * 128:(m + 1) * 128], w=(b.w, te),
                                    inc=(m == j))
                        prf[i] = tk
                        t = V(ve.tensor_copy, pT[i][:, 0:kn], b.t[:, 0:kn], w=(tk, ptf[i]))
                        b.free = [t]
                        pend[h] = (i, t, tr_)
                    if step >= 2:
                        h = step - 2
                        i, t, tr_ = pend[h]
                        for m in range(j + 1):
                            tk = mm(bo_.t[:, h * 64:(h + 1) * 64], pT[i][:, m * 128:(m + 1) * 128],
                                    va[:, m, h * 64:(h + 1) * 64], m == 0, m == j, w=(bo_.w, t, t_va), inc=(m == j))
                        ptf[i] = tk
                for h in range(8):
                    t = V(ve.tensor_scalar, otk[:, j, h * 64:(h + 1) * 64], bo_.t[:, h * 64:(h + 1) * 64],
                          sums[:, 1, j * 8 + h:j * 8 + h + 1], None, ALU.mult, w=(tk, pend[7][2]))
                bo_.free = [t]
                bo_.pin = False
                t_o.append(t)
            t_cat = turn(cat, otk, t_o, chunks=4)
            tcv = []
            for f in range(4):
                t = V(ve.tensor_scalar, yc[:, f, :], hp[:, f, 0:256], cL[:, f:f + 1], cL[:, 136 + f:137 + f],
                      ALU.mult, ALU.add, w=(t_h, t_hz))
                for j in range(1, 31):
                    t = V(ve.scalar_tensor_tensor, yc[:, f, :], hp[:, f, j:j + 256],
                          cL[:, 4 * j + f:4 * j + f + 1], yc[:, f, :], ALU.mult, ALU.add, w=(t,))
                tcv.append(t)
            b = bank()
            for f in range(4):
                tk = mm(b.t[:, 0:256], C("mean"), yc[:, f, :], f == 0, f == 3, w=(b.w, tcv[f]), inc=(f == 3))
            tsq = []
            for f in range(4):
                t = V(ve.tensor_tensor, yc[:, f, :], yc[:, f, :], b.t[:, 0:256], ALU.subtract, w=(tk,))
                tsq.append(A(ae.activation, cat[:, 4 + f, :], yc[:, f, :], ACT.Square, w=(t,)))
            b.free = [t]
            b = bank()
            for f in range(4):
                tk = mm(b.t[:, 0:256], C("mean"), cat[:, 4 + f, :], f == 0, f == 3, w=(b.w, tsq[f]), inc=(f == 3))
            t = V(ve.tensor_scalar, sgc, b.t[:, 0:256], 1e-5, None, ALU.add, w=(tk,))
            b.free = [t]
            t = A(ae.activation, sgc, sgc, ACT.Sqrt, w=(t,))
            t = V(ve.reciprocal, sgc, sgc, w=(t,))
            for f in range(4):
                t2 = V(ve.tensor_tensor, yc[:, f, :], yc[:, f, :], sgc, ALU.mult, w=(t,))
                t_cv = A(ae.activation, cat[:, 4 + f, :], yc[:, f, :], ACT.Silu, bias=cL[:, 144 + f:145 + f],
                         scale=cL[:, 140 + f:141 + f], w=(t2, tk))
            bs = dense(cat, T["mix_w_o_2"][l].rearrange("(k p) n -> p k n", p=128), [t_cat, t_cv])
            t = residual(ALPHA2, bs, None, None)
            t_x = ln_affine(T["ln1_g_2"][l], T["ln1_b_2"][l], t)

            barrier()
            w_kv = T["xa_w_kv_2"][l].rearrange("(k p) n -> p k n", p=128)
            w_q = T["xa_w_q_2"][l].rearrange("(k p) n -> p k n", p=128)
            kx = arena(8, 256, reset=base)
            vx = arena(2, 1024)
            qx = arena(8, 256)
            ox = arena(8, 256)
            pr = [arena(256) for _ in range(4)]
            pT = [arena(2, 256) for _ in range(2)]
            M_ = lambda k: memT[:, k, :]
            for hf in range(2):
                s = load((8, 512), [(lambda v: v, w_kv[:, :, hf * 512:(hf + 1) * 512])])
                for f in range(4):
                    b = feature(lambda k: s.v[:, k, f * 128:(f + 1) * 128], M_, [s.ready, t_mT])
                    t_kx = A(ae.activation, kx[:, hf * 4 + f, :], b.t[:, 0:256], ACT.Copy, w=(b.tk,))
                    b.free = [t_kx]
                s.free = [b.tk]
            for hf in range(2):
                s = load((8, 512), [(lambda v: v, w_kv[:, :, 1024 + hf * 512:1024 + (hf + 1) * 512])])
                for tt in range(2):
                    b = token(lambda k: memT[:, k, tt * 128:(tt + 1) * 128], lambda k: s.v[:, k, :], 512, [s.ready])
                    t_vx = A(ae.activation, vx[:, tt, hf * 512:(hf + 1) * 512], b.t[:, :], ACT.Copy, w=(b.tk,))
                    b.free = [t_vx]
                s.free = [b.tk]
            t_XT = turn(XT, xtok, [t_x])
            for hf in range(2):
                s = load((8, 512), [(lambda v: v, w_q[:, :, hf * 512:(hf + 1) * 512])])
                for f in range(4):
                    b = feature(lambda k: s.v[:, k, f * 128:(f + 1) * 128], X, [s.ready] + t_XT)
                    t_qx = A(ae.activation, qx[:, hf * 4 + f, :], b.t[:, 0:256], ACT.Copy, w=(b.tk,))
                    b.free = [t_qx]
                s.free = [b.tk]
            prf = [None] * 4
            ptf = [None] * 2
            pend = {}
            for step in range(4 + 2):
                if step < 4:
                    h = step
                    for j in range(2):
                        i = (2 * h + j) % 4
                        b = bank()
                        for c in range(2):
                            b.tk = mm(b.t[:, 0:256], qx[:, 2 * h + c, j * 128:(j + 1) * 128], kx[:, 2 * h + c, :],
                                      c == 0, c == 1, w=(b.w, t_qx, t_kx), inc=(c == 1))
                        te, tr_ = softmax(b, 16 + 2 * h + j, 256, pr[i], 1.0 / 16, [prf[i]])
                        pend[(h, j)] = V(ve.tensor_scalar, pr[i], pr[i],
                                         sums[:, 1, 16 + 2 * h + j:17 + 2 * h + j], None, ALU.mult, w=(te, tr_))
                if 1 <= step < 5:
                    h = step - 1
                    b = bank()
                    for j in range(2):
                        i = (2 * h + j) % 4
                        for m in range(2):
                            tk = tr(b.t[:, m * 256 + j * 128:m * 256 + (j + 1) * 128],
                                    pr[i][:, m * 128:(m + 1) * 128], w=(b.w, pend[(h, j)]), inc=(m == 1))
                        prf[i] = tk
                    t = V(ve.tensor_copy, pT[h % 2].rearrange("p a b -> p (a b)"), b.t[:, :], w=(tk, ptf[h % 2]))
                    b.free = [t]
                    pend[h] = t
                if step >= 2:
                    h = step - 2
                    for d in range(2):
                        b = bank()
                        o0 = h * 256 + d * 128
                        for m in range(2):
                            tk = mm(b.t[:, 0:256], vx[:, m, o0:o0 + 128], pT[h % 2][:, m, :], m == 0, m == 1,
                                    w=(b.w, t_vx, pend[h]), inc=(m == 1))
                        t_ox = A(ae.activation, ox[:, 2 * h + d, :], b.t[:, 0:256], ACT.Copy, w=(tk,))
                        b.free = [t_ox]
                    ptf[h % 2] = tk
            bs = dense(ox, T["xa_w_o_2"][l].rearrange("(k p) n -> p k n", p=128), [t_ox])
            t = residual(ALPHA2, bs, None, None)
            t_x = ln_affine(T["ln2_g_2"][l], T["ln2_b_2"][l], t)

            barrier()
            t_XT = turn(XT, xtok, [t_x])
            ff_ = arena(22, 256, reset=base)
            sl = [arena(256) for _ in range(2)]
            slf = [None] * 2
            w_f = T["ffn_w_in_2"][l].rearrange("(k p) n -> p k n", p=128)
            w_d = T["ffn_w_down_2"][l].rearrange("(k p) n -> p k n", p=128)
            for q in range(11):
                s = load((2, 8, 256), [(lambda v: v[:, 0], w_f[:, :, q * 256:(q + 1) * 256]),
                                       (lambda v: v[:, 1], w_f[:, :, 2816 + q * 256:2816 + (q + 1) * 256])])
                for g2 in range(2):
                    f = 2 * q + g2
                    i = f % 2
                    bg = feature(lambda k: s.v[:, 0, k, g2 * 128:(g2 + 1) * 128], X, [s.ready] + t_XT)
                    bu = feature(lambda k: s.v[:, 1, k, g2 * 128:(g2 + 1) * 128], X, [s.ready])
                    t = A(ae.activation, sl[i], bg.t[:, 0:256], ACT.Silu, w=(bg.tk, slf[i]))
                    bg.free = [t]
                    t_f = V(ve.tensor_tensor, ff_[:, f, :], bu.t[:, 0:256], sl[i], ALU.mult, w=(t, bu.tk))
                    bu.free = [t_f]
                    slf[i] = t_f
                s.free = [bu.tk]
            bb = {(tt, h): bank() for h in range(2) for tt in range(2)}
            for q in range(6):
                kn = 4 if q < 5 else 2
                s = load((kn, 1024), [(lambda v: v, w_d[:, 4 * q:4 * q + kn, :])])
                for k in range(kn):
                    kk = 4 * q + k
                    for (tt, h), b in bb.items():
                        b.tk = mm(b.t[:, :], ff_[:, kk, tt * 128:(tt + 1) * 128], s.v[:, k, h * 512:(h + 1) * 512],
                                  kk == 0, kk == 21, w=(b.w, s.ready, t_f), inc=(k == kn - 1))
                s.free = [b.tk]
            t = residual(ALPHA2, [(tt, h, b) for (tt, h), b in bb.items()], None, None)
            t_x = ln_affine(T["ln3_g_2"][l], T["ln3_b_2"][l], t)
        return finish(nc, ctx, PE, V, A, G, SP, out, xtok, sem)


def finish(nc, ctx, PE, V, A, G, SP, out, xtok, sem):
    s = sem("s_out")
    toks = [q.last() for q in (PE, V, A, G) if q.count]
    for tt in range(2):
        SP.items.append((toks, nc.sync.dma_start, (out[0, tt * 128:(tt + 1) * 128, :], xtok[:, tt, :]), {}, s, 16))
    SP.items.append(((( s, 32),), None, (), {}, None, 0))
    block = ctx.enter_context(nc.Block())

    @block.sync
    def _(eng):
        emit(eng, SP.items)

    @block.gpsimd
    def _(eng):
        emit(eng, G.items)

    @block.scalar
    def _(eng):
        emit(eng, A.items)

    @block.vector
    def _(eng):
        emit(eng, V.items)

    @block.tensor
    def _(eng):
        emit(eng, PE.items)


_INS = ["x", "c", "ctx", "c_ctx", "w_ada", "b_ada", "w_in", "b_in", "pool_w", "pool_scale", "qk_conv_w", "qk_conv_b",
        "mlstm_norm_g", "sgu_ln_g", "sgu_ln_b", "sgu_w", "sgu_b", "w_br_pool", "w_br_mlstm", "w_br_sgu", "w_out",
        "ln1_g", "ln1_b", "w_router", "b_router", "w_gate_up", "b_gate_up", "w_down", "b_down", "ln2_g", "ln2_b",
        "mem_2", "positions_2", "mix_w_in_2", "mix_b_in_2", "mla_q_norm_2", "mla_w_uq_2", "mla_kv_norm_2",
        "mla_w_ukv_2", "conv_dw_w_2", "conv_dw_b_2", "conv_norm_g_2", "conv_norm_b_2", "mix_w_o_2", "ln1_g_2",
        "ln1_b_2", "xa_w_q_2", "xa_w_kv_2", "xa_w_o_2", "ln2_g_2", "ln2_b_2", "ffn_w_in_2", "ffn_w_down_2",
        "ln3_g_2", "ln3_b_2"]


def kernel(**inputs):
    import concourse.bacc as bacc
    from concourse.bass_utils import run_bass_kernel_spmd

    nc = bacc.Bacc("TRN2", target_bir_lowering=False, num_devices=1)
    arrays, T = {}, {}
    for name in _INS:
        a = np.ascontiguousarray(inputs[name])
        arrays["in_" + name] = a
        T[name] = nc.dram_tensor("in_" + name, a.shape, mybir.dt.from_np(a.dtype), kind="ExternalInput").ap()
    arrays["in_const"] = constants()
    T["const"] = nc.dram_tensor("in_const", arrays["in_const"].shape, F32, kind="ExternalInput").ap()
    out = nc.dram_tensor("out_0", (1, 256, 1024), F32, kind="ExternalOutput").ap()
    build(nc, T, out)
    r = run_bass_kernel_spmd(nc, [arrays], core_ids=[0])
    return r.results[0]["out_0"]
```

```python
from contextlib import ExitStack

import numpy as np

import concourse.bass as bass
from concourse import mybir

F32 = mybir.dt.float32
I32 = mybir.dt.int32
ALU = mybir.AluOpType
ACT = mybir.ActivationFunctionType
AX = mybir.AxisListType
ALPHA1 = 2.0 ** 0.25
ALPHA2 = 4.0 ** 0.25
NEG = -1e30
NSLOT = 5
STEM = 640

CONST = {}
_at = 0
for _name, _w in (("ident", 128), ("maskf", 128), ("maskb", 128), ("zero", 128), ("maskc", 128), ("pool", 512), ("rot", 96),
                  ("freq", 1), ("sel", 1024), ("mean", 128), ("ones", 128), ("nhalf", 8), ("tri", 128), ("iota", 512)):
    CONST[_name] = (_at, _w)
    _at += _w
NCONST = _at


def constants():
    c = np.zeros((128, NCONST), np.float32)
    p = np.arange(128)

    def put(name, a):
        o, w = CONST[name]
        c[:a.shape[0], o:o + w] = a

    put("ident", np.eye(128))
    put("maskf", np.where(p[:, None] <= p[None, :], 0.0, NEG))
    put("maskb", np.where(p[:, None] >= p[None, :], 0.0, NEG))
    put("maskc", np.where((p[:, None] < 64) & (p[None, :] >= 64), NEG, 0.0))
    pool = np.zeros((128, 4, 128))
    for g, w in enumerate((2, 4, 8, 16)):
        for t in range(128):
            base, tt = t // 64 * 64, t % 64
            lo, hi = max(tt - w // 2, 0), min(tt + w // 2, 64)
            pool[base + lo:base + hi, g, t] += 1.0 / (hi - lo)
            pool[t, g, t] -= 1.0
    put("pool", pool.reshape(128, 512))
    rot = np.zeros((96, 96))
    freq = np.zeros((96, 1), np.float32)
    for i in range(16):
        rot[80 + i, 64 + i] = -1.0
        rot[64 + i, 80 + i] = 1.0
    inv = np.float32(10000.0) ** (-np.arange(0, 32, 2, dtype=np.float32) / np.float32(32))
    freq[64:80, 0] = inv
    freq[80:96, 0] = inv
    put("rot", rot)
    put("freq", freq)
    sel = np.zeros((64, 8, 128))
    for r in range(8):
        sel[32 * (r // 4) + r % 4, r, :] = 1.0
    put("sel", sel.reshape(64, 1024))
    put("mean", np.full((128, 128), 1.0 / 512))
    put("ones", np.ones((128, 128)))
    put("tri", np.where(p[:, None] < p[None, :], 1.0, 0.0))
    put("iota", np.broadcast_to((64 * np.arange(4)[:, None, None] + np.zeros((1, 2, 1)) +
                                 np.arange(64)[None, None, :]).reshape(1, 512), (128, 512)))
    put("nhalf", np.full((128, 8), -0.5))
    return c


class Queue:

    def __init__(self, sems, serial=False):
        self.serial = serial
        self.sems, self.n, self.count, self.items = sems, 0, 0, []

    def __call__(self, fn, *args, w=(), inc=True, **kw):
        if self.serial and self.count:
            w = tuple(w) + (self.last(),)
        if self.count >= 1000 and len(self.sems) > 1:
            self.n += 1
            self.count = 0
        sem = self.sems[self.n] if inc else None
        self.items.append((w, fn, args, kw, sem, 1))
        if inc:
            self.count += 1
            return (sem, self.count)
        return None

    def last(self):
        return (self.sems[self.n], self.count)


class Branch:

    def __init__(self, flag, tiles):
        self.flag, self.tiles = flag, tiles


def emit(eng, items, seen=None):
    seen = {} if seen is None else seen

    def wait(w):
        if w is None:
            return
        if isinstance(w, list):
            for x in w:
                wait(x)
            return
        sem, value = w
        if seen.get(id(sem), 0) < value:
            eng.wait_ge(sem, value)
            seen[id(sem)] = value

    def branch(number, tiles, depth, seen):
        with eng.If(number >= depth):
            emit(eng, tiles[0], seen)
            if len(tiles) > 1:
                branch(number, tiles[1:], depth + 1, dict(seen))
        with eng.Else():
            skipped = {}
            for tile in tiles:
                for w, fn, args, kw, sem, by in tile:
                    if sem is not None:
                        skipped[id(sem)] = (sem, skipped.get(id(sem), (sem, 0))[1] + by)
            for sem, n in skipped.values():
                eng.sem_inc(sem, n)

    for item in items:
        if isinstance(item, Branch):
            number = eng.value_load(item.flag, min_val=0, max_val=3)
            branch(number, item.tiles, 1, dict(seen))
            continue
        w, fn, args, kw, sem, by = item
        for x in w:
            wait(x)
        if fn is None:
            continue
        ins = fn(*args, **kw)
        if sem is not None:
            ins.then_inc(sem, by)


class Box:

    def __init__(self, t, sem=None):
        self.t, self.sem, self.n, self.free, self.ready = t, sem, 0, [], None
        self.pin, self.w = False, []


def build(nc, T, out):
    ctx = ExitStack()
    with ctx:
        def sb(name, shape, dt=F32):
            return ctx.enter_context(nc.sbuf_tensor(name, shape, dt))

        def sem(name):
            return ctx.enter_context(nc.semaphore(name))

        PE = Queue([sem(f"s_pe{i}") for i in range(6)])
        V = Queue([sem(f"s_v{i}") for i in range(8)])
        A = Queue([sem(f"s_a{i}") for i in range(6)])
        G = Queue([sem(f"s_g{i}") for i in range(4)], serial=True)
        SP = Queue([])
        ve, ae, ge, pe = nc.vector, nc.scalar, nc.gpsimd, nc.tensor

        cst = sb("cst", [128, NCONST])

        def C(name, rows=128):
            o, w = CONST[name]
            return cst[0:rows, o:o + w]

        slots = [Box(sb(f"slot{i}", [128, 4096]), sem(f"s_w{i}")) for i in range(NSLOT)]
        rows = [Box(sb(f"rows{i}", [128, 2048]), sem(f"s_r{i}")) for i in range(2)]
        banks = [Box(ctx.enter_context(nc.psum_tensor(f"ps{i}", [128, 512], F32))) for i in range(8)]
        small_sems = [sem(f"s_c{i}") for i in range(26)]
        state = {"slot": 0, "row": 0, "bank": 0, "small": 0}

        def load_into(box, parts):
            free = box.free
            assert free is not None
            box.free = None
            for dst, src in parts:
                SP.items.append(([free], nc.sync.dma_start, (dst, src), {}, box.sem, 16))
            box.n += 16 * len(parts)
            box.ready = (box.sem, box.n)
            return box

        def slot():
            b = slots[state["slot"] % NSLOT]
            state["slot"] += 1
            return b

        def load(shape, parts):
            b = slot()
            n = int(np.prod(shape))
            view = b.t[:, 0:n]
            if len(shape) == 2:
                view = view.rearrange("p (a b) -> p a b", a=shape[0])
            elif len(shape) == 3:
                view = view.rearrange("p (a b c) -> p a b c", a=shape[0], b=shape[1])
            load_into(b, [(f(view), src) for f, src in parts])
            b.v = view
            return b

        def load_rows(vectors):
            b = rows[state["row"] % 2]
            state["row"] += 1
            parts, at = [], 0
            for v in vectors:
                n = v.shape[1]
                parts.append((b.t[:, at:at + n], v.broadcast_to((128, n))))
                at += n
            return load_into(b, parts)

        def small(parts, w=(), q=None):
            eng = nc.sync if q is None else nc.gpsimd
            s = small_sems[state["small"]]
            state["small"] += 1
            for dst, src in parts:
                (q or SP).items.append((list(w), eng.dma_start, (dst, src), {}, s, 16))
            return (s, 16 * len(parts))

        def bank():
            while banks[state["bank"] % 8].pin:
                state["bank"] += 1
            b = banks[state["bank"] % 8]
            state["bank"] += 1
            assert b.free is not None
            b.w, b.free = b.free, None
            return b

        def mm(o, l, r, start, stop, w=(), inc=False, tp=None):
            if tp is None:
                return PE(pe.matmul, o, l, r, w=w, inc=inc, start=start, stop=stop)
            return PE(pe.matmul, o, l, r, w=w, inc=inc, start=start, stop=stop, tile_position=tp)

        def tr(o, i, w=(), inc=False, k=128):
            return PE(pe.transpose, o, i, C("ident", k)[:, 0:k], w=w, inc=inc)

        def barrier():
            toks = [q.last() for q in (PE, V, A, G) if q.count]
            for q in (PE, V, A, G):
                q.items.append((list(toks), None, (), {}, None, 0))

        def row(v, a=None, b=None):
            v = v.rearrange("(o n) -> o n", o=1)
            return v if a is None else v[:, a:b]

        xtok = sb("xtok", [128, 2, 1024])
        XT = sb("XT", [128, 8, 256])
        st6 = sb("st6", [128, 16, 6])
        mv = sb("mv", [128, 16, 2])
        rstd = sb("rstd", [128, 16])
        wrt = sb("wrt", [128, 8, 32])
        AR = sb("AR", [128, 17020])
        ar = {"at": 0}

        def arena(*shape, p=128, reset=None):
            if reset is not None:
                ar["at"] = reset
            n = int(np.prod(shape))
            v = AR[0:p, ar["at"]:ar["at"] + n]
            ar["at"] += n
            assert ar["at"] <= 17020, ar["at"]
            if len(shape) == 2:
                v = v.rearrange("p (a b) -> p a b", a=shape[0])
            if len(shape) == 3:
                v = v.rearrange("p (a b c) -> p a b c", a=shape[0], b=shape[1])
            return v

        def rows128(v):
            return v.rearrange("(r c) -> r c", c=128)

        def columns(parts, dst, i, w=()):
            n = sum(s.shape[0] for _, s in parts)
            t = small([(stage[i][a:a + s.shape[0], :], s) for a, s in parts])
            b = bank()
            tk = tr(b.t[:, 0:n], stage[i][0:n, :], w=(t, t_const, b.w), inc=True, k=n)
            tv = V(ve.tensor_copy, dst, b.t[:, 0:n], w=(tk,) + tuple(w))
            b.free = [tv]
            return tk, tv

        def stats(srcs, eps, base, w=()):
            n = len(srcs)
            for i, s in enumerate(srcs):
                f = s.shape[1]
                if f > 512:
                    for k in range(2):
                        t = V(ve.bn_stats, st6[:, 2 * i + k + base, :], s[:, k * 512:(k + 1) * 512], w=w)
                else:
                    t = V(ve.bn_stats, st6[:, i + base, :], s, w=w)
            for i, s in enumerate(srcs):
                if s.shape[1] > 512:
                    src = st6[:, base + 2 * i:base + 2 * i + 2, :]
                else:
                    src = st6[:, base + i, :]
                t2 = V(ve.bn_aggr, mv[:, base + i, :], src, w=(t,))
            t3 = V(ve.tensor_scalar, rstd[:, base:base + n], mv[:, base:base + n, 1], eps, None, ALU.add, w=(t2,))
            return G(ge.tensor_tensor, rstd[:, base:base + n], rstd[:, base:base + n],
                     C("nhalf")[:, 0:n], ALU.pow, w=(t3, t_const))

        def normal(dst, src, i, w=()):
            return V(ve.tensor_scalar, dst, src, mv[:, i, 0:1], rstd[:, i:i + 1], ALU.subtract, ALU.mult, w=w)

        def turn(dst, src, w, scale=None, bias=None, chunks=8):
            last = None
            for k0 in range(0, chunks, 2):
                b = bank()
                for k in (k0, k0 + 1):
                    for tt in range(2):
                        j = (k - k0) * 2 + tt
                        t = tr(b.t[:, j * 128:(j + 1) * 128], src[:, tt, k * 128:(k + 1) * 128],
                               w=(b.w, w), inc=(j == 3))
                for k in (k0, k0 + 1):
                    src_ = b.t[:, (k - k0) * 256:(k - k0 + 1) * 256]
                    eng = A if k0 % 4 else V
                    if eng is A:
                        last = A(ae.activation, dst[:, k, :], src_, ACT.Identity,
                                 bias=(0.0 if bias is None else bias[:, k:k + 1]),
                                 scale=(1.0 if scale is None else scale[:, k:k + 1]), w=(t,))
                        la = last
                    else:
                        if scale is None:
                            last = V(ve.tensor_copy, dst[:, k, :], src_, w=(t,))
                        else:
                            last = V(ve.tensor_scalar, dst[:, k, :], src_, scale[:, k:k + 1],
                                     0.0 if bias is None else bias[:, k:k + 1], ALU.mult, ALU.add, w=(t,))
                        lv = last
                b.free = [last]
            return [la, lv] if chunks > 2 else [lv]

        def feature(wcols, xT, w, n=256, kk=8):
            b = bank()
            for k in range(kk):
                l = wcols(k)
                t = mm(b.t[0:l.shape[1], 0:n], l, xT(k), k == 0, k == kk - 1, w=(b.w, w), inc=(k == kk - 1))
            b.tk = t
            return b

        def token(xT, wcols, n, w, kk=8, b=None, first=True, last=True):
            b = b or bank()
            for k in range(kk):
                t = mm(b.t[:, 0:n], xT(k), wcols(k), first and k == 0, last and k == kk - 1,
                       w=(b.w, w) if first else (w,), inc=(k == kk - 1))
            b.tk = t
            return b

        stage = [AR[:, 7168 + 128 * i:7296 + 128 * i] for i in range(10)]
        t_const = small([(cst[:, :], T["const"])])
        xc = arena(2, 1024)
        t_x = small([(xtok[:, tt, :], T["x"][0, tt * 128:(tt + 1) * 128, :]) for tt in range(2)])
        t_c = small([(xc[:, tt, :], T["ctx"][0, tt * 128:(tt + 1) * 128, :]) for tt in range(2)])
        b_in = T["b_in"][0]
        colA = sb("colA", [128, 128])
        colB = sb("colB", [128, 32])
        b_ada = T["b_ada"][0]
        _, t_cA = columns([(0, rows128(T["c"][0])), (8, rows128(T["c_ctx"])), (16, rows128(b_ada)),
                           (64, rows128(b_in[256:1280])), (72, rows128(b_in[1792:2304])),
                           (76, rows128(b_in[2320:2576])), (78, rows128(b_in[2832:5904])),
                           (102, rows128(T["pool_scale"][0])),
                           (104, T["qk_conv_w"][0].rearrange("j (r c) -> (j r) c", c=128))], colA[:, :], 0)
        _, t_cB = columns([(0, rows128(T["qk_conv_b"][0])), (8, rows128(T["mlstm_norm_g"][0]))], colB[:, 0:12], 1)
        rowb = load_rows([row(b_in, 0, 256), row(b_in, 1280, 1792), row(b_in, 2576, 2832),
                          row(T["sgu_ln_g"][0]), row(T["sgu_ln_b"][0]),
                          T["sgu_b"][0].rearrange("g (o t) -> o (g t)", o=1)])
        colL = [sb(f"colL{l}", [128, 152]) for l in range(2)]
        t_cL = []
        for l in range(2):
            columns([(0, T["conv_dw_w_2"][l].rearrange("j (r c) -> (j r) c", c=128))], colL[l][:, 0:124], 2 + 2 * l)
            t_cL.append(columns([(0, rows128(T["mix_b_in_2"][l][544:1568])), (8, rows128(T["mla_q_norm_2"][l])),
                                 (10, rows128(T["mla_kv_norm_2"][l])), (12, rows128(T["conv_dw_b_2"][l])),
                                 (16, rows128(T["conv_norm_g_2"][l])), (20, rows128(T["conv_norm_b_2"][l]))],
                                colL[l][:, 124:148], 3 + 2 * l)[1])
        poolw = sb("poolw", [128, 2, 128])
        sguw = sb("sguw", [128, 4, 128])
        gb = sb("gb", [64, 2])
        tz = [G(ge.memset, poolw[:, :, :], 0.0), G(ge.memset, gb[:, :], 0.0)]
        gsem = small_sems[state["small"]]
        state["small"] += 1
        gl = [(poolw[(g % 2) * 64:(g % 2) * 64 + 64, g // 2, (g % 2) * 64:(g % 2) * 64 + 64], T["pool_w"][0, g])
              for g in range(4)]
        for kind in range(4):
            o = 2304 + 4 * kind
            p0 = 32 * (kind // 2)
            gl.append((gb[p0:p0 + 4, kind % 2:kind % 2 + 1], b_in[o:o + 4].rearrange("(a o) -> a o", o=1)))
        gl.append((sguw[:, :, :], T["sgu_w"][0].rearrange("g t s -> t g s")))
        for d, s in gl:
            SP.items.append(([tz], nc.sync.dma_start, (d, s), {}, gsem, 16))
        t_gl = (gsem, 16 * len(gl))

        w_ada = T["w_ada"][0].rearrange("(k p) n -> p k n", p=128)
        scT = sb("scT", [128, 2, 8])
        t_sc = A(ae.activation, scT[:, :, :].rearrange("p a b -> p (a b)"), colA[:, 0:16], ACT.Silu, w=(t_cA,))
        scB = arena(8, 128)
        for k in range(8):
            t_scb = V(ve.tensor_scalar, scB[:, k, :], C("ones"), scT[:, 0, k:k + 1], None, ALU.mult, w=(t_sc, t_const))
        modT = sb("modT", [128, 6, 8, 2])
        gB = sb("gB", [128, 2, 1024])
        rowg = load_rows([row(b_ada, 2048, 3072), row(b_ada, 5120, 6144)])

        def ada_cols(part):
            for h in range(2):
                s = load((8, 512), [(lambda v: v, w_ada[:, :, part * 1024 + h * 512:part * 1024 + (h + 1) * 512])])
                b = bank()
                for f in range(4):
                    for k in range(8):
                        t = mm(b.t[:, f * 2:f * 2 + 2], s.v[:, k, f * 128:(f + 1) * 128], scT[:, :, k],
                               k == 0, k == 7, w=(b.w, s.ready, t_sc), inc=(f == 3 and k == 7))
                s.free = [t]
                f0 = 16 + part * 8 + h * 4
                for src in range(2):
                    tv = V(ve.tensor_tensor, modT[:, part, h * 4:h * 4 + 4, src],
                           b.t[:, 0:8].rearrange("p (f s) -> p f s", s=2)[:, :, src], colA[:, f0:f0 + 4],
                           ALU.add, w=(t, t_cA))
                if part in (1, 4):
                    tv = V(ve.tensor_scalar, modT[:, part, h * 4:h * 4 + 4, :], modT[:, part, h * 4:h * 4 + 4, :],
                           1.0, None, ALU.add, w=(tv,))
                b.free = [tv]
            return tv

        def ada_rows(part, g):
            for h in range(2):
                s = load((8, 512), [(lambda v: v, w_ada[:, :, part * 1024 + h * 512:part * 1024 + (h + 1) * 512])])
                b = token(lambda k: scB[:, k, :], lambda k: s.v[:, k, :], 512, [s.ready, t_scb])
                s.free = [b.tk]
                o = g * 1024 + h * 512
                tv = V(ve.tensor_tensor, gB[:, g, h * 512:(h + 1) * 512], b.t[:, :], rowg.t[:, o:o + 512], ALU.add,
                       w=(b.tk, rowg.ready))
                b.free = [tv]
            return tv

        ada_cols(0)
        t_m1 = ada_cols(1)

        ts = stats([xtok[:, 0, :], xtok[:, 1, :], xc[:, 0, :], xc[:, 1, :]], 1e-5, 0, w=(t_x, t_c))
        xn = arena(2, 1024)
        for tt in range(2):
            tn = normal(xn[:, tt, :], xtok[:, tt, :], tt, w=(ts,))
            tnc = normal(xc[:, tt, :], xc[:, tt, :], 2 + tt, w=(ts,))
        XC = arena(8, 256, reset=5120)
        t_XT = turn(XT, xn, [tn], modT[:, 1, :, 0], modT[:, 0, :, 0])
        t_XC = turn(XC, xc, [tnc], modT[:, 1, :, 1], modT[:, 0, :, 1])
        ada_cols(3)
        t_m4 = ada_cols(4)
        ada_rows(2, 0)
        t_gB = ada_rows(5, 1)
        rowg.free = [t_gB]
        barrier()

        w_in = T["w_in"][0].rearrange("(k p) n -> p k n", p=128)
        X = lambda k: XT[:, k, :]
        XCk = lambda k: XC[:, k, :]
        zpad = arena(2, 258, reset=7168)
        cva = arena(256)
        cvb = arena(256)
        qkT = arena(12, 256)
        vaug = arena(4, 4, 129)
        kN = arena(4, 4, 128)
        bo = 0
        ptok = arena(2, 256, reset=0)
        vs = arena(2, 256)
        uT = arena(2, 256)
        soT = arena(4, 256)
        poolT = arena(2, 256)
        sguT = arena(2, 256)
        dT = arena(2, 256)
        assert ar["at"] <= 5120
        KS = 128.0 ** -0.5

        tz0 = V(ve.memset, zpad[:, :, 0:1], 0.0)
        tz1 = V(ve.memset, zpad[:, :, 257:258], 0.0, w=(tz0,))
        tz2 = V(ve.memset, vaug[:, :, :, 128:129], 1.0)

        s = load((8, 256), [(lambda v: v, w_in[:, :, 0:256])])
        for tt in range(2):
            b = token(lambda k: XT[:, k, tt * 128:(tt + 1) * 128], lambda k: s.v[:, k, :], 256, [s.ready] + t_XT)
            t_p = V(ve.tensor_tensor, ptok[:, tt, :], b.t[:, 0:256], rowb.t[:, 0:256], ALU.add, w=(b.tk, rowb.ready))
            b.free = [t_p]
        s.free = [b.tk]

        conv = {"i": 0, "tok": [tz1, tz1], "a": []}

        def qk(f, xT, dst):
            i = conv["i"] % 2
            conv["i"] += 1
            b = feature(lambda k: s.v[:, k, (f % 4) * 128:(f % 4 + 1) * 128], xT, [s.ready] + t_XT + t_XC)
            z = zpad[:, i, :]
            ta = A(ae.activation, z[:, 1:257], b.t[:, 0:256], ACT.Identity, bias=colA[:, 64 + f:65 + f], scale=1.0,
                   w=(b.tk, conv["tok"][i], t_cA))
            b.free = [ta]
            y = cva if i == 0 else cvb
            t = V(ve.tensor_scalar, y, z[:, 0:256], colA[:, 104 + f:105 + f], colB[:, f:f + 1], ALU.mult, ALU.add,
                  w=(ta, t_cB, conv["a"][-2:-1]))
            for j in (1, 2):
                t = V(ve.scalar_tensor_tensor, y, z[:, j:j + 256], colA[:, 104 + 8 * j + f:105 + 8 * j + f], y,
                      ALU.mult, ALU.add, w=(t,))
            conv["tok"][i] = t
            ta = A(ae.activation, dst, y, ACT.Silu, w=(t,))
            conv["a"].append(ta)
            if f >= 4:
                ta = V(ve.tensor_scalar, dst, dst, KS, None, ALU.mult, w=(ta,))
            return ta, b.tk

        for half in range(2):
            s = load((8, 512), [(lambda v: v, w_in[:, :, 256 + half * 512:768 + half * 512])])
            for f in range(4 * half, 4 * half + 4):
                t_qk, tk = qk(f, X, qkT[:, f, :])
                if half:
                    t_qk, tk = qk(f, XCk, qkT[:, f + 4, :])
            s.free = [tk]
        t_q = [V.last(), A.last()]

        s = load((8, 512), [(lambda v: v, w_in[:, :, 1280:1792])])
        for c in range(4):
            src = (XC if c < 2 else XT)
            b = token(lambda k: src[:, k, (c % 2) * 128:(c % 2 + 1) * 128], lambda k: s.v[:, k, :], 512, [s.ready])
            t_v = V(ve.tensor_tensor, vaug[:, c, :, 0:128], b.t[:, :].rearrange("p (h d) -> p h d", h=4),
                    rowb.t[:, 256:768].rearrange("p (h d) -> p h d", h=4), ALU.add, w=(b.tk, tz2, rowb.ready))
            b.free = [t_v]
        s.free = [b.tk]

        s = load((8, 512), [(lambda v: v, w_in[:, :, 1792:2304])])
        for f in range(4):
            b = feature(lambda k: s.v[:, k, f * 128:(f + 1) * 128], X, [s.ready])
            t_so = A(ae.activation, soT[:, f, :], b.t[:, 0:256], ACT.Sigmoid, bias=colA[:, 72 + f:73 + f], scale=1.0,
                     w=(b.tk,))
            b.free = [t_so]
        s.free = [b.tk]

        s = load((8, 16 + 496), [(lambda v: v, w_in[:, :, 2304:2816])])
        s2 = load((8, 16), [(lambda v: v, w_in[:, :, 2816:2832])])
        wg = AR[:, 15380:16404].rearrange("p (k i m) -> p k i m", k=8, i=2)
        tg = G(ge.memset, wg[:, :, :, :], 0.0)
        for kind in range(4):
            p0 = 32 * (kind // 2)
            tg = G(ge.tensor_copy, wg[:, :, kind % 2, p0:p0 + 4], s.v[:, :, 4 * kind:4 * kind + 4],
                   w=(tg, s.ready))
        rI = arena(512, p=64, reset=4096)
        rF = arena(512, p=64)
        bc = arena(512, p=64, reset=5120)
        uR = arena(512, p=64)
        MR = arena(512, p=64)
        assert ar["at"] <= 17020
        for i, dst in ((0, rI), (1, rF)):
            b = bank()
            for k in range(8):
                mm(b.t[0:64, 0:256], wg[:, k, i, :], XC[:, k, :], k == 0, k == 7, w=(b.w, tg))
            for k in range(8):
                t = mm(b.t[0:64, 256:512], wg[:, k, i, :], XT[:, k, :], k == 0, k == 7, inc=(k == 7))
            t_if = A(ae.activation, dst, b.t[0:64, :], ACT.Identity, bias=gb[:, i:i + 1], scale=1.0, w=(t, t_gl))
            b.free = [t_if]
        for f in range(2):
            b = feature(lambda k: s.v[:, k, 16 + f * 128:144 + f * 128], X, [s.ready])
            t_u = A(ae.activation, uT[:, f, :], b.t[:, 0:256], ACT.Gelu, bias=colA[:, 76 + f:77 + f], scale=1.0,
                    w=(b.tk,))
            b.free = [t_u]
        for tt in range(2):
            b = bank()
            for k in range(8):
                mm(b.t[:, 0:240], XT[:, k, tt * 128:(tt + 1) * 128], s.v[:, k, 272:512], k == 0, k == 7,
                   w=(b.w, s.ready))
            for k in range(8):
                t = mm(b.t[:, 240:256], XT[:, k, tt * 128:(tt + 1) * 128], s2.v[:, k, :], k == 0, k == 7,
                       w=(s2.ready,), inc=(k == 7))
            tv = V(ve.tensor_tensor, vs[:, tt, :], b.t[:, 0:256], rowb.t[:, 768:1024], ALU.add, w=(t,))
            b.free = [tv]
            ta = A(ae.activation, vs[:, tt, :], vs[:, tt, :], ACT.Gelu, w=(tv,))
        s.free = [t, tg]
        s2.free = [t]

        ts = stats([vs[:, 0, :], vs[:, 1, :]], 1e-5, 0, w=(ta,))
        for tt in range(2):
            t = normal(vs[:, tt, :], vs[:, tt, :], tt, w=(ts,))
            t = V(ve.tensor_tensor, vs[:, tt, :], vs[:, tt, :], rowb.t[:, 1024:1280], ALU.mult, w=(t,))
            t_vs = V(ve.tensor_tensor, vs[:, tt, :], vs[:, tt, :], rowb.t[:, 1280:1536], ALU.add, w=(t,))
        wsT = AR[:, 16412:16924].rearrange("p (g t) -> p g t", g=4)
        b = bank()
        for g in range(4):
            t = tr(b.t[:, g * 128:(g + 1) * 128], sguw[:, g, :], w=(b.w, t_gl), inc=(g == 3))
        t_ws = V(ve.tensor_copy, wsT[:, :, :].rearrange("p g t -> p (g t)"), b.t[:, :], w=(t,))
        b.free = [t_ws]
        for g in range(4):
            b = bank()
            for n in range(2):
                t = mm(b.t[:, n * 128:(n + 1) * 128], vs[:, n, (g // 2) * 128:(g // 2 + 1) * 128], wsT[:, g, :],
                       True, True, w=(b.w, t_vs, t_ws), inc=(n == 1))
            q0 = (g % 2) * 64
            for n in range(2):
                tv = V(ve.tensor_tensor, sguT[q0:q0 + 64, g // 2, n * 128:(n + 1) * 128],
                       b.t[q0:q0 + 64, n * 128:(n + 1) * 128],
                       rowb.t[q0:q0 + 64, 1536 + g * 128:1536 + (g + 1) * 128], ALU.add, w=(t,))
            b.free = [tv]
            t_sgu = V(ve.tensor_tensor, sguT[q0:q0 + 64, g // 2, :], sguT[q0:q0 + 64, g // 2, :],
                      uT[q0:q0 + 64, g // 2, :], ALU.mult, w=(tv, t_u))
        rowb.free = [t_sgu]

        for g in range(4):
            b = bank()
            for n in range(2):
                t = mm(b.t[:, n * 128:(n + 1) * 128], ptok[:, n, (g // 2) * 128:(g // 2 + 1) * 128],
                       C("pool")[:, g * 128:(g + 1) * 128], True, True, w=(b.w, t_p), inc=(n == 1))
            q0 = (g % 2) * 64
            t_d = V(ve.tensor_copy, dT[q0:q0 + 64, g // 2, :], b.t[q0:q0 + 64, 0:256], w=(t,))
            b.free = [t_d]
        for j in range(2):
            b = bank()
            t = mm(b.t[:, 0:256], poolw[:, j, :], dT[:, j, :], True, True, w=(b.w, t_d, t_gl), inc=True)
            t_pool = V(ve.tensor_scalar, poolT[:, j, :], b.t[:, 0:256], colA[:, 102 + j:103 + j], None, ALU.mult,
                       w=(t,))
            b.free = [t_pool]

        tmpR = arena(512, p=64)
        assert ar["at"] == 7168
        te = V(ve.scalar_tensor_tensor, tmpR, rF, -1.0, rF, ALU.mult, ALU.max, w=(t_if,))
        te = A(ae.activation, tmpR, tmpR, ACT.Exp, scale=-1.0, w=(te,))
        te = A(ae.activation, tmpR, tmpR, ACT.Ln, bias=1.0, w=(te,))
        te = V(ve.scalar_tensor_tensor, rF, rF, 0.0, tmpR, ALU.min, ALU.subtract, w=(te,))
        tzr = V(ve.memset, tmpR, 0.0, w=(te,))
        tzb = V(ve.memset, bc, 0.0, w=(te,))
        tzm = V(ve.memset, MR, 0.0, w=(te,))
        mst = sb("mst", [64, 8])
        mls = sb("mls", [64, 8])
        tzs = V(ve.memset, mst[:, :], 0.0)
        tzl = V(ve.memset, mls[:, :], 0.0)
        ORD = ((0, 1, 2, 3), (1, 0, 3, 2))
        for d in range(2):
            p0 = 32 * d
            for c in range(4):
                a, e = c * 128, (c + 1) * 128
                cut = slice(a, e) if d == 0 else slice(e - 1, a - 1 if a else None, -1)
                t = V(ve.tensor_tensor_scan, bc[p0:p0 + 4, cut], rF[p0:p0 + 4, cut], tmpR[p0:p0 + 4, cut],
                      0.0, ALU.add, ALU.add, w=(te, tzr, tzb))
        t = V(ve.tensor_tensor, uR, rI, bc, ALU.subtract, w=(t,))
        for st in range(4):
            for d in range(2):
                p0 = 32 * d
                c = ORD[d][st]
                a, e = c * 128, (c + 1) * 128
                cut = slice(a, e) if d == 0 else slice(e - 1, a - 1 if a else None, -1)
                end = e - 1 if d == 0 else a
                tm = V(ve.tensor_tensor_scan, MR[p0:p0 + 4, cut], uR[p0:p0 + 4, cut], uR[p0:p0 + 4, cut],
                       mst[p0:p0 + 4, st:st + 1], ALU.max, ALU.max, w=(t, tzs, tzm, tzl))
                tm2 = V(ve.tensor_tensor, mst[p0:p0 + 4, st + 1:st + 2], MR[p0:p0 + 4, end:end + 1],
                        bc[p0:p0 + 4, end:end + 1], ALU.add, w=(tm,))
                tm3 = V(ve.tensor_scalar, mls[p0:p0 + 4, st:st + 1], MR[p0:p0 + 4, end:end + 1], -1.0, None,
                        ALU.mult, w=(tm,))
            t = tm2
        t = V(ve.tensor_tensor, mls[:, 4:8], mst[:, 0:4], mls[:, 0:4], ALU.add, w=(tm2, tm3))
        t_a = A(ae.activation, mls[:, 4:8], mls[:, 4:8], ACT.Exp, w=(t,))
        t = V(ve.tensor_tensor, bc, bc, MR, ALU.add, w=(tm2,))
        t_em = A(ae.activation, bc, bc, ACT.Exp, scale=-1.0, w=(t,))
        for d in range(2):
            p0 = 32 * d
            for st in range(4):
                c = ORD[d][st]
                a, e = c * 128, (c + 1) * 128
                t_wk = A(ae.activation, rI[p0:p0 + 32, a:e], uR[p0:p0 + 32, a:e], ACT.Exp,
                         bias=mls[p0:p0 + 32, st:st + 1], scale=1.0, w=(tm3,))
                t_dc = A(ae.activation, rF[p0:p0 + 32, a:e], MR[p0:p0 + 32, a:e], ACT.Exp,
                         bias=mst[p0:p0 + 32, st:st + 1], scale=-1.0, w=(tm2, te))
        t_nm = V(ve.tensor_scalar, MR, MR, -1.0, None, ALU.mult, w=(t_dc, t_em))
        cols = AR[:, 0:768].rearrange("p (a b) -> p a b", a=12)
        lst = [(uR, c) for c in range(4)] + [(rI, c) for c in range(4)] + [(rF, 2), (rF, 3), (bc, 2), (bc, 3)]
        for h in range(2):
            b = bank()
            for i in range(6):
                r, c = lst[h * 6 + i]
                t = tr(b.t[:, i * 64:(i + 1) * 64], r[:, c * 128:(c + 1) * 128], w=(b.w, t_wk, t_dc, t_em),
                       inc=(i == 5), k=64)
            t_cols = V(ve.tensor_copy, cols[:, h * 6:h * 6 + 6, :].rearrange("p a b -> p (a b)"), b.t[:, 0:384],
                       w=(t, t_d, t_sgu))
            b.free = [t_cols]
        aB = sb("aB", [128, 8, 4])
        b = bank()
        sel = C("sel", 64).rearrange("p (r m) -> p r m", r=8)
        for r in range(8):
            t = mm(b.t[:, r * 4:r * 4 + 4], sel[:, r, :], mls[:, 4:8], True, True, w=(b.w, t_a), inc=(r == 7))
        t_aB = V(ve.tensor_copy, aB[:, :, :].rearrange("p a b -> p (a b)"), b.t[:, 0:32], w=(t,))
        b.free = [t_aB]
        for c in range(4):
            b = bank()
            for h in range(4):
                src = qkT[:, (8 if c < 2 else 4) + h, (c % 2) * 128:(c % 2 + 1) * 128]
                t = tr(b.t[:, h * 128:(h + 1) * 128], src, w=(b.w, t_q), inc=(h == 3))
            t_kN = V(ve.tensor_copy, kN[:, c, :, :].rearrange("p a b -> p (a b)"), b.t[:, :], w=(t,))
            b.free = [t_kN]

        barrier()
        CT = arena(8, 129, reset=15380)
        Et = [arena(128, reset=7168), arena(128)]
        SC = [arena(128), arena(128)]
        vw = [arena(129) for _ in range(2)]
        nd = [arena(129) for _ in range(2)]
        assert ar["at"] <= 8196
        tmpI = [arena(129, reset=3584), arena(129)]
        hsum = arena(2, 4, 128, reset=4096)
        dn = sb("dn", [128, 32])
        vw_free = [None, None]
        ct_tok = [None] * 8
        ct_use = [None] * 8
        et_free = [None, None]
        sc_free = [None, None]
        nd_tok = [None, None]
        ti_free = [None, None]
        cnt = {"u": 0, "o": 0}
        hs_tok = {}

        def col(kind, r):
            j = 32 * (r // 4) + r % 4
            return cols[:, kind, j:j + 1]

        def update(r, st):
            d, h = r // 4, r % 4
            c = ORD[d][st]
            i = cnt["u"] % 2
            cnt["u"] += 1
            tw = A(ae.activation, vw[i], vaug[:, c, h, :], ACT.Copy, scale=col(4 + c, r), w=(vw_free[i], t_v, t_cols))
            b = bank()
            t = mm(b.t[:, 0:129], kN[:, c, h, :], vw[i], True, True, w=(b.w, tw, t_kN), inc=True)
            vw_free[i] = t
            if st == 0:
                tv = V(ve.tensor_copy, CT[:, r, :], b.t[:, 0:129], w=(t,))
            else:
                tv = V(ve.scalar_tensor_tensor, CT[:, r, :], CT[:, r, :], aB[:, r, st:st + 1], b.t[:, 0:129],
                       ALU.mult, ALU.add, w=(t, ct_tok[r], ct_use[r], t_aB))
            b.free = [tv]
            ct_tok[r] = tv

        def output(r, st):
            d, h = r // 4, r % 4
            c = ORD[d][st]
            n = c - 2
            i = cnt["o"] % 2
            j = cnt["o"]
            cnt["o"] += 1
            tc = slice(n * 128, (n + 1) * 128)
            bD = bank()
            mm(bD.t[:, 0:128], sel[:, r, :], MR[:, c * 128:(c + 1) * 128], True, False, w=(bD.w, t_nm))
            t = mm(bD.t[:, 0:128], C("ident"), C("maskf" if d == 0 else "maskb"), False, True, inc=True)
            tE = A(ae.activation, Et[i], bD.t[:, 0:128], ACT.Exp, bias=col(c, r), scale=1.0, w=(t, et_free[i]))
            bD.free = [tE]
            bS = bank()
            t = mm(bS.t[:, 0:128], qkT[:, 4 + h, tc], qkT[:, h, tc], True, True, w=(bS.w, t_q), inc=True)
            tS = V(ve.tensor_tensor, SC[i], bS.t[:, 0:128], Et[i], ALU.mult, w=(t, tE, sc_free[i]))
            bS.free = [tS]
            et_free[i] = tS
            bI = bank()
            t = mm(bI.t[:, 0:129], qkT[:, h, tc], CT[:, r, :], True, True, w=(bI.w, ct_tok[r]), inc=True)
            ct_use[r] = t
            tI = A(ae.activation, tmpI[i], bI.t[:, 0:129], ACT.Copy, scale=col(8 + n, r), w=(t, ti_free[i]))
            bI.free = [tI]
            bN = bank()
            t = mm(bN.t[:, 0:129], SC[i], vaug[:, c, h, :], True, True, w=(bN.w, tS), inc=True)
            sc_free[i] = t
            t = V(ve.tensor_tensor, nd[i], bN.t[:, 0:129], tmpI[i], ALU.add, w=(t, tI, nd_tok[i]))
            bN.free = [t]
            ti_free[i] = t
            den = nd[i][:, 128:129]
            t = V(ve.scalar_tensor_tensor, dn[:, j:j + 1], den, -1.0, den, ALU.mult, ALU.max, w=(t,))
            t = V(ve.tensor_tensor, dn[:, j:j + 1], dn[:, j:j + 1], col(10 + n, r), ALU.max, w=(t,))
            t = V(ve.reciprocal, dn[:, j:j + 1], dn[:, j:j + 1], w=(t,))
            if (h, n) not in hs_tok:
                t = V(ve.tensor_scalar, hsum[:, n, h, :], nd[i][:, 0:128], dn[:, j:j + 1], None, ALU.mult, w=(t,))
            else:
                t = V(ve.scalar_tensor_tensor, hsum[:, n, h, :], nd[i][:, 0:128], dn[:, j:j + 1], hsum[:, n, h, :],
                      ALU.mult, ALU.add, w=(t, hs_tok[(h, n)]))
            hs_tok[(h, n)] = t
            nd_tok[i] = t

        for st in range(4):
            for r in range(8):
                if st >= 2:
                    output(r, st)
                if st < 3:
                    update(r, st)
        t_hs = V.last()
        mlT = arena(4, 256, reset=0)
        ts = stats([hsum[:, n, h, :] for n in range(2) for h in range(4)], 1e-6, 0, w=(t_hs,))
        for n in range(2):
            for h in range(4):
                t = normal(hsum[:, n, h, :], hsum[:, n, h, :], n * 4 + h, w=(ts,))
        barrier()
        for h in range(4):
            b = bank()
            for n in range(2):
                tk = tr(b.t[:, n * 128:(n + 1) * 128], hsum[:, n, h, :], w=(b.w, t), inc=(n == 1))
            t_ml = V(ve.scalar_tensor_tensor, mlT[:, h, :], b.t[:, 0:256], colB[:, 8 + h:9 + h], soT[:, h, :],
                     ALU.mult, ALU.mult, w=(tk, t_so, t_cB))
            b.free = [t_ml]
        barrier()

        sig = arena(24, 256, reset=8196)
        yT = arena(8, 256)
        for q in range(6):
            s = load((8, 512), [(lambda v: v, w_in[:, :, 2832 + q * 512:2832 + (q + 1) * 512])])
            for f in range(4):
                j = q * 4 + f
                b = feature(lambda k: s.v[:, k, f * 128:(f + 1) * 128], X, [s.ready])
                ts = A(ae.activation, sig[:, j, :], b.t[:, 0:256], ACT.Sigmoid, bias=colA[:, 78 + j:79 + j],
                       scale=1.0, w=(b.tk,))
                b.free = [ts]
            s.free = [b.tk]
        wb = [T[n][0].rearrange("(k p) n -> p k n", p=128) for n in ("w_br_pool", "w_br_mlstm", "w_br_sgu")]
        yt = [arena(256, reset=5120), arena(256)]
        ty = [None, None]
        for half in range(2):
            cs = slice(half * 512, (half + 1) * 512)
            s = load((8, 512), [(lambda v: v[:, 0:2, :], wb[0][:, :, cs]), (lambda v: v[:, 2:6, :], wb[1][:, :, cs]),
                                (lambda v: v[:, 6:8, :], wb[2][:, :, cs])])
            for f in range(4):
                j = half * 4 + f
                tprev = None
                for br, (k0, kn, src) in enumerate(((0, 2, poolT), (2, 4, mlT), (6, 2, sguT))):
                    b = feature(lambda k: s.v[:, k0 + k, f * 128:(f + 1) * 128], lambda k: src[:, k, :],
                                [s.ready, t_ml, t_pool, t_sgu], kk=kn)
                    if br == 0:
                        tprev = V(ve.tensor_tensor, yT[:, j, :], b.t[:, 0:256], sig[:, j, :], ALU.mult, w=(b.tk, ts))
                        b.free = [tprev]
                    else:
                        i = br - 1
                        t = V(ve.tensor_tensor, yt[i], b.t[:, 0:256], sig[:, 8 * br + j, :], ALU.mult,
                              w=(b.tk, ts, ty[i]))
                        b.free = [t]
                        tprev = G(ge.tensor_tensor, yT[:, j, :], yT[:, j, :], yt[i], ALU.add, w=(t, tprev))
                        ty[i] = tprev
            s.free = [b.tk]
        t_y = tprev
        w_out = T["w_out"][0].rearrange("(k p) n -> p k n", p=128)

        xtmp = arena(2, 1024, reset=0)
        rtmp = arena(2, 1024)

        def residual(alpha, banks4, gate, w):
            for tt, h, b in banks4:
                cs = slice(h * 512, (h + 1) * 512)
                if gate is None:
                    t = V(ve.scalar_tensor_tensor, xtok[:, tt, cs], xtok[:, tt, cs], alpha, b.t[:, :], ALU.mult,
                          ALU.add, w=(b.tk, w))
                    b.free = [t]
                else:
                    t = V(ve.tensor_tensor, rtmp[:, tt, cs], b.t[:, :], gate[:, cs], ALU.mult, w=(b.tk, w))
                    b.free = [t]
                    t = V(ve.scalar_tensor_tensor, xtok[:, tt, cs], xtok[:, tt, cs], alpha, rtmp[:, tt, cs],
                          ALU.mult, ALU.add, w=(t,))
            return t

        def ln_affine(g, bvec, w):
            r = load_rows([row(g), row(bvec)])
            ts = stats([xtok[:, 0, :], xtok[:, 1, :]], 1e-5, 0, w=(w,))
            out_ = []
            for tt in range(2):
                t = normal(xtok[:, tt, :], xtok[:, tt, :], tt, w=(ts,))
                t = V(ve.tensor_tensor, xtok[:, tt, :], xtok[:, tt, :], r.t[:, 0:1024], ALU.mult, w=(t, r.ready))
                t = G(ge.tensor_tensor, xtok[:, tt, :], xtok[:, tt, :], r.t[:, 1024:2048], ALU.add, w=(t, r.ready))
                out_.append(t)
            r.free = list(out_)
            return out_

        def dense(xT, wsrc, w, kk=8):
            got = []
            for h in range(2):
                s = load((8, 512), [(lambda v: v, wsrc[:, :, h * 512:(h + 1) * 512])])
                for tt in range(2):
                    b = token(lambda k: xT[:, k, tt * 128:(tt + 1) * 128], lambda k: s.v[:, k, :], 512,
                              [s.ready, w])
                    got.append((tt, h, b))
                s.free = [b.tk]
            return got

        bs = dense(yT, w_out, t_y)
        t = residual(ALPHA1, bs, gB[:, 0, :], t_gB)
        tl = ln_affine(T["ln1_g"][0], T["ln1_b"][0], t)
        ts = stats([xtok[:, 0, :], xtok[:, 1, :]], 1e-5, 4, w=(tl,))
        for tt in range(2):
            t = normal(xtmp[:, tt, :], xtok[:, tt, :], 4 + tt, w=(ts,))
        t_h = turn(XT, xtmp, [t], modT[:, 4, :, 0], modT[:, 3, :, 0])
        for tt in range(2):
            for c in range(2):
                b = bank()
                for q in range(4):
                    tk = tr(b.t[:, q * 128:(q + 1) * 128], XT[:, 4 * c + q, tt * 128:(tt + 1) * 128],
                            w=(b.w, t_h), inc=(q == 3))
                tn_h = V(ve.tensor_copy, xtmp[:, tt, c * 512:(c + 1) * 512], b.t[:, :], w=(tk,))
                b.free = [tn_h]

        t_wr = small([(wrt[:, :, :], T["w_router"][0].rearrange("(k p) n -> p k n", p=128))])
        rowr = load_rows([row(T["b_router"][0])])
        barrier()
        t_mk = []
        cw = arena(2, 32, reset=2048)
        cwT = arena(256, p=32)
        lg = arena(2, 32)
        lg2 = arena(2, 32)
        top = arena(2, 8)
        eq = arena(2, 32)
        cs = arena(2, 32)
        zr = arena(2, 32)
        tzz = V(ve.memset, zr, 0.0)
        sm = arena(2, 4)
        bdn = arena(1024, p=32)
        t_bd = small([(bdn, T["b_down"][0])], q=G)
        acc = arena(2, 1024)
        number = sb("number", [1, 32], I32)
        rg = rows[state["row"] % 2]
        state["row"] += 1
        load_into(rg, [(rg.t[0:32, :], T["b_gate_up"][0])])
        bguR, t_bguR = rg.t[0:32, :], rg.ready
        for tt in range(2):
            b = token(lambda k: XT[:, k, tt * 128:(tt + 1) * 128], lambda k: wrt[:, k, :], 32, [t_wr, t_h])
            t = V(ve.tensor_tensor, lg[:, tt, :], b.t[:, 0:32], rowr.t[:, 0:32], ALU.add, w=(b.tk, rowr.ready))
            b.free = [t]
            rowr.free = [t]
            t0 = V(ve.max, top[:, tt, :], lg[:, tt, :], w=(t,))
            v4 = top[:, tt, 3:4]
            tg = V(ve.tensor_scalar, lg2[:, tt, :], lg[:, tt, :], v4, None, ALU.is_gt, w=(t0,))
            tn = V(ve.tensor_reduce, sm[:, tt, 3:4], lg2[:, tt, :], AX.X, ALU.add, w=(tg,))
            tq = V(ve.tensor_scalar, eq[:, tt, :], lg[:, tt, :], v4, None, ALU.is_equal, w=(t0,))
            tc_ = V(ve.tensor_tensor_scan, cs[:, tt, :], eq[:, tt, :], zr[:, tt, :], 0.0, ALU.add, ALU.add,
                    w=(tq, tzz))
            tc_ = V(ve.tensor_scalar, cs[:, tt, :], cs[:, tt, :], sm[:, tt, 3:4], 4.5, ALU.add, ALU.is_lt,
                    w=(tc_, tn))
            tc_ = V(ve.tensor_tensor, eq[:, tt, :], eq[:, tt, :], cs[:, tt, :], ALU.mult, w=(tc_,))
            te2 = V(ve.tensor_tensor, lg2[:, tt, :], lg2[:, tt, :], eq[:, tt, :], ALU.add, w=(tc_,))
            t = V(ve.tensor_scalar, sm[:, tt, 0:1], top[:, tt, 0:1], -1.0, None, ALU.mult, w=(t0,))
            te = A(ae.activation, lg[:, tt, :], lg[:, tt, :], ACT.Exp, bias=sm[:, tt, 0:1], scale=1.0, w=(t, te2))
            t_mk.append(te2)
            t = V(ve.tensor_tensor, cw[:, tt, :], lg[:, tt, :], lg2[:, tt, :], ALU.mult, w=(te, te2))
            t = V(ve.tensor_reduce, sm[:, tt, 1:2], cw[:, tt, :], AX.X, ALU.add, w=(t,))
            t = V(ve.reciprocal, sm[:, tt, 2:3], sm[:, tt, 1:2], w=(t,))
            t_cw = V(ve.tensor_scalar, cw[:, tt, :], cw[:, tt, :], sm[:, tt, 2:3], None, ALU.mult, w=(t,))
        b = bank()
        for tt in range(2):
            tk = tr(b.t[0:32, tt * 128:(tt + 1) * 128], cw[:, tt, :], w=(b.w, t_cw), inc=(tt == 1))
        t_cwT = V(ve.tensor_copy, cwT, b.t[0:32, 0:256], w=(tk,))
        b.free = [t_cwT]
        for tt in range(2):
            for h in range(2):
                b = bank()
                tk = mm(b.t[:, :], cwT[:, tt * 128:(tt + 1) * 128], bdn[:, h * 512:(h + 1) * 512], True, True,
                        w=(b.w, t_cwT, t_bd), inc=True)
                t_acc = V(ve.tensor_copy, acc[:, tt, h * 512:(h + 1) * 512], b.t[:, :], w=(tk,))
                b.free = [t_acc]

        b = bank()
        mm(b.t[:, 0:32], C("tri"), lg2[:, 0, :], True, True, w=(b.w, t_mk))
        mm(b.t[:, 32:64], C("ones"), lg2[:, 0, :], True, False)
        mm(b.t[:, 32:64], C("tri"), lg2[:, 1, :], False, True)
        mm(b.t[0:1, 64:96], C("ones")[:, 0:1], lg2[:, 0, :], True, False)
        tk = mm(b.t[0:1, 64:96], C("ones")[:, 0:1], lg2[:, 1, :], False, True, inc=True)
        pos = eq
        for tt in range(2):
            t = V(ve.scalar_tensor_tensor, pos[:, tt, :], b.t[:, 32 * tt:32 * tt + 32], 1.0, lg2[:, tt, :],
                  ALU.add, ALU.mult, w=(tk,))
            t_pos_ = V(ve.tensor_scalar, pos[:, tt, :], pos[:, tt, :], -1.0, None, ALU.add, w=(t,))
        tx = [V(ve.tensor_scalar, cs[0:1, 0, :], b.t[0:1, 64:96], 64.5, None, ALU.is_gt, w=(tk,))]
        for m in (2, 3):
            t = V(ve.tensor_scalar, cs[0:1, 1, :], b.t[0:1, 64:96], 64.0 * m + 0.5, None, ALU.is_gt,
                  w=(tk, tx[-1]))
            tx.append(V(ve.tensor_tensor, cs[0:1, 0, :], cs[0:1, 0, :], cs[0:1, 1, :], ALU.add, w=(t, tx[0])))
        b.free = [tx[-1], t_pos_]
        t_num = V(ve.tensor_copy, number[:, :], cs[0:1, 0, :], w=(tx[-1],))

        hid_at = ar["at"]
        hg = arena(512)
        hgT = [arena(4, 2, 64) for _ in range(2)]
        gt, up, sg = arena(512), arena(512), arena(512)
        hidT = [arena(4, 2, 64) for _ in range(2)]
        selg = arena(2, 64)
        selw = arena(2, 128)
        selT = [arena(2, 128) for _ in range(3)]
        yy = arena(512)
        xt = XT[:, :, :].rearrange("p a b -> p (a b)")
        fhg, fhgT = xt[:, 0:512], xt[:, 512:1024].rearrange("p (a b c) -> p a b c", a=4, b=2)
        fgt, fup = xt[:, 1024:1536], xt[:, 1536:2048]
        fhid = [arena(4, 2, 64) for _ in range(3)]
        fselg = selg2 = arena(2, 64)
        fselw = arena(2, 128)
        fselT = [arena(2, 128) for _ in range(3)]
        iota = C("iota").rearrange("p (m a b) -> p m a b", m=4, a=2)

        acc_tok = {(tt, h): [t_acc] for tt in range(2) for h in range(2)}

        def select(Vq, e, m, g, wt, w):
            for tt in range(2):
                p_ = pos[:, tt, e:e + 1]
                t1 = Vq(ve.tensor_scalar, g[:, tt, :], iota[:, m, 0, :], p_, None, ALU.is_equal, w=(t_pos_, w))
                t2 = Vq(ve.tensor_scalar, wt[:, tt, :], iota[:, m, :, :].rearrange("p a b -> p (a b)"), p_,
                        cw[:, tt, e:e + 1], ALU.is_equal, ALU.mult, w=(t_pos_, t_cw, w))
            return t1, t2

        def turn_selection(P, Vq, b, wt, dst, w):
            for tt in range(2):
                tk = P(pe.transpose, b.t[:, tt * 128:(tt + 1) * 128], wt[:, tt, :], C("ident"), w=(b.w, w),
                       inc=(tt == 1))
            return tk, Vq(ve.tensor_copy, dst.rearrange("p a b -> p (a b)"), b.t[:, 0:256], w=(tk,))

        def gather(P, b, g, w):
            for tt in range(2):
                for h in range(2):
                    tk = P(pe.matmul, b.t[64 * h:64 * h + 64, :], g[:, tt, :], xtmp[:, tt, h * 512:(h + 1) * 512],
                           start=(tt == 0), stop=(tt == 1), skip_group_check=True, w=(b.w, w),
                           inc=(tt == 1 and h == 1))
            return tk

        def four(P, b, src, w):
            for q in range(4):
                tk = P(pe.transpose, b.t[:, q * 128:(q + 1) * 128], src[:, q * 128:(q + 1) * 128], C("ident"),
                       w=(b.w, w), inc=(q == 3))
            return tk

        def gate_up(P, bG, bU, e, xT, ws, w):
            for c in range(4):
                b_ = (bG, bU)[c // 2]
                o = 64 * (c % 2)
                P(pe.matmul, b_.t[o:o + 64, :], C("ident", 32)[:, e:e + 1].broadcast_to((32, 64)),
                  bguR[:, c * 512:(c + 1) * 512], start=True, stop=False, skip_group_check=True,
                  w=(b_.w, w, t_bguR), inc=False)
            toks = []
            for k in range(8):
                s = ws[k // 2]
                for c in range(4):
                    b_ = (bG, bU)[c // 2]
                    o = 64 * (c % 2)
                    tk = P(pe.matmul, b_.t[o:o + 64, :], xT[:, k % 4, k // 4, :], s.v[:, k % 2, c * 512:(c + 1) * 512],
                           start=False, stop=(k == 7), skip_group_check=True, w=(s.ready,),
                           inc=(k % 2 == 1 and c == 3))
                if k % 2:
                    toks.append(tk)
            return toks

        def activate(Vq, Aq, bG, bU, g, u, s_, tk, w):
            t = Vq(ve.tensor_scalar, g, bG.t[:, :], 7.0, None, ALU.min, w=(tk, w))
            tG = t
            ta = Aq(ae.activation, s_, g, ACT.Sigmoid, scale=1.702, w=(t, w))
            tU = Vq(ve.tensor_scalar, u, bU.t[:, :], 7.0, -7.0, ALU.min, ALU.max, w=(tk, w))
            t = Vq(ve.scalar_tensor_tensor, u, u, 1.0, g, ALU.add, ALU.mult, w=(tU,))
            return tG, tU, Vq(ve.tensor_tensor, u, u, s_, ALU.mult, w=(t, ta))

        def down(P, b, hT, ws, w):
            toks = []
            for k in range(8):
                s = ws[k // 4]
                for c in range(2):
                    tk = P(pe.matmul, b.t[64 * c:64 * c + 64, :], hT[:, k % 4, k // 4, :],
                           s.v[:, k % 4, c * 512:(c + 1) * 512], start=(k == 0), stop=(k == 7),
                           skip_group_check=True, w=(b.w, s.ready, w), inc=(k % 4 == 3 and c == 1))
                if k % 4 == 3:
                    toks.append(tk)
            return toks

        def spread(P, b, tt, h, sT, y, w):
            return P(pe.matmul, b.t[:, :], sT[64 * h:64 * h + 64, tt, :], y[64 * h:64 * h + 64, :], start=True,
                     stop=True, w=(b.w, w), inc=True)

        def add(Vq, b, tt, h, w):
            a = acc[:, tt, h * 512:(h + 1) * 512]
            return Vq(ve.tensor_tensor, a, a, b.t[:, :], ALU.add, w=(w, acc_tok[(tt, h)]))

        fq = {}

        def side(e):
            if e % 8 == 0 and e not in fq:
                fq[e] = tuple(Queue([sem(f"s_f{n}{e}")]) for n in "pva")
            return fq[e - e % 8]

        def extra(e, body):
            qs = side(e)
            tiles = ([], [], [])
            for m in (1, 2, 3):
                for q in qs:
                    q.items = []
                body(m, *qs)
                done = [q.last() for q in qs if q.count]
                for q, tl_ in zip(qs, tiles):
                    q.items.append((done, None, (), {}, None, 0))
                    tl_.append(q.items)
            for main, tl_ in zip((PE, V, A), tiles):
                main.items.append(((t_num,), None, (), {}, None, 0))
                main.items.append(Branch(number[0:1, e:e + 1], tl_))
            return qs[0].last()

        def prepare(e):
            i = e % 2
            t1, t2 = select(V, e, 0, selg, selw, E.get("sel_free"))
            b = bank()
            E["sel_pe"], t = turn_selection(PE, V, b, selw, selT[e % 3], [t2, E.get(("sc", e - 3))])
            b.free = [t]
            E[("selT", e)] = t
            b = bank()
            tk = gather(PE, b, selg, [t1, t_hx])
            E["sel_free"] = [tk]
            t = V(ve.tensor_copy, hg, b.t[:, :], w=(tk, E.get("hg_free")))
            b.free = [t]
            E[("hg", e)] = t

        def turn_gathered(e):
            b = bank()
            tk = four(PE, b, hg, [E[("hg", e)]])
            E["hg_free"] = tk
            t = A(ae.activation, hgT[e % 2].rearrange("p a b c -> p (a b c)"), b.t[:, :], ACT.Copy,
                  w=(tk, E.get(("gu", e - 2))))
            b.free = [t]
            E[("hgT", e)] = t

        def load_gu(e):
            wgu = T["w_gate_up"][0, e].rearrange("(k p) n -> p k n", p=128)
            return [load((2, 2048), [(lambda v: v, wgu[:, 2 * q:2 * q + 2, :])]) for q in range(4)]

        def load_d(e):
            wdn = T["w_down"][0, e].rearrange("(k p) n -> p k n", p=128)
            return [load((4, 1024), [(lambda v: v, wdn[:, 4 * q:4 * q + 4, :])]) for q in range(2)]

        E = {}
        t_hx = tn_h
        prepare(0)
        turn_gathered(0)
        for e in range(33):
            if e + 1 < 32:
                prepare(e + 1)
            if e < 32:
                ws = load_gu(e)
                bG, bU = bank(), bank()
                toks = gate_up(PE, bG, bU, e, hgT[e % 2], ws, [E[("hgT", e)]])
                E[("gu", e)] = toks[-1]
                tG, tU, t_act = activate(V, A, bG, bU, gt, up, sg, [toks[-1]], E.get("act_free"))
                bG.free, bU.free = [tG], [tU]

                b1, b2 = bank(), bank()

                def first(m, P, Vq, Aq):
                    Z = lambda q: [q.last()] if q.count else []
                    t1, t2 = select(Vq, e, m, fselg, fselw, [])
                    w0 = [b1.w, b2.w]
                    tk, t = turn_selection(P, Vq, b1, fselw, fselT[m - 1], [t2])
                    tk = gather(P, b2, fselg, [t1, t_hx])
                    t = Vq(ve.tensor_copy, fhg, b2.t[:, :], w=(tk,))
                    tk = four(P, b1, fhg, [t])
                    t = Vq(ve.tensor_copy, fhgT.rearrange("p a b c -> p (a b c)"), b1.t[:, :], w=(tk,))
                    tk = gate_up(P, b1, b2, e, fhgT, ws, [t])[-1]
                    _, _, t = activate(Vq, Aq, b1, b2, fgt, fup, fhg, [tk], [])
                    tk = four(P, b1, fup, [t])
                    Vq(ve.tensor_copy, fhid[m - 1].rearrange("p a b c -> p (a b c)"), b1.t[:, :], w=(tk,))

                f1 = extra(e, first)
                b1.free, b2.free = [b1.w, f1], [b2.w, f1]
                for s, tk in zip(ws, toks):
                    s.free = [tk, f1]
            if e > 0:
                d = e - 1
                wd = load_d(d)
                b = bank()
                toks = down(PE, b, hidT[d % 2], wd, [E[("hidT", d)]])
                t_y = A(ae.activation, yy, b.t[:, :], ACT.Copy, w=(toks[-1], E.get("y_free")))
                b.free = [t_y]
            if e + 1 < 32:
                turn_gathered(e + 1)
            if e < 32:
                b = bank()
                tk = four(PE, b, up, [t_act])
                E["act_free"] = [tk]
                t = A(ae.activation, hidT[e % 2].rearrange("p a b c -> p (a b c)"), b.t[:, :], ACT.Copy, w=(tk,))
                b.free = [t]
                E[("hidT", e)] = t
            if e > 0:
                for tt in range(2):
                    for h in range(2):
                        b = bank()
                        tk = spread(PE, b, tt, h, selT[d % 3], yy, [t_y, E[("selT", d)]])
                        t = add(V, b, tt, h, [tk])
                        b.free = [t]
                        acc_tok[(tt, h)] = [t]
                E["y_free"] = tk
                E[("sc", d)] = tk
                b1, b2 = bank(), bank()

                def second(m, P, Vq, Aq):
                    tk = down(P, b1, fhid[m - 1], wd, [f_prev])[-1]
                    t = Vq(ve.tensor_copy, fhg, b1.t[:, :], w=(tk,))
                    for tt in range(2):
                        for h in range(2):
                            b_ = (b2, b1)[h]
                            tk = spread(P, b_, tt, h, fselT[m - 1], fhg, [t])
                            t = add(Vq, b_, tt, h, [tk])

                f2 = extra(d, second)
                b1.free, b2.free = [b1.w, f2], [b2.w, f2]
                for k in acc_tok:
                    acc_tok[k] = acc_tok[k] + [f2]
                for s, tk in zip(wd, toks):
                    s.free = [tk, f2]
            f_prev = f1
        rg.free = [PE.last(), f2]
        t_moe = [acc_tok[k] for k in acc_tok]
        for tt in range(2):
            t = V(ve.tensor_tensor, acc[:, tt, :], acc[:, tt, :], gB[:, 1, :], ALU.mult, w=(t_moe,))
            t = V(ve.scalar_tensor_tensor, xtok[:, tt, :], xtok[:, tt, :], ALPHA1, acc[:, tt, :], ALU.mult, ALU.add,
                  w=(t,))
        tl = ln_affine(T["ln2_g"][0], T["ln2_b"][0], t)
        barrier()
        memT = arena(8, 256, reset=0)
        RC = arena(256, p=96)
        RS = arena(256, p=96)
        base = ar["at"]
        mtok = arena(2, 1024)
        t_mem = small([(mtok[:, tt, :], T["mem_2"][0, tt * 128:(tt + 1) * 128, :]) for tt in range(2)],
                      w=(PE.last(), V.last(), A.last(), G.last()))
        posi = sb("posi", [96, 256], I32)
        t_pos = small([(posi[:, :], T["positions_2"].broadcast_to((96, 256)))])
        t_mT = turn(memT, mtok, [t_mem])
        an = arena(256, p=96)
        kk_ = arena(256, p=96)
        t = V(ve.tensor_copy, an, posi[:, :], w=(t_pos,))
        t = V(ve.tensor_scalar, an, an, C("freq", 96), None, ALU.mult, w=(t,))
        t = V(ve.tensor_scalar, kk_, an, 1.0 / (2 * np.pi), None, ALU.mult, w=(t,))
        t = V(ve.tensor_scalar, kk_, kk_, 12582912.0, None, ALU.add, w=(t,))
        t = V(ve.tensor_scalar, kk_, kk_, -12582912.0, None, ALU.add, w=(t,))
        rest = 2 * np.pi
        for bits in (5, 13, 21, None):
            part = float(np.float32(rest)) if bits is None else np.floor(rest * 2.0 ** bits) / 2.0 ** bits
            rest -= part
            t = V(ve.scalar_tensor_tensor, an, kk_, -part, an, ALU.mult, ALU.add, w=(t,))
        t = V(ve.tensor_scalar, RS, an, 3.1415925, -3.1415925, ALU.min, ALU.max, w=(t,))
        t_rs = A(ae.activation, RS, RS, ACT.Sin, w=(t,))
        t = V(ve.tensor_scalar, an, an, np.pi / 2, None, ALU.add, w=(t,))
        t = V(ve.tensor_scalar, kk_, an, 3.1415927, -2 * np.pi, ALU.is_gt, ALU.mult, w=(t,))
        t = V(ve.tensor_tensor, an, an, kk_, ALU.add, w=(t,))
        t = V(ve.tensor_scalar, RC, an, 3.1415925, -3.1415925, ALU.min, ALU.max, w=(t,))
        t_rc = A(ae.activation, RC, RC, ACT.Sin, w=(t,))
        krb = sb("krb", [96, 2])
        tkb = G(ge.memset, krb[:, :], 0.0)
        t_krb = small([(krb[64:96, l:l + 1], T["mix_b_in_2"][l][512:544].rearrange("(a o) -> a o", o=1))
                       for l in range(2)], w=(tkb,))
        rq = sb("rq", [128, 8])
        sums = sb("sums", [128, 2, 24])
        t_x = tl

        def softmax(b, n, width, dst, scale, w):
            t = V(ve.tensor_reduce, sums[:, 0, n:n + 1], b.t[:, 0:width], AX.X, ALU.max, w=(b.tk, w))
            t = V(ve.tensor_scalar, sums[:, 0, n:n + 1], sums[:, 0, n:n + 1], -scale, None, ALU.mult, w=(t,))
            t = A(ae.activation, dst, b.t[:, 0:width], ACT.Exp, bias=sums[:, 0, n:n + 1], scale=scale,
                  accum_out=sums[:, 1, n:n + 1], w=(t, w))
            b.free = [t]
            t2 = V(ve.reciprocal, sums[:, 1, n:n + 1], sums[:, 1, n:n + 1], w=(t,))
            return t, t2

        for l in range(2):
            cL = colL[l]
            w_mix = T["mix_w_in_2"][l].rearrange("(k p) n -> p k n", p=128)
            barrier()
            t_XT = turn(XT, xtok, [t_x])
            cq = arena(2, 2, 256, reset=base)
            cT = arena(2, 2, 256)
            qh = arena(8, 256, p=96)
            Kh = arena(8, 256, p=96)
            va = arena(2, 512)
            hp = arena(4, 286)
            yc = arena(4, 256)
            cat = arena(8, 256)
            otk = AR[:, base:base + 1024].rearrange("p (a b) -> p a b", a=2)
            krw = arena(8, 96)
            tq_ = [arena(2, 256, p=96) for _ in range(1)]
            pr = [arena(256) for _ in range(3)]
            pT = [arena(256) for _ in range(3)]
            sgc = arena(256)
            rowm = load_rows([row(T["mix_b_in_2"][l], 0, 512)])
            s = load((8, 512), [(lambda v: v, w_mix[:, :, 0:512])])
            tcq = []
            for tt in range(2):
                b = token(lambda k: XT[:, k, tt * 128:(tt + 1) * 128], lambda k: s.v[:, k, :], 512,
                          [s.ready] + t_XT)
                t = V(ve.tensor_tensor, cq[:, tt, :, :].rearrange("p a b -> p (a b)"), b.t[:, :], rowm.t[:, 0:512],
                      ALU.add, w=(b.tk, rowm.ready))
                b.free = [t]
                for a in range(2):
                    tcq.append(A(ae.activation, sgc, cq[:, tt, a, :], ACT.Square,
                                 accum_out=rq[:, tt * 2 + a:tt * 2 + a + 1], w=(t, tcq[-1] if tcq else None)))
            rowm.free = [t]
            s.free = [b.tk]
            t = V(ve.tensor_scalar, rq[:, 0:4], rq[:, 0:4], 1.0 / 256, 1e-6, ALU.mult, ALU.add, w=(tcq,))
            t = G(ge.tensor_tensor, rq[:, 0:4], rq[:, 0:4], C("nhalf")[:, 0:4], ALU.pow, w=(t,))
            for tt in range(2):
                for a in range(2):
                    t2 = V(ve.tensor_scalar, cq[:, tt, a, :], cq[:, tt, a, :], rq[:, tt * 2 + a:tt * 2 + a + 1],
                           None, ALU.mult, w=(t,))
            t_cT = []
            for a in range(2):
                t_cT += turn(cT[:, a], cq[:, :, a, :], [t2], cL[:, 132 + 2 * a:134 + 2 * a], None, chunks=2)
            tkz = G(ge.memset, krw, 0.0)
            t_kr = small([(krw[:, :, 64:96], w_mix[:, :, 512:544])], w=(tkz,))
            b = feature(lambda k: krw[:, k, :], X, [t_kr])
            krr = tq_[0]
            t = A(ae.activation, krr[:, 0, :], b.t[0:96, 0:256], ACT.Identity, bias=krb[:, l:l + 1], scale=1.0,
                  w=(b.tk, t_krb))
            b.free = [t]
            b = bank()
            tk = mm(b.t[0:96, 0:256], C("rot", 96), krr[:, 0, :], True, True, w=(b.w, t), inc=True)
            t2 = V(ve.tensor_tensor, krr[:, 1, :], b.t[0:96, 0:256], RS, ALU.mult, w=(tk, t_rs))
            b.free = [t2]
            t3 = V(ve.tensor_tensor, krr[:, 0, :], krr[:, 0, :], RC, ALU.mult, w=(tk, t_rc))
            t3 = V(ve.tensor_tensor, krr[:, 0, :], krr[:, 0, :], krr[:, 1, :], ALU.add, w=(t3, t2))
            for h in range(8):
                t_kh = G(ge.tensor_copy, Kh[64:96, h, :], krr[64:96, 0, :], w=(t3,))
            sa = load((8, 512), [(lambda v: v, w_mix[:, :, 544:1056])])
            sg_ = load((8, 512), [(lambda v: v, w_mix[:, :, 1056:1568])])
            t_hz = G(ge.memset, hp[:, :, 0:30], 0.0)
            t_h = []
            tsg = None
            for f in range(4):
                ba = feature(lambda k: sa.v[:, k, f * 128:(f + 1) * 128], X, [sa.ready])
                bg = feature(lambda k: sg_.v[:, k, f * 128:(f + 1) * 128], X, [sg_.ready])
                t = A(ae.activation, sgc, bg.t[:, 0:256], ACT.Sigmoid, bias=cL[:, 128 + f:129 + f], scale=1.0,
                      w=(bg.tk, tsg, t_cL[l], tcq))
                bg.free = [t]
                t = V(ve.scalar_tensor_tensor, hp[:, f, 30:286], ba.t[:, 0:256], cL[:, 124 + f:125 + f], sgc,
                      ALU.add, ALU.mult, w=(t, ba.tk))
                ba.free = [t]
                tsg = t
                t_h.append(t)
            sa.free = [ba.tk]
            sg_.free = [bg.tk]
            su = load((3584,), [(lambda v: v[:, 0:1536].rearrange("p (k n) -> p k n", k=2),
                                 T["mla_w_uq_2"][l].rearrange("(k p) n -> p k n", p=128)),
                                (lambda v: v[:, 1536:3584].rearrange("p (k n) -> p k n", k=2),
                                 T["mla_w_ukv_2"][l].rearrange("(k p) n -> p k n", p=128))])
            wuq = su.v[:, 0:1536].rearrange("p (k n) -> p k n", k=2)
            wukv = su.v[:, 1536:3584].rearrange("p (k h n) -> p k h n", k=2, h=8)
            for hh in range(4):
                b = bank()
                for i in range(2):
                    h = 2 * hh + i
                    for k in range(2):
                        tk = mm(b.t[0:64, i * 256:(i + 1) * 256], wukv[:, k, h, 0:64], cT[:, 1, k, :], k == 0,
                                k == 1, w=(b.w, su.ready, t_cT), inc=(i == 1 and k == 1))
                t_kh2 = A(ae.activation, Kh[0:64, 2 * hh:2 * hh + 2, :],
                          b.t[0:64, :].rearrange("p (a b) -> p a b", a=2), ACT.Copy, w=(tk,))
                b.free = [t_kh2]
            for tt in range(2):
                b = bank()
                for k in range(2):
                    tk = mm(b.t[:, :].rearrange("p (h n) -> p h n", h=8), cT[:, 1, k, tt * 128:(tt + 1) * 128],
                            wukv[:, k, :, 64:128], k == 0, k == 1, w=(b.w, su.ready, t_cT), inc=(k == 1))
                t_va = A(ae.activation, va[:, tt, :], b.t[:, :], ACT.Copy, w=(tk,))
                b.free = [t_va]
            t_q = t3
            for hh in range(4):
                b = bank()
                for i in range(2):
                    h = 2 * hh + i
                    for k in range(2):
                        tk = mm(b.t[0:96, i * 256:(i + 1) * 256], wuq[:, k, h * 96:(h + 1) * 96], cT[:, 0, k, :],
                                k == 0, k == 1, w=(b.w, su.ready, t_cT), inc=(i == 1 and k == 1))
                qv = qh[:, 2 * hh:2 * hh + 2, :]
                t = A(ae.activation, qv, b.t[0:96, :].rearrange("p (a b) -> p a b", a=2), ACT.Copy, w=(tk,))
                b.free = [t]
                b = bank()
                tk = mm(b.t[0:96, :], C("rot", 96), qv.rearrange("p a b -> p (a b)"), True, True, w=(b.w, t),
                        inc=True)
                for i in range(2):
                    t2 = V(ve.tensor_tensor, tq_[0][:, i, :], b.t[0:96, i * 256:(i + 1) * 256], RS, ALU.mult,
                           w=(tk, t_rs, t_q, t_kh))
                    t3 = V(ve.tensor_tensor, qv[:, i, :], qv[:, i, :], RC, ALU.mult, w=(tk, t_rc))
                b.free = [t2]
                t_q = V(ve.tensor_tensor, qv, qv, tq_[0], ALU.add, w=(t3, t2))
            su.free = [tk]
            SCL = 96.0 ** -0.5
            t_o = []
            n_ = 0
            prf = [None] * 3
            ptf = [None] * 3
            for j in range(2):
                kn = 128 * (j + 1)
                bo_ = bank()
                bo_.pin = True
                pend = {}
                for step in range(8 + 2):
                    if step < 8:
                        h = step
                        i = n_ % 3
                        b = bank()
                        mm(b.t[:, 0:kn], qh[:, h, j * 128:(j + 1) * 128], Kh[:, h, 0:kn], True, False,
                           w=(b.w, t_q, t_kh, t_kh2))
                        zo = CONST["zero"][0] + 128 * (1 - j)
                        b.tk = mm(b.t[:, 0:kn], C("ident"), cst[:, zo:zo + kn], False, True, inc=True)
                        te, tr_ = softmax(b, j * 8 + h, kn, pr[i][:, 0:kn], SCL, [prf[i]])
                        pend[h] = (i, te, tr_)
                        n_ += 1
                    if 1 <= step < 9:
                        h = step - 1
                        i, te, tr_ = pend[h]
                        b = bank()
                        for m in range(j + 1):
                            tk = tr(b.t[:, m * 128:(m + 1) * 128], pr[i][:, m * 128:(m + 1) * 128], w=(b.w, te),
                                    inc=(m == j))
                        prf[i] = tk
                        t = V(ve.tensor_copy, pT[i][:, 0:kn], b.t[:, 0:kn], w=(tk, ptf[i]))
                        b.free = [t]
                        pend[h] = (i, t, tr_)
                    if step >= 2:
                        h = step - 2
                        i, t, tr_ = pend[h]
                        for m in range(j + 1):
                            tk = mm(bo_.t[:, h * 64:(h + 1) * 64], pT[i][:, m * 128:(m + 1) * 128],
                                    va[:, m, h * 64:(h + 1) * 64], m == 0, m == j, w=(bo_.w, t, t_va), inc=(m == j))
                        ptf[i] = tk
                for h in range(8):
                    t = V(ve.tensor_scalar, otk[:, j, h * 64:(h + 1) * 64], bo_.t[:, h * 64:(h + 1) * 64],
                          sums[:, 1, j * 8 + h:j * 8 + h + 1], None, ALU.mult, w=(tk, pend[7][2]))
                bo_.free = [t]
                bo_.pin = False
                t_o.append(t)
            t_cat = turn(cat, otk, t_o, chunks=4)
            tcv = []
            for f in range(4):
                t = V(ve.tensor_scalar, yc[:, f, :], hp[:, f, 0:256], cL[:, f:f + 1], cL[:, 136 + f:137 + f],
                      ALU.mult, ALU.add, w=(t_h, t_hz))
                for j in range(1, 31):
                    t = V(ve.scalar_tensor_tensor, yc[:, f, :], hp[:, f, j:j + 256],
                          cL[:, 4 * j + f:4 * j + f + 1], yc[:, f, :], ALU.mult, ALU.add, w=(t,))
                tcv.append(t)
            b = bank()
            for f in range(4):
                tk = mm(b.t[:, 0:256], C("mean"), yc[:, f, :], f == 0, f == 3, w=(b.w, tcv[f]), inc=(f == 3))
            tsq = []
            for f in range(4):
                t = V(ve.tensor_tensor, yc[:, f, :], yc[:, f, :], b.t[:, 0:256], ALU.subtract, w=(tk,))
                tsq.append(A(ae.activation, cat[:, 4 + f, :], yc[:, f, :], ACT.Square, w=(t,)))
            b.free = [t]
            b = bank()
            for f in range(4):
                tk = mm(b.t[:, 0:256], C("mean"), cat[:, 4 + f, :], f == 0, f == 3, w=(b.w, tsq[f]), inc=(f == 3))
            t = V(ve.tensor_scalar, sgc, b.t[:, 0:256], 1e-5, None, ALU.add, w=(tk,))
            b.free = [t]
            t = A(ae.activation, sgc, sgc, ACT.Sqrt, w=(t,))
            t = V(ve.reciprocal, sgc, sgc, w=(t,))
            for f in range(4):
                t2 = V(ve.tensor_tensor, yc[:, f, :], yc[:, f, :], sgc, ALU.mult, w=(t,))
                t_cv = A(ae.activation, cat[:, 4 + f, :], yc[:, f, :], ACT.Silu, bias=cL[:, 144 + f:145 + f],
                         scale=cL[:, 140 + f:141 + f], w=(t2, tk))
            bs = dense(cat, T["mix_w_o_2"][l].rearrange("(k p) n -> p k n", p=128), [t_cat, t_cv])
            t = residual(ALPHA2, bs, None, None)
            t_x = ln_affine(T["ln1_g_2"][l], T["ln1_b_2"][l], t)

            barrier()
            w_kv = T["xa_w_kv_2"][l].rearrange("(k p) n -> p k n", p=128)
            w_q = T["xa_w_q_2"][l].rearrange("(k p) n -> p k n", p=128)
            kx = arena(8, 256, reset=base)
            vx = arena(2, 1024)
            qx = arena(8, 256)
            ox = arena(8, 256)
            pr = [arena(256) for _ in range(4)]
            pT = [arena(2, 256) for _ in range(2)]
            M_ = lambda k: memT[:, k, :]
            for hf in range(2):
                s = load((8, 512), [(lambda v: v, w_kv[:, :, hf * 512:(hf + 1) * 512])])
                for f in range(4):
                    b = feature(lambda k: s.v[:, k, f * 128:(f + 1) * 128], M_, [s.ready, t_mT])
                    t_kx = A(ae.activation, kx[:, hf * 4 + f, :], b.t[:, 0:256], ACT.Copy, w=(b.tk,))
                    b.free = [t_kx]
                s.free = [b.tk]
            for hf in range(2):
                s = load((8, 512), [(lambda v: v, w_kv[:, :, 1024 + hf * 512:1024 + (hf + 1) * 512])])
                for tt in range(2):
                    b = token(lambda k: memT[:, k, tt * 128:(tt + 1) * 128], lambda k: s.v[:, k, :], 512, [s.ready])
                    t_vx = A(ae.activation, vx[:, tt, hf * 512:(hf + 1) * 512], b.t[:, :], ACT.Copy, w=(b.tk,))
                    b.free = [t_vx]
                s.free = [b.tk]
            t_XT = turn(XT, xtok, [t_x])
            for hf in range(2):
                s = load((8, 512), [(lambda v: v, w_q[:, :, hf * 512:(hf + 1) * 512])])
                for f in range(4):
                    b = feature(lambda k: s.v[:, k, f * 128:(f + 1) * 128], X, [s.ready] + t_XT)
                    t_qx = A(ae.activation, qx[:, hf * 4 + f, :], b.t[:, 0:256], ACT.Copy, w=(b.tk,))
                    b.free = [t_qx]
                s.free = [b.tk]
            prf = [None] * 4
            ptf = [None] * 2
            pend = {}
            for step in range(4 + 2):
                if step < 4:
                    h = step
                    for j in range(2):
                        i = (2 * h + j) % 4
                        b = bank()
                        for c in range(2):
                            b.tk = mm(b.t[:, 0:256], qx[:, 2 * h + c, j * 128:(j + 1) * 128], kx[:, 2 * h + c, :],
                                      c == 0, c == 1, w=(b.w, t_qx, t_kx), inc=(c == 1))
                        te, tr_ = softmax(b, 16 + 2 * h + j, 256, pr[i], 1.0 / 16, [prf[i]])
                        pend[(h, j)] = V(ve.tensor_scalar, pr[i], pr[i],
                                         sums[:, 1, 16 + 2 * h + j:17 + 2 * h + j], None, ALU.mult, w=(te, tr_))
                if 1 <= step < 5:
                    h = step - 1
                    b = bank()
                    for j in range(2):
                        i = (2 * h + j) % 4
                        for m in range(2):
                            tk = tr(b.t[:, m * 256 + j * 128:m * 256 + (j + 1) * 128],
                                    pr[i][:, m * 128:(m + 1) * 128], w=(b.w, pend[(h, j)]), inc=(m == 1))
                        prf[i] = tk
                    t = V(ve.tensor_copy, pT[h % 2].rearrange("p a b -> p (a b)"), b.t[:, :], w=(tk, ptf[h % 2]))
                    b.free = [t]
                    pend[h] = t
                if step >= 2:
                    h = step - 2
                    for d in range(2):
                        b = bank()
                        o0 = h * 256 + d * 128
                        for m in range(2):
                            tk = mm(b.t[:, 0:256], vx[:, m, o0:o0 + 128], pT[h % 2][:, m, :], m == 0, m == 1,
                                    w=(b.w, t_vx, pend[h]), inc=(m == 1))
                        t_ox = A(ae.activation, ox[:, 2 * h + d, :], b.t[:, 0:256], ACT.Copy, w=(tk,))
                        b.free = [t_ox]
                    ptf[h % 2] = tk
            bs = dense(ox, T["xa_w_o_2"][l].rearrange("(k p) n -> p k n", p=128), [t_ox])
            t = residual(ALPHA2, bs, None, None)
            t_x = ln_affine(T["ln2_g_2"][l], T["ln2_b_2"][l], t)

            barrier()
            t_XT = turn(XT, xtok, [t_x])
            ff_ = arena(22, 256, reset=base)
            sl = [arena(256) for _ in range(2)]
            slf = [None] * 2
            w_f = T["ffn_w_in_2"][l].rearrange("(k p) n -> p k n", p=128)
            w_d = T["ffn_w_down_2"][l].rearrange("(k p) n -> p k n", p=128)
            for q in range(11):
                s = load((2, 8, 256), [(lambda v: v[:, 0], w_f[:, :, q * 256:(q + 1) * 256]),
                                       (lambda v: v[:, 1], w_f[:, :, 2816 + q * 256:2816 + (q + 1) * 256])])
                for g2 in range(2):
                    f = 2 * q + g2
                    i = f % 2
                    bg = feature(lambda k: s.v[:, 0, k, g2 * 128:(g2 + 1) * 128], X, [s.ready] + t_XT)
                    bu = feature(lambda k: s.v[:, 1, k, g2 * 128:(g2 + 1) * 128], X, [s.ready])
                    t = A(ae.activation, sl[i], bg.t[:, 0:256], ACT.Silu, w=(bg.tk, slf[i]))
                    bg.free = [t]
                    t_f = V(ve.tensor_tensor, ff_[:, f, :], bu.t[:, 0:256], sl[i], ALU.mult, w=(t, bu.tk))
                    bu.free = [t_f]
                    slf[i] = t_f
                s.free = [bu.tk]
            bb = {(tt, h): bank() for h in range(2) for tt in range(2)}
            for q in range(6):
                kn = 4 if q < 5 else 2
                s = load((kn, 1024), [(lambda v: v, w_d[:, 4 * q:4 * q + kn, :])])
                for k in range(kn):
                    kk = 4 * q + k
                    for (tt, h), b in bb.items():
                        b.tk = mm(b.t[:, :], ff_[:, kk, tt * 128:(tt + 1) * 128], s.v[:, k, h * 512:(h + 1) * 512],
                                  kk == 0, kk == 21, w=(b.w, s.ready, t_f), inc=(k == kn - 1))
                s.free = [b.tk]
            t = residual(ALPHA2, [(tt, h, b) for (tt, h), b in bb.items()], None, None)
            t_x = ln_affine(T["ln3_g_2"][l], T["ln3_b_2"][l], t)
        return finish(nc, ctx, PE, V, A, G, SP, out, xtok, sem)


def finish(nc, ctx, PE, V, A, G, SP, out, xtok, sem):
    s = sem("s_out")
    toks = [q.last() for q in (PE, V, A, G) if q.count]
    for tt in range(2):
        SP.items.append((toks, nc.sync.dma_start, (out[0, tt * 128:(tt + 1) * 128, :], xtok[:, tt, :]), {}, s, 16))
    SP.items.append(((( s, 32),), None, (), {}, None, 0))
    block = ctx.enter_context(nc.Block())

    @block.sync
    def _(eng):
        emit(eng, SP.items)

    @block.gpsimd
    def _(eng):
        emit(eng, G.items)

    @block.scalar
    def _(eng):
        emit(eng, A.items)

    @block.vector
    def _(eng):
        emit(eng, V.items)

    @block.tensor
    def _(eng):
        emit(eng, PE.items)


_INS = ["x", "c", "ctx", "c_ctx", "w_ada", "b_ada", "w_in", "b_in", "pool_w", "pool_scale", "qk_conv_w", "qk_conv_b",
        "mlstm_norm_g", "sgu_ln_g", "sgu_ln_b", "sgu_w", "sgu_b", "w_br_pool", "w_br_mlstm", "w_br_sgu", "w_out",
        "ln1_g", "ln1_b", "w_router", "b_router", "w_gate_up", "b_gate_up", "w_down", "b_down", "ln2_g", "ln2_b",
        "mem_2", "positions_2", "mix_w_in_2", "mix_b_in_2", "mla_q_norm_2", "mla_w_uq_2", "mla_kv_norm_2",
        "mla_w_ukv_2", "conv_dw_w_2", "conv_dw_b_2", "conv_norm_g_2", "conv_norm_b_2", "mix_w_o_2", "ln1_g_2",
        "ln1_b_2", "xa_w_q_2", "xa_w_kv_2", "xa_w_o_2", "ln2_g_2", "ln2_b_2", "ffn_w_in_2", "ffn_w_down_2",
        "ln3_g_2", "ln3_b_2"]


def kernel(**inputs):
    import concourse.bacc as bacc
    from concourse.bass_utils import run_bass_kernel_spmd

    nc = bacc.Bacc("TRN2", target_bir_lowering=False, num_devices=1)
    arrays, T = {}, {}
    for name in _INS:
        a = np.ascontiguousarray(inputs[name])
        arrays["in_" + name] = a
        T[name] = nc.dram_tensor("in_" + name, a.shape, mybir.dt.from_np(a.dtype), kind="ExternalInput").ap()
    arrays["in_const"] = constants()
    T["const"] = nc.dram_tensor("in_const", arrays["in_const"].shape, F32, kind="ExternalInput").ap()
    out = nc.dram_tensor("out_0", (1, 256, 1024), F32, kind="ExternalOutput").ap()
    build(nc, T, out)
    r = run_bass_kernel_spmd(nc, [arrays], core_ids=[0])
    return r.results[0]["out_0"]
```

```python
from contextlib import ExitStack

import numpy as np

import concourse.bass as bass
from concourse import mybir

F32 = mybir.dt.float32
FR = mybir.dt.float32r
I32 = mybir.dt.int32
ALU = mybir.AluOpType
ACT = mybir.ActivationFunctionType
AX = mybir.AxisListType
ALPHA1 = 2.0 ** 0.25
ALPHA2 = 4.0 ** 0.25
NEG = -1e30
UNITS = 12
STEM = 640

CONST = {}
_at = 0
for _name, _w in (("ident", 128), ("comb", 2), ("combb", 128), ("nhalf", 8), ("maskf", 128), ("maskb", 128), ("zero", 128), ("maskc", 128), ("pool", 512), ("rot", 96),
                  ("freq", 1), ("sel", 1024), ("mean", 128), ("ones", 128), ("tri", 128), ("iota", 512)):
    CONST[_name] = (_at, _w)
    _at += _w
NCONST = _at


def constants():
    c = np.zeros((128, NCONST), np.float32)
    p = np.arange(128)

    def put(name, a):
        o, w = CONST[name]
        c[:a.shape[0], o:o + w] = a

    put("ident", np.eye(128))
    put("maskf", np.where(p[:, None] <= p[None, :], 0.0, NEG))
    put("maskb", np.where(p[:, None] >= p[None, :], 0.0, NEG))
    put("maskc", np.where((p[:, None] < 64) & (p[None, :] >= 64), NEG, 0.0))
    pool = np.zeros((128, 4, 128))
    for g, w in enumerate((2, 4, 8, 16)):
        for t in range(128):
            base, tt = t // 64 * 64, t % 64
            lo, hi = max(tt - w // 2, 0), min(tt + w // 2, 64)
            pool[base + lo:base + hi, g, t] += 1.0 / (hi - lo)
            pool[t, g, t] -= 1.0
    put("pool", pool.reshape(128, 512))
    rot = np.zeros((96, 96))
    freq = np.zeros((96, 1), np.float32)
    for i in range(16):
        rot[80 + i, 64 + i] = -1.0
        rot[64 + i, 80 + i] = 1.0
    inv = np.float32(10000.0) ** (-np.arange(0, 32, 2, dtype=np.float32) / np.float32(32))
    freq[64:80, 0] = inv
    freq[80:96, 0] = inv
    put("rot", rot)
    put("freq", freq)
    sel = np.zeros((64, 8, 128))
    for r in range(8):
        sel[32 * (r // 4) + r % 4, r, :] = 1.0
    put("sel", sel.reshape(64, 1024))
    put("mean", np.full((128, 128), 1.0 / 512))
    put("ones", np.ones((128, 128)))
    comb = (p[:, None] % 32 == np.arange(2)[None, :]).astype(np.float32)
    put("comb", comb)
    put("combb", np.repeat(comb[:, 0:1], 128, axis=1))
    put("tri", np.where(p[:, None] < p[None, :], 1.0, 0.0))
    put("iota", np.broadcast_to((64 * np.arange(4)[:, None, None] + np.zeros((1, 2, 1)) +
                                 np.arange(64)[None, None, :]).reshape(1, 512), (128, 512)))
    put("nhalf", np.full((128, 8), -0.5))
    return c


class Queue:

    def __init__(self, sems, serial=False):
        self.serial = serial
        self.sems, self.n, self.count, self.items = sems, 0, 0, []

    def __call__(self, fn, *args, w=(), inc=True, **kw):
        if self.serial and self.count:
            w = tuple(w) + (self.last(),)
        if self.count >= 1000 and len(self.sems) > 1:
            self.n += 1
            self.count = 0
        sem = self.sems[self.n] if inc else None
        self.items.append((w, fn, args, kw, sem, 1))
        if inc:
            self.count += 1
            return (sem, self.count)
        return None

    def last(self):
        return (self.sems[self.n], self.count)


class Branch:

    def __init__(self, flag, tiles):
        self.flag, self.tiles = flag, tiles


def emit(eng, items, seen=None):
    seen = {} if seen is None else seen

    def wait(w):
        if w is None:
            return
        if isinstance(w, list):
            for x in w:
                wait(x)
            return
        sem, value = w
        if seen.get(id(sem), 0) < value:
            eng.wait_ge(sem, value)
            seen[id(sem)] = value

    def skip(tiles):
        skipped = {}
        for tile in tiles:
            for w, fn, args, kw, sem, by in tile:
                if sem is not None:
                    skipped[id(sem)] = (sem, skipped.get(id(sem), (sem, 0))[1] + by)
        for sem, n in skipped.values():
            eng.sem_inc(sem, n)

    def branches(number, tiles, seen):
        with eng.If(number >= 1):
            with eng.If(number >= 2):
                with eng.If(number >= 3):
                    emit(eng, tiles[2], dict(seen))
                with eng.Else():
                    skip(tiles[2:])
                emit(eng, tiles[1], dict(seen))
            with eng.Else():
                skip(tiles[1:])
            emit(eng, tiles[0], dict(seen))
        with eng.Else():
            skip(tiles)

    for item in items:
        if isinstance(item, Branch):
            number = eng.value_load(item.flag, min_val=0, max_val=3)
            branches(number, item.tiles, seen)
            continue
        w, fn, args, kw, sem, by = item
        for x in w:
            wait(x)
        if fn is None:
            continue
        ins = fn(*args, **kw)
        if sem is not None:
            ins.then_inc(sem, by)


class Box:

    def __init__(self, t, sem=None):
        self.t, self.sem, self.n, self.free, self.ready = t, sem, 0, [], None
        self.pin, self.w = False, []


class Feed:

    def __init__(self, boxes):
        self.boxes, self.got = boxes, []

    def ahead(self):
        for b in self.boxes:
            self.got.append(b)
            return

    def take(self):
        if not self.got:
            self.ahead()
        return self.got.pop(0)


class Lease:

    def __init__(self, boxes, view, ready):
        self.boxes, self.t, self.v, self.ready = boxes, view, view, ready

    @property
    def free(self):
        return self.boxes[0].free

    @free.setter
    def free(self, tokens):
        for b in self.boxes:
            b.free, b.pin = tokens, False


def build(nc, T, out):
    ctx = ExitStack()
    with ctx:
        def sb(name, shape, dt=F32):
            return ctx.enter_context(nc.sbuf_tensor(name, shape, dt))

        def sem(name):
            return ctx.enter_context(nc.semaphore(name))

        PE = Queue([sem(f"s_pe{i}") for i in range(6)])
        V = Queue([sem(f"s_v{i}") for i in range(8)])
        A = Queue([sem(f"s_a{i}") for i in range(6)])
        G = Queue([sem(f"s_g{i}") for i in range(4)], serial=True)
        SP = Queue([])
        ve, ae, ge, pe = nc.vector, nc.scalar, nc.gpsimd, nc.tensor

        cst = sb("cst", [128, NCONST])

        def C(name, rows=128):
            o, w = CONST[name]
            return cst[0:rows, o:o + w]

        ring_at = -(-nc.sbuf_base // 32) * 32
        ring = sb("ring", [128, 2048 * UNITS])
        units = [Box(None, sem(f"s_w{i}")) for i in range(UNITS)]
        banks = [Box(ctx.enter_context(nc.psum_tensor(f"ps{i}", [128, 512], F32))) for i in range(8)]
        small_sems = [sem(f"s_c{i}") for i in range(26)]
        state = {"slot": 0, "bank": 0, "small": 0, "units": UNITS}

        def lease(n, parts, pin=False):
            k = -(-n // 2048)
            top = state["units"]
            i = state["slot"] % top
            while i + k > top or any(u.pin for u in units[i:i + k]):
                i = (i + 1) % top
            state["slot"] = i + k
            boxes = units[i:i + k]
            frees = [u.free for u in boxes]
            assert None not in frees
            view = ring[:, i * 2048:i * 2048 + n]
            got = parts(view)
            first = boxes[0]
            for dst, src in got:
                SP.items.append((frees, nc.sync.dma_start, (dst, src), {}, first.sem, 16))
            first.n += 16 * len(got)
            for u in boxes:
                u.free, u.pin = None, pin
            s = Lease(boxes, view, (first.sem, first.n))
            s.frees, s.at = frees, i
            return s

        def load(shape, parts):
            def cut(view):
                if len(shape) == 2:
                    return view.rearrange("p (a b) -> p a b", a=shape[0])
                if len(shape) == 3:
                    return view.rearrange("p (a b c) -> p a b c", a=shape[0], b=shape[1])
                return view

            s = lease(int(np.prod(shape)), lambda view: [(f(cut(view)), src) for f, src in parts])
            s.v = cut(s.t)
            return s

        def load_rows(vectors):
            def parts(view):
                got, at = [], 0
                for v in vectors:
                    n = v.shape[1]
                    got.append((view[:, at:at + n], v.broadcast_to((128, n))))
                    at += n
                return got

            return lease(sum(v.shape[1] for v in vectors), parts, pin=True)

        def small(parts, w=(), q=None):
            eng = nc.sync if q is None else nc.gpsimd
            s = small_sems[state["small"]]
            state["small"] += 1
            for dst, src in parts:
                (q or SP).items.append((list(w), eng.dma_start, (dst, src), {}, s, 16))
            return (s, 16 * len(parts))

        def bank():
            while banks[state["bank"] % 8].pin:
                state["bank"] += 1
            b = banks[state["bank"] % 8]
            state["bank"] += 1
            assert b.free is not None
            b.w, b.free = b.free, None
            return b

        def mm(o, l, r, start, stop, w=(), inc=False, tp=None):
            if tp is None:
                return PE(pe.matmul, o, l, r, w=w, inc=inc, start=start, stop=stop)
            return PE(pe.matmul, o, l, r, w=w, inc=inc, start=start, stop=stop, tile_position=tp)

        def tr(o, i, w=(), inc=False, k=128):
            return PE(pe.transpose, o, i, C("ident", k)[:, 0:k], w=w, inc=inc)

        FILL = []

        def fill(n=1):
            for _ in range(min(n, len(FILL))):
                FILL.pop(0)()

        def barrier():
            toks = [q.last() for q in (PE, V, A, G) if q.count]
            for q in (PE, V, A, G):
                q.items.append((list(toks), None, (), {}, None, 0))

        def row(v, a=None, b=None):
            v = v.rearrange("(o n) -> o n", o=1)
            return v if a is None else v[:, a:b]

        xtok = sb("xtok", [128, 2, 1024])
        xt_at = -(-nc.sbuf_base // 32) * 32
        XT = sb("XT", [128, 8, 256])
        st6 = sb("st6", [128, 16, 6])
        mv = sb("mv", [128, 16, 2])
        rstd = sb("rstd", [128, 16])
        wrt = sb("wrt", [128, 8, 32])
        ar_at = -(-nc.sbuf_base // 32) * 32
        AR = sb("AR", [128, 17020])
        ar = {"at": 0}

        def arena(*shape, p=128, reset=None):
            if reset is not None:
                ar["at"] = reset
            n = int(np.prod(shape))
            v = AR[0:p, ar["at"]:ar["at"] + n]
            ar["at"] += n
            assert ar["at"] <= 17020, ar["at"]
            if len(shape) == 2:
                v = v.rearrange("p (a b) -> p a b", a=shape[0])
            if len(shape) == 3:
                v = v.rearrange("p (a b c) -> p a b c", a=shape[0], b=shape[1])
            return v

        def rows128(v):
            return v.rearrange("(r c) -> r c", c=128)

        def columns(parts, dst, i, w=()):
            n = sum(s.shape[0] for _, s in parts)
            t = small([(stage[i][a:a + s.shape[0], :], s) for a, s in parts])
            b = bank()
            tk = tr(b.t[:, 0:n], stage[i][0:n, :], w=(t, t_const, b.w), inc=True, k=n)
            tv = V(ve.tensor_copy, dst, b.t[:, 0:n], w=(tk,) + tuple(w))
            b.free = [tv]
            return tk, tv

        def stats(srcs, eps, base, w=()):
            n = len(srcs)
            for i, s in enumerate(srcs):
                f = s.shape[1]
                if f > 512:
                    for k in range(2):
                        t = V(ve.bn_stats, st6[:, 2 * i + k + base, :], s[:, k * 512:(k + 1) * 512], w=w)
                else:
                    t = V(ve.bn_stats, st6[:, i + base, :], s, w=w)
            for i, s in enumerate(srcs):
                if s.shape[1] > 512:
                    src = st6[:, base + 2 * i:base + 2 * i + 2, :]
                else:
                    src = st6[:, base + i, :]
                t2 = V(ve.bn_aggr, mv[:, base + i, :], src, w=(t,))
            t3 = V(ve.tensor_scalar, rstd[:, base:base + n], mv[:, base:base + n, 1], eps, None, ALU.add, w=(t2,))
            return G(ge.tensor_tensor, rstd[:, base:base + n], rstd[:, base:base + n],
                     C("nhalf")[:, 0:n], ALU.pow, w=(t3, t_const))

        def normal(dst, src, i, w=()):
            return V(ve.tensor_scalar, dst, src, mv[:, i, 0:1], rstd[:, i:i + 1], ALU.subtract, ALU.mult, w=w)

        def turn(dst, src, w, scale=None, bias=None, chunks=8):
            last = None
            for k0 in range(0, chunks, 2):
                b = bank()
                for k in (k0, k0 + 1):
                    for tt in range(2):
                        j = (k - k0) * 2 + tt
                        t = tr(b.t[:, j * 128:(j + 1) * 128], src[:, tt, k * 128:(k + 1) * 128],
                               w=(b.w, w), inc=(j == 3))
                for k in (k0, k0 + 1):
                    src_ = b.t[:, (k - k0) * 256:(k - k0 + 1) * 256]
                    eng = A if k0 % 4 else V
                    if eng is A:
                        last = A(ae.activation, dst[:, k, :], src_, ACT.Identity,
                                 bias=(0.0 if bias is None else bias[:, k:k + 1]),
                                 scale=(1.0 if scale is None else scale[:, k:k + 1]), w=(t,))
                        la = last
                    else:
                        if scale is None:
                            last = V(ve.tensor_copy, dst[:, k, :], src_, w=(t,))
                        else:
                            last = V(ve.tensor_scalar, dst[:, k, :], src_, scale[:, k:k + 1],
                                     0.0 if bias is None else bias[:, k:k + 1], ALU.mult, ALU.add, w=(t,))
                        lv = last
                b.free = [last]
            return [la, lv] if chunks > 2 else [lv]

        def feature(wcols, xT, w, n=256, kk=8):
            b = bank()
            for k in range(kk):
                l = wcols(k)
                t = mm(b.t[0:l.shape[1], 0:n], l, xT(k), k == 0, k == kk - 1, w=(b.w, w), inc=(k == kk - 1))
            b.tk = t
            return b

        def token(xT, wcols, n, w, kk=8, b=None, first=True, last=True):
            b = b or bank()
            for k in range(kk):
                t = mm(b.t[:, 0:n], xT(k), wcols(k), first and k == 0, last and k == kk - 1,
                       w=(b.w, w) if first else (w,), inc=(k == kk - 1))
            b.tk = t
            return b

        stage = [AR[:, 7168 + 128 * i:7296 + 128 * i] for i in range(10)]
        t_const = small([(cst[:, 0:266], T["const"][:, 0:266])])
        keep = lease(6144, lambda view: [], pin=True)
        sig = keep.t.rearrange("p (a b) -> p a b", a=24)
        odd = lease(2048, lambda view: [], pin=True)
        adr = [odd.t[:, 0:512], odd.t[:, 512:1024]]
        wsT = odd.t[:, 1024:1536].rearrange("p (g t) -> p g t", g=4)
        xc = arena(2, 1024)
        b_in = T["b_in"][0]
        colA = sb("colA", [128, 128])
        colB = sb("colB", [128, 32])
        b_ada = T["b_ada"][0]
        _, t_cA = columns([(0, rows128(T["c"][0])), (8, rows128(T["c_ctx"])), (16, rows128(b_ada)),
                           (64, rows128(b_in[256:1280])), (72, rows128(b_in[1792:2304])),
                           (76, rows128(b_in[2320:2576])), (78, rows128(b_in[2832:5904])),
                           (102, rows128(T["pool_scale"][0])),
                           (104, T["qk_conv_w"][0].rearrange("j (r c) -> (j r) c", c=128))], colA[:, :], 0)
        w_ada = T["w_ada"][0].rearrange("(k p) n -> p k n", p=128)
        ada_s = {}

        def load_ada(part, h):
            ada_s[(part, h)] = load((8, 512), [(lambda v: v, w_ada[:, :, part * 1024 + h * 512:
                                                                   part * 1024 + (h + 1) * 512])])

        load_ada(0, 0)
        load_ada(0, 1)
        load_ada(1, 0)
        scT = sb("scT", [128, 2, 8])
        t_sc = A(ae.activation, scT[:, :, :].rearrange("p a b -> p (a b)"), colA[:, 0:16], ACT.Silu, w=(t_cA,))
        scP = odd.t[:, 1536:1792].rearrange("p (k m) -> p k m", k=8)
        t_z = V(ve.memset, scP, 0.0)
        for i in range(2):
            t_scb = V(ve.tensor_copy, scP[:, :, i], scT[:, i, :], w=(t_sc, t_z))
        modT = sb("modT", [128, 6, 8, 2])
        gB = sb("gB", [128, 2, 1024])

        adf = [None, None]

        def ada_half(part, h):
            if (part, h) not in ada_s:
                load_ada(part, h)
            s = ada_s[(part, h)]
            b = bank()
            for k in range(8):
                o = 32 * (k % 4)
                t = PE(pe.matmul, b.t[o:o + 32, :], scP[:, k, :], s.v[:, k, :], start=(k < 4), stop=(k >= 4),
                       tile_position=(0, o), skip_group_check=True, w=(b.w, s.ready, t_scb), inc=(k == 7))
            s.free = [t]
            t = A(ae.activation, adr[h], b.t[:, :], ACT.Copy, w=(t, adf[h]))
            b.free = [t]
            return t

        def ada_cols(part, h):
            ta = ada_half(part, h)
            b = bank()
            for f in range(4):
                t = mm(b.t[:, f * 2:f * 2 + 2], adr[h][:, f * 128:(f + 1) * 128], C("comb"), True, True,
                       w=(b.w, ta), inc=(f == 3))
            adf[h] = t
            f0 = 16 + part * 8 + h * 4
            for src in range(2):
                tv = V(ve.tensor_tensor, modT[:, part, h * 4:h * 4 + 4, src],
                       b.t[:, 0:8].rearrange("p (f s) -> p f s", s=2)[:, :, src], colA[:, f0:f0 + 4],
                       ALU.add, w=(t, t_cA))
            b.free = [tv]
            if part in (1, 4):
                tv = V(ve.tensor_scalar, modT[:, part, h * 4:h * 4 + 4, :], modT[:, part, h * 4:h * 4 + 4, :],
                       1.0, None, ALU.add, w=(tv,))
            MD[part] = tv
            return tv

        def ada_rows(part, g, h):
            ta = ada_half(part, h)
            b = bank()
            t = mm(b.t[:, :], C("combb"), adr[h], True, True, w=(b.w, ta), inc=True)
            adf[h] = t
            o = g * 1024 + h * 512
            tv = V(ve.tensor_tensor, gB[:, g, h * 512:(h + 1) * 512], b.t[:, :], rowg.t[:, o:o + 512], ALU.add,
                   w=(t, rowg.ready))
            b.free = [tv]
            MD["g", g] = tv
            return tv

        MD = {}

        t_x = small([(xtok[:, tt, :], T["x"][0, tt * 128:(tt + 1) * 128, :]) for tt in range(2)])
        for part in range(2):
            for h in range(2):
                ada_cols(part, h)
        t_c = small([(xc[:, tt, :], T["ctx"][0, tt * 128:(tt + 1) * 128, :]) for tt in range(2)])
        t_const2 = small([(cst[:, 266:NCONST], T["const"][:, 266:NCONST])])
        _, t_cB = columns([(0, rows128(T["qk_conv_b"][0])), (8, rows128(T["mlstm_norm_g"][0]))], colB[:, 0:12], 1)
        rowb = load_rows([row(b_in, 0, 256), row(b_in, 1280, 1792), row(b_in, 2576, 2832),
                          row(T["sgu_ln_g"][0]), row(T["sgu_ln_b"][0]),
                          T["sgu_b"][0].rearrange("g (o t) -> o (g t)", o=1)])
        colL = [sb(f"colL{l}", [128, 152]) for l in range(2)]
        t_cL = []
        for l in range(2):
            columns([(0, T["conv_dw_w_2"][l].rearrange("j (r c) -> (j r) c", c=128))], colL[l][:, 0:124], 2 + 2 * l)
            t_cL.append(columns([(0, rows128(T["mix_b_in_2"][l][544:1568])), (8, rows128(T["mla_q_norm_2"][l])),
                                 (10, rows128(T["mla_kv_norm_2"][l])), (12, rows128(T["conv_dw_b_2"][l])),
                                 (16, rows128(T["conv_norm_g_2"][l])), (20, rows128(T["conv_norm_b_2"][l]))],
                                colL[l][:, 124:148], 3 + 2 * l)[1])
        poolw = sb("poolw", [128, 2, 128])
        sguw = sb("sguw", [128, 4, 128])
        gb = sb("gb", [64, 2])
        tz = [G(ge.memset, poolw[:, :, :], 0.0), G(ge.memset, gb[:, :], 0.0)]
        gsem = small_sems[state["small"]]
        state["small"] += 1
        gl = [(poolw[(g % 2) * 64:(g % 2) * 64 + 64, g // 2, (g % 2) * 64:(g % 2) * 64 + 64], T["pool_w"][0, g])
              for g in range(4)]
        for kind in range(4):
            o = 2304 + 4 * kind
            p0 = 32 * (kind // 2)
            gl.append((gb[p0:p0 + 4, kind % 2:kind % 2 + 1], b_in[o:o + 4].rearrange("(a o) -> a o", o=1)))
        gl.append((sguw[:, :, :], T["sgu_w"][0].rearrange("g t s -> t g s")))
        for d, s in gl:
            SP.items.append(([tz], nc.sync.dma_start, (d, s), {}, gsem, 16))
        t_gl = (gsem, 16 * len(gl))

        rowg = load_rows([row(b_ada, 2048, 3072), row(b_ada, 5120, 6144)])

        ts = stats([xtok[:, 0, :], xtok[:, 1, :], xc[:, 0, :], xc[:, 1, :]], 1e-5, 0, w=(t_x, t_c))
        xn = arena(2, 1024)
        for tt in range(2):
            tn = normal(xn[:, tt, :], xtok[:, tt, :], tt, w=(ts,))
            tnc = normal(xc[:, tt, :], xc[:, tt, :], 2 + tt, w=(ts,))
        XC = arena(8, 256, reset=5120)
        t_XT = turn(XT, xn, [tn], modT[:, 1, :, 0], modT[:, 0, :, 0])
        t_XC = turn(XC, xc, [tnc], modT[:, 1, :, 1], modT[:, 0, :, 1])
        barrier()

        w_in = T["w_in"][0].rearrange("(k p) n -> p k n", p=128)
        X = lambda k: XT[:, k, :]
        XCk = lambda k: XC[:, k, :]
        zpad = arena(2, 258, reset=7168)
        cva = arena(256)
        cvb = arena(256)
        qkT = arena(12, 256)
        vaug = arena(4, 4, 129)
        kN = arena(4, 4, 128)
        bo = 0
        ptok = arena(2, 256, reset=0)
        vs = arena(2, 256)
        uT = arena(2, 256)
        soT = arena(4, 256)
        poolT = arena(2, 256)
        sguT = arena(2, 256)
        dT = arena(2, 256)
        assert ar["at"] <= 5120
        KS = 128.0 ** -0.5

        tz0 = V(ve.memset, zpad[:, :, 0:1], 0.0)
        tz1 = V(ve.memset, zpad[:, :, 257:258], 0.0, w=(tz0,))
        tz2 = V(ve.memset, vaug[:, :, :, 128:129], 1.0)

        s = load((8, 16 + 496), [(lambda v: v, w_in[:, :, 2304:2816])])
        s2 = load((8, 16), [(lambda v: v, w_in[:, :, 2816:2832])])
        wg = AR[:, 13332:14356].rearrange("p (k i m) -> p k i m", k=8, i=2)
        tg = G(ge.memset, wg[:, :, :, :], 0.0)
        for kind in range(4):
            p0 = 32 * (kind // 2)
            tg = G(ge.tensor_copy, wg[:, :, kind % 2, p0:p0 + 4], s.v[:, :, 4 * kind:4 * kind + 4],
                   w=(tg, s.ready))
        rI = arena(512, p=64, reset=4096)
        rF = arena(512, p=64)
        bc = arena(512, p=64, reset=15380)
        tmpR = arena(512, p=64)
        uR = arena(512, p=64, reset=14356)
        MR = arena(512, p=64, reset=16416)
        for i, dst in ((0, rI), (1, rF)):
            b = bank()
            for k in range(8):
                mm(b.t[0:64, 0:256], wg[:, k, i, :], XC[:, k, :], k == 0, k == 7, w=(b.w, tg))
            for k in range(8):
                t = mm(b.t[0:64, 256:512], wg[:, k, i, :], XT[:, k, :], k == 0, k == 7, inc=(k == 7))
            t_if = A(ae.activation, dst, b.t[0:64, :], ACT.Identity, bias=gb[:, i:i + 1], scale=1.0, w=(t, t_gl))
            b.free = [t_if]
        for f in range(2):
            b = feature(lambda k: s.v[:, k, 16 + f * 128:144 + f * 128], X, [s.ready])
            t_u = A(ae.activation, uT[:, f, :], b.t[:, 0:256], ACT.Gelu, bias=colA[:, 76 + f:77 + f], scale=1.0,
                    w=(b.tk,))
            b.free = [t_u]
        for tt in range(2):
            b = bank()
            for k in range(8):
                mm(b.t[:, 0:240], XT[:, k, tt * 128:(tt + 1) * 128], s.v[:, k, 272:512], k == 0, k == 7,
                   w=(b.w, s.ready))
            for k in range(8):
                t = mm(b.t[:, 240:256], XT[:, k, tt * 128:(tt + 1) * 128], s2.v[:, k, :], k == 0, k == 7,
                       w=(s2.ready,), inc=(k == 7))
            tv = V(ve.tensor_tensor, vs[:, tt, :], b.t[:, 0:256], rowb.t[:, 768:1024], ALU.add, w=(t,))
            b.free = [tv]
            ta = A(ae.activation, vs[:, tt, :], vs[:, tt, :], ACT.Gelu, w=(tv,))
        s.free = [t, tg]
        s2.free = [t]

        te = V(ve.scalar_tensor_tensor, tmpR, rF, -1.0, rF, ALU.mult, ALU.max, w=(t_if,))
        te = A(ae.activation, tmpR, tmpR, ACT.Exp, scale=-1.0, w=(te,))
        te = A(ae.activation, tmpR, tmpR, ACT.Ln, bias=1.0, w=(te,))
        te = V(ve.scalar_tensor_tensor, rF, rF, 0.0, tmpR, ALU.min, ALU.subtract, w=(te,))
        tzr = V(ve.memset, tmpR, 0.0, w=(te,))
        tzb = V(ve.memset, bc, 0.0, w=(te,))
        tzm = V(ve.memset, MR, 0.0, w=(te,))
        mst = sb("mst", [64, 8])
        mls = sb("mls", [64, 8])
        tzs = V(ve.memset, mst[:, :], 0.0)
        tzl = V(ve.memset, mls[:, :], 0.0)
        ORD = ((0, 1, 2, 3), (1, 0, 3, 2))
        for d in range(2):
            p0 = 32 * d
            for c in range(4):
                a, e = c * 128, (c + 1) * 128
                cut = slice(a, e) if d == 0 else slice(e - 1, a - 1 if a else None, -1)
                t = V(ve.tensor_tensor_scan, bc[p0:p0 + 4, cut], rF[p0:p0 + 4, cut], tmpR[p0:p0 + 4, cut],
                      0.0, ALU.add, ALU.add, w=(te, tzr, tzb))
        t = V(ve.tensor_tensor, uR, rI, bc, ALU.subtract, w=(t,))
        for st in range(4):
            for d in range(2):
                p0 = 32 * d
                c = ORD[d][st]
                a, e = c * 128, (c + 1) * 128
                cut = slice(a, e) if d == 0 else slice(e - 1, a - 1 if a else None, -1)
                end = e - 1 if d == 0 else a
                tm = V(ve.tensor_tensor_scan, MR[p0:p0 + 4, cut], uR[p0:p0 + 4, cut], uR[p0:p0 + 4, cut],
                       mst[p0:p0 + 4, st:st + 1], ALU.max, ALU.max, w=(t, tzs, tzm, tzl))
                tm2 = V(ve.tensor_tensor, mst[p0:p0 + 4, st + 1:st + 2], MR[p0:p0 + 4, end:end + 1],
                        bc[p0:p0 + 4, end:end + 1], ALU.add, w=(tm,))
                tm3 = V(ve.tensor_scalar, mls[p0:p0 + 4, st:st + 1], MR[p0:p0 + 4, end:end + 1], -1.0, None,
                        ALU.mult, w=(tm,))
            t = tm2
        t = V(ve.tensor_tensor, mls[:, 4:8], mst[:, 0:4], mls[:, 0:4], ALU.add, w=(tm2, tm3))
        t_a = A(ae.activation, mls[:, 4:8], mls[:, 4:8], ACT.Exp, w=(t,))
        t = V(ve.tensor_tensor, bc, bc, MR, ALU.add, w=(tm2,))
        t_em = A(ae.activation, bc, bc, ACT.Exp, scale=-1.0, w=(t,))
        for d in range(2):
            p0 = 32 * d
            for st in range(4):
                c = ORD[d][st]
                a, e = c * 128, (c + 1) * 128
                t_wk = A(ae.activation, rI[p0:p0 + 32, a:e], uR[p0:p0 + 32, a:e], ACT.Exp,
                         bias=mls[p0:p0 + 32, st:st + 1], scale=1.0, w=(tm3,))
                t_dc = A(ae.activation, rF[p0:p0 + 32, a:e], MR[p0:p0 + 32, a:e], ACT.Exp,
                         bias=mst[p0:p0 + 32, st:st + 1], scale=-1.0, w=(tm2, te))
        t_nm = V(ve.tensor_scalar, MR, MR, -1.0, None, ALU.mult, w=(t_dc, t_em))
        conv = {"i": 0, "tok": [tz1, tz1], "a": []}

        def qk(f, xT, dst):
            i = conv["i"] % 2
            conv["i"] += 1
            b = feature(lambda k: s.v[:, k, (f % 4) * 128:(f % 4 + 1) * 128], xT, [s.ready] + t_XT + t_XC)
            z = zpad[:, i, :]
            ta = A(ae.activation, z[:, 1:257], b.t[:, 0:256], ACT.Identity, bias=colA[:, 64 + f:65 + f], scale=1.0,
                   w=(b.tk, conv["tok"][i], t_cA))
            b.free = [ta]
            y = cva if i == 0 else cvb
            t = V(ve.tensor_scalar, y, z[:, 0:256], colA[:, 104 + f:105 + f], colB[:, f:f + 1], ALU.mult, ALU.add,
                  w=(ta, t_cB, conv["a"][-2:-1]))
            for j in (1, 2):
                t = V(ve.scalar_tensor_tensor, y, z[:, j:j + 256], colA[:, 104 + 8 * j + f:105 + 8 * j + f], y,
                      ALU.mult, ALU.add, w=(t,))
            conv["tok"][i] = t
            ta = A(ae.activation, dst, y, ACT.Silu, w=(t,))
            conv["a"].append(ta)
            if f >= 4:
                ta = V(ve.tensor_scalar, dst, dst, KS, None, ALU.mult, w=(ta,))
            return ta, b.tk

        for half in range(2):
            s = load((8, 512), [(lambda v: v, w_in[:, :, 256 + half * 512:768 + half * 512])])
            for f in range(4 * half, 4 * half + 4):
                t_qk, tk = qk(f, X, qkT[:, f, :])
                if half:
                    t_qk, tk = qk(f, XCk, qkT[:, f + 4, :])
            s.free = [tk]
        t_q = [V.last(), A.last()]

        s = load((8, 512), [(lambda v: v, w_in[:, :, 1280:1792])])
        for c in range(4):
            src = (XC if c < 2 else XT)
            b = token(lambda k: src[:, k, (c % 2) * 128:(c % 2 + 1) * 128], lambda k: s.v[:, k, :], 512, [s.ready])
            t_v = V(ve.tensor_tensor, vaug[:, c, :, 0:128], b.t[:, :].rearrange("p (h d) -> p h d", h=4),
                    rowb.t[:, 256:768].rearrange("p (h d) -> p h d", h=4), ALU.add, w=(b.tk, tz2, rowb.ready))
            b.free = [t_v]
        s.free = [b.tk]

        s = load((8, 256), [(lambda v: v, w_in[:, :, 0:256])])
        for tt in range(2):
            b = token(lambda k: XT[:, k, tt * 128:(tt + 1) * 128], lambda k: s.v[:, k, :], 256, [s.ready] + t_XT)
            t_p = V(ve.tensor_tensor, ptok[:, tt, :], b.t[:, 0:256], rowb.t[:, 0:256], ALU.add, w=(b.tk, rowb.ready))
            b.free = [t_p]
        s.free = [b.tk]

        s = load((8, 512), [(lambda v: v, w_in[:, :, 1792:2304])])
        for f in range(4):
            b = feature(lambda k: s.v[:, k, f * 128:(f + 1) * 128], X, [s.ready])
            t_so = A(ae.activation, soT[:, f, :], b.t[:, 0:256], ACT.Sigmoid, bias=colA[:, 72 + f:73 + f], scale=1.0,
                     w=(b.tk,))
            b.free = [t_so]
        s.free = [b.tk]

        ts = stats([vs[:, 0, :], vs[:, 1, :]], 1e-5, 0, w=(ta,))
        for tt in range(2):
            t = normal(vs[:, tt, :], vs[:, tt, :], tt, w=(ts,))
            t = V(ve.tensor_tensor, vs[:, tt, :], vs[:, tt, :], rowb.t[:, 1024:1280], ALU.mult, w=(t,))
            t_vs = V(ve.tensor_tensor, vs[:, tt, :], vs[:, tt, :], rowb.t[:, 1280:1536], ALU.add, w=(t,))
        b = bank()
        for g in range(4):
            t = tr(b.t[:, g * 128:(g + 1) * 128], sguw[:, g, :], w=(b.w, t_gl), inc=(g == 3))
        t_ws = V(ve.tensor_copy, wsT[:, :, :].rearrange("p g t -> p (g t)"), b.t[:, :], w=(t,))
        b.free = [t_ws]
        for g in range(4):
            b = bank()
            for n in range(2):
                t = mm(b.t[:, n * 128:(n + 1) * 128], vs[:, n, (g // 2) * 128:(g // 2 + 1) * 128], wsT[:, g, :],
                       True, True, w=(b.w, t_vs, t_ws), inc=(n == 1))
            q0 = (g % 2) * 64
            for n in range(2):
                tv = V(ve.tensor_tensor, sguT[q0:q0 + 64, g // 2, n * 128:(n + 1) * 128],
                       b.t[q0:q0 + 64, n * 128:(n + 1) * 128],
                       rowb.t[q0:q0 + 64, 1536 + g * 128:1536 + (g + 1) * 128], ALU.add, w=(t,))
            b.free = [tv]
            t_sgu = V(ve.tensor_tensor, sguT[q0:q0 + 64, g // 2, :], sguT[q0:q0 + 64, g // 2, :],
                      uT[q0:q0 + 64, g // 2, :], ALU.mult, w=(tv, t_u))
        rowb.free = [t_sgu]

        for g in range(4):
            b = bank()
            for n in range(2):
                t = mm(b.t[:, n * 128:(n + 1) * 128], ptok[:, n, (g // 2) * 128:(g // 2 + 1) * 128],
                       C("pool")[:, g * 128:(g + 1) * 128], True, True, w=(b.w, t_p), inc=(n == 1))
            q0 = (g % 2) * 64
            t_d = V(ve.tensor_copy, dT[q0:q0 + 64, g // 2, :], b.t[q0:q0 + 64, 0:256], w=(t,))
            b.free = [t_d]
        for j in range(2):
            b = bank()
            t = mm(b.t[:, 0:256], poolw[:, j, :], dT[:, j, :], True, True, w=(b.w, t_d, t_gl), inc=True)
            t_pool = V(ve.tensor_scalar, poolT[:, j, :], b.t[:, 0:256], colA[:, 102 + j:103 + j], None, ALU.mult,
                       w=(t,))
            b.free = [t_pool]

        cols = AR[:, 0:768].rearrange("p (a b) -> p a b", a=12)
        lst = [(uR, c) for c in range(4)] + [(rI, c) for c in range(4)] + [(rF, 2), (rF, 3), (bc, 2), (bc, 3)]
        for h in range(2):
            b = bank()
            for i in range(6):
                r, c = lst[h * 6 + i]
                t = tr(b.t[:, i * 64:(i + 1) * 64], r[:, c * 128:(c + 1) * 128], w=(b.w, t_wk, t_dc, t_em),
                       inc=(i == 5), k=64)
            t_cols = V(ve.tensor_copy, cols[:, h * 6:h * 6 + 6, :].rearrange("p a b -> p (a b)"), b.t[:, 0:384],
                       w=(t, t_d, t_sgu))
            b.free = [t_cols]
        aB = sb("aB", [128, 8, 4])
        b = bank()
        sel = C("sel", 64).rearrange("p (r m) -> p r m", r=8)
        for r in range(8):
            t = mm(b.t[:, r * 4:r * 4 + 4], sel[:, r, :], mls[:, 4:8], True, True, w=(b.w, t_a), inc=(r == 7))
        t_aB = V(ve.tensor_copy, aB[:, :, :].rearrange("p a b -> p (a b)"), b.t[:, 0:32], w=(t,))
        b.free = [t_aB]
        for c in range(4):
            b = bank()
            for h in range(4):
                src = qkT[:, (8 if c < 2 else 4) + h, (c % 2) * 128:(c % 2 + 1) * 128]
                t = tr(b.t[:, h * 128:(h + 1) * 128], src, w=(b.w, t_q), inc=(h == 3))
            t_kN = V(ve.tensor_copy, kN[:, c, :, :].rearrange("p a b -> p (a b)"), b.t[:, :], w=(t,))
            b.free = [t_kN]

        SG = []
        mgs = {}

        RR = nc.alloc_sbuf_tensor_at("RR", [128, 2048 * UNITS], FR, offset=ring_at)
        XTR = nc.alloc_sbuf_tensor_at("XTR", [128, 8, 256], FR, offset=xt_at)
        state["slot"] = 4
        hx_ = lease(2048, lambda view: [], pin=True)
        w2 = lease(4096, lambda view: [], pin=True)
        XTH = RR[:, hx_.at * 2048:(hx_.at + 1) * 2048].rearrange("p (a b) -> p a b", a=8)
        t = A(ae.activation, XTH, XT[:, :, :], ACT.Copy, w=(hx_.frees, t_XT))
        t_xh = V(ve.tensor_tensor, XTR[:, :, :], XT[:, :, :], XTH.bitcast(F32), ALU.subtract, w=(t, PE.last()))
        mgb = []
        for i in range(2):
            o = (w2.at + i) * 2048
            mgb.append(Box([RR[:, o + 1024 * a:o + 1024 * (a + 1)].rearrange("p (a b) -> p a b", a=8)
                            for a in range(2)]))
            mgb[i].free = [w2.frees[i]]

        def merge_half(j):
            if j % 2 == 0:
                mgs["s"] = load((8, 256), [(lambda v: v, w_in[:, :, 2832 + j * 128:3088 + j * 128])])
            sm_ = mgs["s"]
            h, l_ = mgb[j % 2].t
            src = sm_.v[:, :, (j % 2) * 128:(j % 2 + 1) * 128]
            t = A(ae.activation, h, src, ACT.Copy, w=(sm_.ready, mgb[j % 2].free))
            mgb[j % 2].tk = V(ve.tensor_tensor, l_, src, h.bitcast(F32), ALU.subtract, w=(t, mgb[j % 2].free))
            if j % 2:
                sm_.free = [mgb[j % 2].tk]

        merge_half(0)

        def merge_gate(j):
            if j < 23:
                merge_half(j + 1)
            hb = mgb[j % 2]
            b = bank()
            for k in range(8):
                PE(pe.matmul, b.t[:, 0:256], hb.t[0][:, k, :], XTH[:, k, :], w=(b.w, hb.tk, t_xh), inc=False,
                   start=(k == 0), stop=False)
                PE(pe.matmul, b.t[:, 0:256], hb.t[0][:, k, :], XTR[:, k, :], inc=False, start=False, stop=False)
                b.tk = PE(pe.matmul, b.t[:, 0:256], hb.t[1][:, k, :], XTH[:, k, :], inc=(k == 7), start=False,
                          stop=(k == 7))
            hb.free = [b.tk]
            t = A(ae.activation, sig[:, j, :], b.t[:, 0:256], ACT.Identity, bias=colA[:, 78 + j:79 + j], scale=1.0,
                  w=(b.tk, t_cA))
            SG.append(t)
            b.free = [t]

        rest = [lambda part=part, h=h: ada_cols(part, h) for part in (3, 4) for h in range(2)]
        rest += [lambda part=part, g=g, h=h: ada_rows(part, g, h) for part, g in ((2, 0), (5, 1)) for h in range(2)]
        for j in range(24):
            FILL.append(lambda j=j: merge_gate(j))
            if j % 3 == 1:
                FILL.append(rest[j // 3])
        CT = arena(8, 129, reset=15380)
        Et = [arena(128, reset=7168), arena(128)]
        SC = [arena(128), arena(128)]
        vw = [arena(129) for _ in range(2)]
        nd = [arena(129) for _ in range(2)]
        assert ar["at"] <= 8196
        tmpI = [arena(129, reset=3584), arena(129)]
        hsum = arena(2, 4, 128, reset=4096)
        dn = sb("dn", [128, 32])
        vw_free = [None, None]
        ct_tok = [None] * 8
        ct_use = [None] * 8
        et_free = [None, None]
        sc_free = [None, None]
        nd_tok = [None, None]
        ti_free = [None, None]
        cnt = {"u": 0, "o": 0}
        hs_tok = {}

        def col(kind, r):
            j = 32 * (r // 4) + r % 4
            return cols[:, kind, j:j + 1]

        def update(r, st):
            d, h = r // 4, r % 4
            c = ORD[d][st]
            i = cnt["u"] % 2
            cnt["u"] += 1
            tw = A(ae.activation, vw[i], vaug[:, c, h, :], ACT.Copy, scale=col(4 + c, r), w=(vw_free[i], t_v, t_cols))
            b = bank()
            t = mm(b.t[:, 0:129], kN[:, c, h, :], vw[i], True, True, w=(b.w, tw, t_kN), inc=True)
            vw_free[i] = t
            if st == 0:
                tv = V(ve.tensor_copy, CT[:, r, :], b.t[:, 0:129], w=(t,))
            else:
                tv = V(ve.scalar_tensor_tensor, CT[:, r, :], CT[:, r, :], aB[:, r, st:st + 1], b.t[:, 0:129],
                       ALU.mult, ALU.add, w=(t, ct_tok[r], ct_use[r], t_aB))
            b.free = [tv]
            ct_tok[r] = tv

        def output(r, st):
            d, h = r // 4, r % 4
            c = ORD[d][st]
            n = c - 2
            i = cnt["o"] % 2
            j = cnt["o"]
            cnt["o"] += 1
            tc = slice(n * 128, (n + 1) * 128)
            bD = bank()
            mm(bD.t[:, 0:128], sel[:, r, :], MR[:, c * 128:(c + 1) * 128], True, False, w=(bD.w, t_nm))
            t = mm(bD.t[:, 0:128], C("ident"), C("maskf" if d == 0 else "maskb"), False, True, inc=True)
            tE = A(ae.activation, Et[i], bD.t[:, 0:128], ACT.Exp, bias=col(c, r), scale=1.0, w=(t, et_free[i]))
            bD.free = [tE]
            bS = bank()
            t = mm(bS.t[:, 0:128], qkT[:, 4 + h, tc], qkT[:, h, tc], True, True, w=(bS.w, t_q), inc=True)
            tS = V(ve.tensor_tensor, SC[i], bS.t[:, 0:128], Et[i], ALU.mult, w=(t, tE, sc_free[i]))
            bS.free = [tS]
            et_free[i] = tS
            bI = bank()
            t = mm(bI.t[:, 0:129], qkT[:, h, tc], CT[:, r, :], True, True, w=(bI.w, ct_tok[r]), inc=True)
            ct_use[r] = t
            tI = A(ae.activation, tmpI[i], bI.t[:, 0:129], ACT.Copy, scale=col(8 + n, r), w=(t, ti_free[i]))
            bI.free = [tI]
            fill()
            bN = bank()
            t = mm(bN.t[:, 0:129], SC[i], vaug[:, c, h, :], True, True, w=(bN.w, tS), inc=True)
            sc_free[i] = t
            t = V(ve.tensor_tensor, nd[i], bN.t[:, 0:129], tmpI[i], ALU.add, w=(t, tI, nd_tok[i]))
            bN.free = [t]
            ti_free[i] = t
            den = nd[i][:, 128:129]
            t = V(ve.scalar_tensor_tensor, dn[:, j:j + 1], den, -1.0, den, ALU.mult, ALU.max, w=(t,))
            t = V(ve.tensor_tensor, dn[:, j:j + 1], dn[:, j:j + 1], col(10 + n, r), ALU.max, w=(t,))
            t = V(ve.reciprocal, dn[:, j:j + 1], dn[:, j:j + 1], w=(t,))
            if (h, n) not in hs_tok:
                t = V(ve.tensor_scalar, hsum[:, n, h, :], nd[i][:, 0:128], dn[:, j:j + 1], None, ALU.mult, w=(t,))
            else:
                t = V(ve.scalar_tensor_tensor, hsum[:, n, h, :], nd[i][:, 0:128], dn[:, j:j + 1], hsum[:, n, h, :],
                      ALU.mult, ALU.add, w=(t, hs_tok[(h, n)]))
            hs_tok[(h, n)] = t
            nd_tok[i] = t

        for st in range(4):
            for r in range(8):
                if st >= 2:
                    output(r, st)
                if st < 3:
                    update(r, st)
                if st < 2 and r % 2:
                    fill()
        t_hs = V.last()
        mlT = arena(4, 256, reset=0)
        ts = stats([hsum[:, n, h, :] for n in range(2) for h in range(4)], 1e-6, 0, w=(t_hs,))
        for n in range(2):
            for h in range(4):
                t = normal(hsum[:, n, h, :], hsum[:, n, h, :], n * 4 + h, w=(ts,))
        fill(len(FILL))
        hx_.free = w2.free = mgb[1].free
        for h in range(4):
            b = bank()
            for n in range(2):
                tk = tr(b.t[:, n * 128:(n + 1) * 128], hsum[:, n, h, :], w=(b.w, t), inc=(n == 1))
            t_ml = V(ve.scalar_tensor_tensor, mlT[:, h, :], b.t[:, 0:256], colB[:, 8 + h:9 + h], soT[:, h, :],
                     ALU.mult, ALU.mult, w=(tk, t_so, t_cB))
            b.free = [t_ml]

        rowg.free = [MD["g", 0], MD["g", 1]]
        yT = arena(8, 256, reset=8196)
        for br in range(3):
            ts = A(ae.activation, sig[:, 8 * br:8 * br + 8, :], sig[:, 8 * br:8 * br + 8, :], ACT.Sigmoid, w=(SG,))
        wb = [T[n][0].rearrange("(k p) n -> p k n", p=128) for n in ("w_br_pool", "w_br_mlstm", "w_br_sgu")]
        yt = [arena(256, reset=5120), arena(256)]
        ty = [None, None]
        for half in range(2):
            cs = slice(half * 512, (half + 1) * 512)
            s = load((8, 512), [(lambda v: v[:, 0:2, :], wb[0][:, :, cs]), (lambda v: v[:, 2:6, :], wb[1][:, :, cs]),
                                (lambda v: v[:, 6:8, :], wb[2][:, :, cs])])
            for f in range(4):
                j = half * 4 + f
                tprev = None
                for br, (k0, kn, src) in enumerate(((0, 2, poolT), (2, 4, mlT), (6, 2, sguT))):
                    b = feature(lambda k: s.v[:, k0 + k, f * 128:(f + 1) * 128], lambda k: src[:, k, :],
                                [s.ready, t_ml, t_pool, t_sgu], kk=kn)
                    if br == 0:
                        tprev = V(ve.tensor_tensor, yT[:, j, :], b.t[:, 0:256], sig[:, j, :], ALU.mult, w=(b.tk, ts))
                        b.free = [tprev]
                    else:
                        i = br - 1
                        t = V(ve.tensor_tensor, yt[i], b.t[:, 0:256], sig[:, 8 * br + j, :], ALU.mult,
                              w=(b.tk, ts, ty[i]))
                        b.free = [t]
                        tprev = G(ge.tensor_tensor, yT[:, j, :], yT[:, j, :], yt[i], ALU.add, w=(t, tprev))
                        ty[i] = tprev
            s.free = [b.tk]
        t_y = tprev
        w_out = T["w_out"][0].rearrange("(k p) n -> p k n", p=128)

        xtmp = arena(2, 1024, reset=0)
        rtmp = arena(2, 1024)

        def dense(xT, wsrc, w, kk=8):
            ss = [load((8, 512), [(lambda v: v, wsrc[:, :, h * 512:(h + 1) * 512])]) for h in range(2)]
            for tt in range(2):
                for h in range(2):
                    b = token(lambda k: xT[k][:, tt * 128:(tt + 1) * 128], lambda k: ss[h].v[:, k, :], 512,
                              [ss[h].ready, w])
                    if tt == 1:
                        ss[h].free = [b.tk]
                    yield tt, h, b

        def close(alpha, gate, w, lng, lnb, parts, then=None):
            r = load_rows([row(lng), row(lnb)])
            ta, done = {}, {}
            for tt, h, b in parts:
                cs_ = slice(h * 512, (h + 1) * 512)
                x_ = xtok[:, tt, cs_]
                if gate is None:
                    t = V(ve.scalar_tensor_tensor, x_, x_, alpha, b.t[:, :], ALU.mult, ALU.add, w=(b.tk, w))
                    b.free = [t]
                else:
                    t = V(ve.tensor_tensor, rtmp[:, tt, cs_], b.t[:, :], gate[:, cs_], ALU.mult, w=(b.tk, w))
                    b.free = [t]
                    t = V(ve.scalar_tensor_tensor, x_, x_, alpha, rtmp[:, tt, cs_], ALU.mult, ALU.add, w=(t,))
                ta[(tt, h)] = V(ve.bn_stats, st6[:, 2 * tt + h, :], x_, w=(t,))
                if h == 1:
                    norm_tile(tt, [ta[(tt, 0)], ta[(tt, 1)]], r, done)
                    if then is not None:
                        then(tt, [done[(tt, 0)], done[(tt, 1)]])
            r.free = [done[k] for k in done]
            return done

        def norm_tile(tt, toks, r, done):
            t = V(ve.bn_aggr, mv[:, tt, :], st6[:, 2 * tt:2 * tt + 2, :], w=(toks,))
            te = V(ve.tensor_scalar, rstd[:, tt:tt + 1], mv[:, tt, 1:2], 1e-5, None, ALU.add, w=(t,))
            tp = G(ge.tensor_tensor, rstd[:, tt:tt + 1], rstd[:, tt:tt + 1], C("nhalf")[:, 0:1], ALU.pow, w=(te,))
            tg = []
            for h in range(2):
                cs_ = slice(h * 512, (h + 1) * 512)
                tg.append(V(ve.scalar_tensor_tensor, xtok[:, tt, cs_], xtok[:, tt, cs_], mv[:, tt, 0:1],
                            r.t[:, cs_], ALU.subtract, ALU.mult, w=(te, r.ready)))
            for h in range(2):
                cs_ = slice(h * 512, (h + 1) * 512)
                done[(tt, h)] = V(ve.scalar_tensor_tensor, xtok[:, tt, cs_], xtok[:, tt, cs_], rstd[:, tt:tt + 1],
                                  r.t[:, 1024 + h * 512:1536 + h * 512], ALU.mult, ALU.add, w=(tg[h], tp))

        def turn_x(done):
            got = []
            for tt in range(2):
                for h in range(2):
                    b = bank()
                    for q in range(4):
                        tk = tr(b.t[:, q * 128:(q + 1) * 128], xtok[:, tt, (4 * h + q) * 128:(4 * h + q + 1) * 128],
                                w=(b.w, done[(tt, h)]), inc=(q == 3))
                    dst = XT[:, 4 * h:4 * h + 4, tt * 128:(tt + 1) * 128]
                    src = b.t[:, :].rearrange("p (a b) -> p a b", a=4)
                    if h:
                        t = A(ae.activation, dst, src, ACT.Copy, w=(tk,))
                    else:
                        t = V(ve.tensor_copy, dst, src, w=(tk,))
                    b.free = [t]
                    got.append(t)
            return got

        keys = [(tt, h) for tt in range(2) for h in range(2)]

        tn_ = {}

        def again(tt, w):
            b = 4 + 2 * tt
            for h in range(2):
                t = V(ve.bn_stats, st6[:, b + h, :], xtok[:, tt, h * 512:(h + 1) * 512], w=w)
            t = V(ve.bn_aggr, mv[:, 4 + tt, :], st6[:, b:b + 2, :], w=(t,))
            t = V(ve.tensor_scalar, rstd[:, 4 + tt:5 + tt], mv[:, 4 + tt, 1:2], 1e-5, None, ALU.add, w=(t,))
            t = G(ge.tensor_tensor, rstd[:, 4 + tt:5 + tt], rstd[:, 4 + tt:5 + tt], C("nhalf")[:, 0:1], ALU.pow,
                  w=(t,))
            tn_[tt] = t

        done = close(ALPHA1, gB[:, 0, :], MD["g", 0], T["ln1_g"][0], T["ln1_b"][0],
                     dense([yT[:, k, :] for k in range(8)], w_out, t_y), again)
        keep.free = [t_y]
        odd.free = [PE.last(), V.last(), A.last()]
        t_h = []
        for tt in range(2):
            t = normal(xtmp[:, tt, :], xtok[:, tt, :], 4 + tt, w=(tn_[tt],))
            for k0 in (0, 4):
                b = bank()
                for k in range(4):
                    tk = tr(b.t[:, k * 128:(k + 1) * 128], xtmp[:, tt, (k0 + k) * 128:(k0 + k + 1) * 128],
                            w=(b.w, t), inc=(k == 3))
                for k in range(4):
                    d, s_ = XT[:, k0 + k, tt * 128:(tt + 1) * 128], b.t[:, k * 128:(k + 1) * 128]
                    sc_, sh_ = modT[:, 4, k0 + k, 0:1], modT[:, 3, k0 + k, 0:1]
                    if k0:
                        th = A(ae.activation, d, s_, ACT.Identity, bias=sh_, scale=sc_, w=(tk, MD[3], MD[4]))
                    else:
                        th = V(ve.tensor_scalar, d, s_, sc_, sh_, ALU.mult, ALU.add, w=(tk, MD[3], MD[4]))
                b.free = [th]
                t_h.append(th)
        t_wr = small([(wrt[:, :, :], T["w_router"][0].rearrange("(k p) n -> p k n", p=128))])
        rowr = load_rows([row(T["b_router"][0])])
        barrier()
        t_mk = []
        cw = arena(2, 32, reset=2048)
        cwT = arena(256, p=32)
        lg = arena(2, 32)
        lg2 = arena(2, 32)
        top = arena(2, 8)
        eq = arena(2, 32)
        cs = arena(2, 32)
        zr = arena(2, 32)
        tzz = V(ve.memset, zr, 0.0)
        sm = arena(2, 4)
        bdn = arena(1024, p=32)
        t_bd = small([(bdn, T["b_down"][0])], q=G)
        acc = arena(2, 1024)
        number = sb("number", [1, 32], I32)
        rg = lease(2048, lambda view: [(view[0:32, :], T["b_gate_up"][0])], pin=True)
        bguR, t_bguR = rg.t[0:32, :], rg.ready
        for tt in range(2):
            b = token(lambda k: XT[:, k, tt * 128:(tt + 1) * 128], lambda k: wrt[:, k, :], 32, [t_wr, t_h])
            t = V(ve.tensor_tensor, lg[:, tt, :], b.t[:, 0:32], rowr.t[:, 0:32], ALU.add, w=(b.tk, rowr.ready))
            b.free = [t]
            rowr.free = [t]
            t0 = V(ve.max, top[:, tt, :], lg[:, tt, :], w=(t,))
            v4 = top[:, tt, 3:4]
            tg = V(ve.tensor_scalar, lg2[:, tt, :], lg[:, tt, :], v4, None, ALU.is_gt, w=(t0,))
            tn = V(ve.tensor_reduce, sm[:, tt, 3:4], lg2[:, tt, :], AX.X, ALU.add, w=(tg,))
            tq = V(ve.tensor_scalar, eq[:, tt, :], lg[:, tt, :], v4, None, ALU.is_equal, w=(t0,))
            tc_ = V(ve.tensor_tensor_scan, cs[:, tt, :], eq[:, tt, :], zr[:, tt, :], 0.0, ALU.add, ALU.add,
                    w=(tq, tzz))
            tc_ = V(ve.tensor_scalar, cs[:, tt, :], cs[:, tt, :], sm[:, tt, 3:4], 4.5, ALU.add, ALU.is_lt,
                    w=(tc_, tn))
            tc_ = V(ve.tensor_tensor, eq[:, tt, :], eq[:, tt, :], cs[:, tt, :], ALU.mult, w=(tc_,))
            te2 = V(ve.tensor_tensor, lg2[:, tt, :], lg2[:, tt, :], eq[:, tt, :], ALU.add, w=(tc_,))
            t = V(ve.tensor_scalar, sm[:, tt, 0:1], top[:, tt, 0:1], -1.0, None, ALU.mult, w=(t0,))
            te = A(ae.activation, lg[:, tt, :], lg[:, tt, :], ACT.Exp, bias=sm[:, tt, 0:1], scale=1.0, w=(t, te2))
            t_mk.append(te2)
            t = V(ve.tensor_tensor, cw[:, tt, :], lg[:, tt, :], lg2[:, tt, :], ALU.mult, w=(te, te2))
            t = V(ve.tensor_reduce, sm[:, tt, 1:2], cw[:, tt, :], AX.X, ALU.add, w=(t,))
            t = V(ve.reciprocal, sm[:, tt, 2:3], sm[:, tt, 1:2], w=(t,))
            t_cw = V(ve.tensor_scalar, cw[:, tt, :], cw[:, tt, :], sm[:, tt, 2:3], None, ALU.mult, w=(t,))
        for tt in range(2):
            for c in range(2):
                b = bank()
                for q in range(4):
                    tk = tr(b.t[:, q * 128:(q + 1) * 128], XT[:, 4 * c + q, tt * 128:(tt + 1) * 128],
                            w=(b.w, t_h), inc=(q == 3))
                tn_h = A(ae.activation, xtmp[:, tt, c * 512:(c + 1) * 512], b.t[:, :], ACT.Copy, w=(tk,))
                b.free = [tn_h]

        b = bank()
        for tt in range(2):
            tk = tr(b.t[0:32, tt * 128:(tt + 1) * 128], cw[:, tt, :], w=(b.w, t_cw), inc=(tt == 1))
        t_cwT = V(ve.tensor_copy, cwT, b.t[0:32, 0:256], w=(tk,))
        b.free = [t_cwT]
        b = bank()
        mm(b.t[:, 0:32], C("tri"), lg2[:, 0, :], True, True, w=(b.w, t_mk))
        mm(b.t[:, 32:64], C("ones"), lg2[:, 0, :], True, False)
        mm(b.t[:, 32:64], C("tri"), lg2[:, 1, :], False, True)
        mm(b.t[0:1, 64:96], C("ones")[:, 0:1], lg2[:, 0, :], True, False)
        tk = mm(b.t[0:1, 64:96], C("ones")[:, 0:1], lg2[:, 1, :], False, True, inc=True)
        pos = eq
        for tt in range(2):
            t = V(ve.scalar_tensor_tensor, pos[:, tt, :], b.t[:, 32 * tt:32 * tt + 32], 1.0, lg2[:, tt, :],
                  ALU.add, ALU.mult, w=(tk,))
            t_pos_ = V(ve.tensor_scalar, pos[:, tt, :], pos[:, tt, :], -1.0, None, ALU.add, w=(t,))
        tx = [V(ve.tensor_scalar, cs[0:1, 0, :], b.t[0:1, 64:96], 64.5, None, ALU.is_gt, w=(tk,))]
        for m in (2, 3):
            t = V(ve.tensor_scalar, cs[0:1, 1, :], b.t[0:1, 64:96], 64.0 * m + 0.5, None, ALU.is_gt,
                  w=(tk, tx[-1]))
            tx.append(V(ve.tensor_tensor, cs[0:1, 0, :], cs[0:1, 0, :], cs[0:1, 1, :], ALU.add, w=(t, tx[0])))
        b.free = [tx[-1], t_pos_]
        t_num = V(ve.tensor_copy, number[:, :], cs[0:1, 0, :], w=(tx[-1],))

        hid_at = ar["at"]
        hg = arena(512)
        hgT = [arena(4, 2, 64) for _ in range(2)]
        gt, up, sg = arena(512), arena(512), arena(512)
        hidT = [arena(4, 2, 64) for _ in range(2)]
        selg = arena(2, 64)
        selw = arena(2, 128)
        selT = [arena(2, 128) for _ in range(3)]
        yy = arena(512)
        xt = XT[:, :, :].rearrange("p a b -> p (a b)")
        fhg, fhgT = xt[:, 0:512], xt[:, 512:1024].rearrange("p (a b c) -> p a b c", a=4, b=2)
        fgt, fup = xt[:, 1024:1536], xt[:, 1536:2048]
        fhid = [arena(4, 2, 64) for _ in range(3)]
        fselg = selg2 = arena(2, 64)
        fselw = arena(2, 128)
        fselT = [arena(2, 128) for _ in range(3)]
        iota = C("iota").rearrange("p (m a b) -> p m a b", m=4, a=2)

        acc_tok = {}

        def start_acc():
            for tt in range(2):
                for h in range(2):
                    b = bank()
                    tk = mm(b.t[:, :], cwT[:, tt * 128:(tt + 1) * 128], bdn[:, h * 512:(h + 1) * 512], True, True,
                            w=(b.w, t_cwT, t_bd), inc=True)
                    t = V(ve.tensor_copy, acc[:, tt, h * 512:(h + 1) * 512], b.t[:, :], w=(tk,))
                    acc_tok[(tt, h)] = [t]
                    b.free = [t]

        def select(Vq, e, m, g, wt, w):
            for tt in range(2):
                p_ = pos[:, tt, e:e + 1]
                t1 = Vq(ve.tensor_scalar, g[:, tt, :], iota[:, m, 0, :], p_, None, ALU.is_equal, w=(t_pos_, w))
                t2 = Vq(ve.tensor_scalar, wt[:, tt, :], iota[:, m, :, :].rearrange("p a b -> p (a b)"), p_,
                        cw[:, tt, e:e + 1], ALU.is_equal, ALU.mult, w=(t_pos_, t_cw, w))
            return t1, t2

        def turn_selection(P, Vq, b, wt, dst, w):
            for tt in range(2):
                tk = P(pe.transpose, b.t[:, tt * 128:(tt + 1) * 128], wt[:, tt, :], C("ident"), w=(b.w, w),
                       inc=(tt == 1))
            return tk, Vq(ve.tensor_copy, dst.rearrange("p a b -> p (a b)"), b.t[:, 0:256], w=(tk,))

        def gather(P, b, g, w):
            for tt in range(2):
                for h in range(2):
                    tk = P(pe.matmul, b.t[64 * h:64 * h + 64, :], g[:, tt, :], xtmp[:, tt, h * 512:(h + 1) * 512],
                           start=(tt == 0), stop=(tt == 1), skip_group_check=True, w=(b.w, w),
                           inc=(tt == 1 and h == 1))
            return tk

        def four(P, b, src, w):
            for q in range(4):
                tk = P(pe.transpose, b.t[:, q * 128:(q + 1) * 128], src[:, q * 128:(q + 1) * 128], C("ident"),
                       w=(b.w, w), inc=(q == 3))
            return tk

        def gate_up(P, bG, bU, e, xT, ws, w):
            for c in range(4):
                b_ = (bG, bU)[c // 2]
                o = 64 * (c % 2)
                P(pe.matmul, b_.t[o:o + 64, :], C("ident", 32)[:, e:e + 1].broadcast_to((32, 64)),
                  bguR[:, c * 512:(c + 1) * 512], start=True, stop=False, skip_group_check=True,
                  w=(b_.w, w, t_bguR), inc=False)
            toks = []
            for k in range(8):
                s = ws[k]
                for c in range(4):
                    b_ = (bG, bU)[c // 2]
                    o = 64 * (c % 2)
                    tk = P(pe.matmul, b_.t[o:o + 64, :], xT[:, k % 4, k // 4, :], s.v[:, 0, c * 512:(c + 1) * 512],
                           start=False, stop=(k == 7), skip_group_check=True, w=(s.ready,),
                           inc=(c == 3))
                toks.append(tk)
            return toks

        def activate(Vq, Aq, bG, bU, g, u, s_, tk, w):
            t = Vq(ve.tensor_scalar, g, bG.t[:, :], 7.0, None, ALU.min, w=(tk, w))
            tG = t
            ta = Aq(ae.activation, s_, g, ACT.Sigmoid, scale=1.702, w=(t, w))
            tU = Vq(ve.tensor_scalar, u, bU.t[:, :], 7.0, -7.0, ALU.min, ALU.max, w=(tk, w))
            t = Vq(ve.scalar_tensor_tensor, u, u, 1.0, g, ALU.add, ALU.mult, w=(tU,))
            return tG, tU, Vq(ve.tensor_tensor, u, u, s_, ALU.mult, w=(t, ta))

        def down(P, b, hT, ws, w):
            toks = []
            for k in range(8):
                s = ws[k // 2]
                for c in range(2):
                    tk = P(pe.matmul, b.t[64 * c:64 * c + 64, :], hT[:, k % 4, k // 4, :],
                           s.v[:, k % 2, c * 512:(c + 1) * 512], start=(k == 0), stop=(k == 7),
                           skip_group_check=True, w=(b.w, s.ready, w), inc=(k % 2 == 1 and c == 1))
                if k % 2:
                    toks.append(tk)
            return toks

        def spread(P, b, tt, h, sT, y, w):
            return P(pe.matmul, b.t[:, :], sT[64 * h:64 * h + 64, tt, :], y[64 * h:64 * h + 64, :], start=True,
                     stop=True, w=(b.w, w), inc=True)

        def add(Vq, b, tt, h, w):
            a = acc[:, tt, h * 512:(h + 1) * 512]
            return Vq(ve.tensor_tensor, a, a, b.t[:, :], ALU.add, w=(w, acc_tok[(tt, h)]))

        fq = {}

        def side(e):
            if e % 8 == 0 and e not in fq:
                fq[e] = tuple(Queue([sem(f"s_f{n}{e}")]) for n in "pva")
            return fq[e - e % 8]

        def extra(e, body):
            qs = side(e)
            tiles = ([], [], [])
            for m in (3, 2, 1):
                for q in qs:
                    q.items = []
                body(m, *qs)
                done = [q.last() for q in qs if q.count]
                for q, tl_ in zip(qs, tiles):
                    q.items.append((done, None, (), {}, None, 0))
                    tl_.insert(0, q.items)
            for main, tl_ in zip((PE, V, A), tiles):
                main.items.append(((t_num,), None, (), {}, None, 0))
                main.items.append(Branch(number[0:1, e:e + 1], tl_))
            return qs[0].last()

        def prepare(e):
            i = e % 2
            t1, t2 = select(V, e, 0, selg, selw, E.get("sel_free"))
            b = bank()
            E["sel_pe"], t = turn_selection(PE, V, b, selw, selT[e % 3], [t2, E.get(("sc", e - 3))])
            b.free = [t]
            E[("selT", e)] = t
            b = bank()
            tk = gather(PE, b, selg, [t1, t_hx])
            E["sel_free"] = [tk]
            t = V(ve.tensor_copy, hg, b.t[:, :], w=(tk, E.get("hg_free")))
            b.free = [t]
            E[("hg", e)] = t

        def turn_gathered(e):
            b = bank()
            tk = four(PE, b, hg, [E[("hg", e)]])
            E["hg_free"] = tk
            t = A(ae.activation, hgT[e % 2].rearrange("p a b c -> p (a b c)"), b.t[:, :], ACT.Copy,
                  w=(tk, E.get(("gu", e - 2))))
            b.free = [t]
            E[("hgT", e)] = t

        def load_gu(e):
            wgu = T["w_gate_up"][0, e].rearrange("(k p) n -> p k n", p=128)
            return [load((1, 2048), [(lambda v: v, wgu[:, k:k + 1, :])]) for k in range(8)]

        def load_d(e):
            wdn = T["w_down"][0, e].rearrange("(k p) n -> p k n", p=128)
            return [load((2, 1024), [(lambda v: v, wdn[:, 2 * q:2 * q + 2, :])]) for q in range(4)]


        def memory_and_angles():
            s = lease(2048, lambda view: [(view[:, 1024 * tt:1024 * tt + 1024],
                                           T["mem_2"][0, tt * 128:(tt + 1) * 128, :]) for tt in range(2)])
            mtok = s.t.rearrange("p (a b) -> p a b", a=2)
            for k0 in range(0, 8, 2):
                b = bank()
                for k in (k0, k0 + 1):
                    for tt in range(2):
                        j = (k - k0) * 2 + tt
                        tk = tr(b.t[:, j * 128:(j + 1) * 128], mtok[:, tt, k * 128:(k + 1) * 128],
                                w=(b.w, s.ready), inc=(j == 3))
                t = A(ae.activation, memT[:, k0:k0 + 2, :], b.t[:, :].rearrange("p (a b) -> p a b", a=2), ACT.Copy,
                      w=(tk,))
                b.free = [t]
            s.free = [tk]
            E["mT"] = t
            s = lease(1024, lambda view: [(view[0:96, 0:256].bitcast(I32), T["positions_2"].broadcast_to((96, 256)))])
            posi = s.t[0:96, 0:256].bitcast(I32)
            an, kk_ = s.t[0:96, 256:512], s.t[0:96, 512:768]
            t = V(ve.tensor_copy, an, posi, w=(s.ready,))
            t = V(ve.tensor_scalar, an, an, C("freq", 96), None, ALU.mult, w=(t,))
            t = V(ve.tensor_scalar, kk_, an, 1.0 / (2 * np.pi), None, ALU.mult, w=(t,))
            t = V(ve.tensor_scalar, kk_, kk_, 12582912.0, None, ALU.add, w=(t,))
            t = V(ve.tensor_scalar, kk_, kk_, -12582912.0, None, ALU.add, w=(t,))
            rest = 2 * np.pi
            for bits in (5, 13, 21, None):
                part = float(np.float32(rest)) if bits is None else np.floor(rest * 2.0 ** bits) / 2.0 ** bits
                rest -= part
                t = V(ve.scalar_tensor_tensor, an, kk_, -part, an, ALU.mult, ALU.add, w=(t,))
            t = V(ve.tensor_scalar, RS, an, 3.1415925, -3.1415925, ALU.min, ALU.max, w=(t,))
            E["rs"] = A(ae.activation, RS, RS, ACT.Sin, w=(t,))
            t = V(ve.tensor_scalar, an, an, np.pi / 2, None, ALU.add, w=(t,))
            t = V(ve.tensor_scalar, kk_, an, 3.1415927, -2 * np.pi, ALU.is_gt, ALU.mult, w=(t,))
            t = V(ve.tensor_tensor, an, an, kk_, ALU.add, w=(t,))
            t = V(ve.tensor_scalar, RC, an, 3.1415925, -3.1415925, ALU.min, ALU.max, w=(t,))
            E["rc"] = A(ae.activation, RC, RC, ACT.Sin, w=(t,))
            s.free = [t]
            tkb = G(ge.memset, krb[:, :], 0.0)
            E["krb"] = small([(krb[64:96, l:l + 1], T["mix_b_in_2"][l][512:544].rearrange("(a o) -> a o", o=1))
                              for l in range(2)], w=(tkb,))

        krb = sb("krb", [96, 2])
        rq = sb("rq", [128, 8])
        sums = sb("sums", [128, 2, 24])
        assert ar["at"] <= 14460
        RC = AR[0:96, 14460:14716]
        RS = AR[0:96, 14716:14972]
        memT = AR[:, 14972:17020].rearrange("p (a b) -> p a b", a=8)
        E = {}
        t_hx = tn_h
        prepare(0)
        turn_gathered(0)
        for e in range(33):
            if e + 1 < 32:
                prepare(e + 1)
            if e == 1:
                start_acc()
            if e == 4:
                memory_and_angles()
            if e < 32:
                ws = load_gu(e)
                bG, bU = bank(), bank()
                toks = gate_up(PE, bG, bU, e, hgT[e % 2], ws, [E[("hgT", e)]])
                E[("gu", e)] = toks[-1]
                tG, tU, t_act = activate(V, A, bG, bU, gt, up, sg, [toks[-1]], E.get("act_free"))
                bG.free, bU.free = [tG], [tU]

                b1, b2 = bank(), bank()

                ftoks = []

                def first(m, P, Vq, Aq):
                    Z = lambda q: [q.last()] if q.count else []
                    t1, t2 = select(Vq, e, m, fselg, fselw, [])
                    w0 = [b1.w, b2.w]
                    tk, t = turn_selection(P, Vq, b1, fselw, fselT[m - 1], [t2])
                    tk = gather(P, b2, fselg, [t1, t_hx])
                    t = Vq(ve.tensor_copy, fhg, b2.t[:, :], w=(tk,))
                    tk = four(P, b1, fhg, [t])
                    t = Vq(ve.tensor_copy, fhgT.rearrange("p a b c -> p (a b c)"), b1.t[:, :], w=(tk,))
                    ftoks[:] = gate_up(P, b1, b2, e, fhgT, ws, [t])
                    tk = ftoks[-1]
                    _, _, t = activate(Vq, Aq, b1, b2, fgt, fup, fhg, [tk], [])
                    tk = four(P, b1, fup, [t])
                    Vq(ve.tensor_copy, fhid[m - 1].rearrange("p a b c -> p (a b c)"), b1.t[:, :], w=(tk,))

                f1 = extra(e, first)
                b1.free, b2.free = [b1.w, f1], [b2.w, f1]
                for s, tk, fk in zip(ws, toks, ftoks):
                    s.free = [tk, fk]
            if e > 0:
                d = e - 1
                if e == 32:
                    state["slot"] = 7
                    r = load_rows([row(T["ln2_g"][0]), row(T["ln2_b"][0])])
                wd = load_d(d)
                b = bank()
                toks = down(PE, b, hidT[d % 2], wd, [E[("hidT", d)]])
                t_y = A(ae.activation, yy, b.t[:, :], ACT.Copy, w=(toks[-1], E.get("y_free")))
                b.free = [t_y]
            if e + 1 < 32:
                turn_gathered(e + 1)
            if e < 32:
                b = bank()
                tk = four(PE, b, up, [t_act])
                E["act_free"] = [tk]
                t = A(ae.activation, hidT[e % 2].rearrange("p a b c -> p (a b c)"), b.t[:, :], ACT.Copy, w=(tk,))
                b.free = [t]
                E[("hidT", e)] = t
            if e > 0:
                for tt in range(2):
                    for h in range(2):
                        b = bank()
                        tk = spread(PE, b, tt, h, selT[d % 3], yy, [t_y, E[("selT", d)]])
                        t = add(V, b, tt, h, [tk])
                        b.free = [t]
                        acc_tok[(tt, h)] = [t]
                E["y_free"] = tk
                E[("sc", d)] = tk
                b1, b2 = bank(), bank()

                ftoks = []

                def second(m, P, Vq, Aq):
                    ftoks[:] = down(P, b1, fhid[m - 1], wd, [f_prev])
                    tk = ftoks[-1]
                    t = Vq(ve.tensor_copy, fhg, b1.t[:, :], w=(tk,))
                    for tt in range(2):
                        for h in range(2):
                            b_ = (b2, b1)[h]
                            tk = spread(P, b_, tt, h, fselT[m - 1], fhg, [t])
                            t = add(Vq, b_, tt, h, [tk])

                f2 = extra(d, second)
                b1.free, b2.free = [b1.w, f2], [b2.w, f2]
                for k in acc_tok:
                    acc_tok[k] = acc_tok[k] + [f2]
                for s, tk, fk in zip(wd, toks, ftoks):
                    s.free = [tk, fk]
            f_prev = f1
        rg.free = [PE.last(), f2]
        t_moe = [acc_tok[k] for k in acc_tok]
        state["units"] = UNITS - 6
        XH = XTR
        ARR = nc.alloc_sbuf_tensor_at("ARR", [128, 17020], FR, offset=ar_at)
        WST = nc.alloc_sbuf_tensor_at("WST", [128, 6, 2048], FR, offset=ring_at + 4 * 2048 * (UNITS - 6))
        wst = [Box((WST[:, 2 * i, :], WST[:, 2 * i + 1, :])) for i in (2, 1, 0)]
        under = {id(b): units[UNITS - 6 + 2 * i:UNITS - 4 + 2 * i] for b, i in zip(wst, (2, 1, 0))}
        halves_n = [0]

        def halves(src, w):
            b = wst[halves_n[0] % 3]
            halves_n[0] += 1
            free = b.free
            assert free is not None
            if id(b) in under:
                free = [u.free for u in under.pop(id(b))]
                assert None not in free
            b.free = None
            dims = src.shape[1:]
            if len(dims) == 3:
                h, l_ = (x.rearrange("p (a b c) -> p a b c", a=dims[0], b=dims[1]) for x in b.t)
            else:
                h, l_ = (x.rearrange("p (a b) -> p a b", a=dims[0]) for x in b.t)
            b.H, b.L = h, l_
            t = A(ae.activation, h, src, ACT.Copy, w=(w, free))
            b.tk = V(ve.tensor_tensor, l_, src, h.bitcast(F32), ALU.subtract, w=(t, free))
            return b

        def three(o, lh, ll, rh, rl, start, stop, w=(), inc=False):
            PE(pe.matmul, o, lh, rh, w=w, inc=False, start=start, stop=False)
            PE(pe.matmul, o, lh, rl, inc=False, start=False, stop=False)
            return PE(pe.matmul, o, ll, rh, inc=inc, start=False, stop=stop)

        def arr(o, k):
            return ARR[:, o:o + 256 * k].rearrange("p (a b) -> p a b", a=k)

        def feature3(hb, f, XL, w=None):
            b = bank()
            c = slice(f * 128, (f + 1) * 128)
            for k in range(8):
                b.tk = three(b.t[:, 0:256], hb.H[:, k, c], hb.L[:, k, c], XH[:, k, :], XL[:, k, :], k == 0, k == 7,
                             w=(b.w, hb.tk, w), inc=(k == 7))
            return b

        def columns_of(srcs):
            for src in srcs:
                s = load((8, 512), [(lambda v: v, src)])
                for c in range(2):
                    b = halves(s.v[:, :, c * 256:(c + 1) * 256], s.ready)
                    if c:
                        s.free = [b.tk]
                    yield b

        def rows_of(srcs):
            for src in srcs:
                s = load((8, 512), [(lambda v: v, src)])
                for c in range(2):
                    b = halves(s.v[:, 4 * c:4 * c + 4, :], s.ready)
                    if c:
                        s.free = [b.tk]
                    yield b

        def quarters_of(w):
            order = [(c, h) for c in range(2) for h in range(2)]
            ss = []
            for i in range(4):
                while len(ss) < min(i + 3, 4):
                    c, h = order[len(ss)]
                    ss.append(load((4, 512), [(lambda v: v, w[:, 4 * c:4 * c + 4, h * 512:(h + 1) * 512])]))
                b = halves(ss[i].v, ss[i].ready)
                ss[i].free = [b.tk]
                yield b

        def part3(b, xh, xl, hb, tt, c, w):
            ts_ = slice(tt * 128, (tt + 1) * 128)
            for k in range(4):
                kk = 4 * c + k
                b.tk = three(b.t[:, :], xh[:, kk, ts_], xl[:, kk, ts_], hb.H[:, k, :], hb.L[:, k, :], kk == 0,
                             kk == 7, w=(b.w, hb.tk, w), inc=(k == 3))
            return b.tk

        def token3(xh, xl, feed, w0, w1, then):
            bs = {(tt, h): bank() for tt in range(2) for h in range(2)}
            for h in range(2):
                hb = feed.take()
                feed.ahead()
                for tt in range(2):
                    tk = part3(bs[(tt, h)], xh, xl, hb, tt, 0, w0)
                hb.free = [tk]
            pair = [feed.take(), feed.take()]
            for tt in range(2):
                if tt:
                    then()
                for h in range(2):
                    tk = part3(bs[(tt, h)], xh, xl, pair[h], tt, 1, w1)
                    if tt:
                        pair[h].free = [tk]
                    yield tt, h, bs[(tt, h)]

        def turn_halves(done, XL):
            got = []
            for tt in range(2):
                for h in range(2):
                    b = bank()
                    for q in range(4):
                        tk = tr(b.t[:, q * 128:(q + 1) * 128], xtok[:, tt, (4 * h + q) * 128:(4 * h + q + 1) * 128],
                                w=(b.w, done[(tt, h)]), inc=(q == 3))
                    at = (slice(None), slice(4 * h, 4 * h + 4), slice(tt * 128, (tt + 1) * 128))
                    src = b.t[:, :].rearrange("p (a b) -> p a b", a=4)
                    t = A(ae.activation, XH[at], src, ACT.Copy, w=(tk,))
                    t = V(ve.tensor_tensor, XL[at], src, XH[at].bitcast(F32), ALU.subtract, w=(t,))
                    b.free = [t]
                    got.append(t)
            return got

        w_mix = [T["mix_w_in_2"][l].rearrange("(k p) n -> p k n", p=128) for l in range(2)]
        first = Feed(rows_of([w_mix[0][:, :, 0:512]]))
        memT_ = memT
        w_v = [T["xa_w_kv_2"][l].rearrange("(k p) n -> p k n", p=128) for l in range(2)]
        vtok = {0: [], 1: []}

        def load_values(l, hf):
            s_ = load((8, 512), [(lambda v: v, w_v[l][:, :, 1024 + hf * 512:1024 + (hf + 1) * 512])])
            for u in s_.boxes:
                u.pin = True
            vtok[(l, hf)] = s_

        def values(l, hf, tt, w=None):
            s_ = vtok[(l, hf)]
            b = token(lambda k: memT_[:, k, tt * 128:(tt + 1) * 128], lambda k: s_.v[:, k, :], 512,
                      [s_.ready, t_mT])
            t = A(ae.activation, gB[:, tt, hf * 512:(hf + 1) * 512], b.t[:, :], ACT.Copy, w=(b.tk, w))
            vtok[l].append(t)
            b.free = [t]
            if tt == 1:
                s_.free = [b.tk]

        t_mT, t_rs, t_rc, t_krb = E["mT"], E["rs"], E["rc"], E["krb"]
        load_values(0, 0)
        load_values(0, 1)
        values(0, 0, 0)
        values(0, 1, 0)
        done = {}
        for tt in range(2):
            ta = []
            for h in range(2):
                cs_ = slice(h * 512, (h + 1) * 512)
                t = V(ve.tensor_tensor, acc[:, tt, cs_], acc[:, tt, cs_], gB[:, 1, cs_], ALU.mult,
                      w=(acc_tok[(tt, h)], MD["g", 1]))
                t = V(ve.scalar_tensor_tensor, xtok[:, tt, cs_], xtok[:, tt, cs_], ALPHA1, acc[:, tt, cs_], ALU.mult,
                      ALU.add, w=(t,))
                ta.append(V(ve.bn_stats, st6[:, 2 * tt + h, :], xtok[:, tt, cs_], w=(t,)))
            norm_tile(tt, ta, r, done)
        for hf in range(2):
            values(0, hf, 1, ta)
        first.ahead()
        r.free = [done[k] for k in keys]
        base = 0

        def softmax(b, n, width, dst, scale, w):
            t = V(ve.tensor_reduce, sums[:, 0, n:n + 1], b.t[:, 0:width], AX.X, ALU.max, w=(b.tk, w))
            t = V(ve.tensor_scalar, sums[:, 0, n:n + 1], sums[:, 0, n:n + 1], -scale, None, ALU.mult, w=(t,))
            t = A(ae.activation, dst, b.t[:, 0:width], ACT.Exp, bias=sums[:, 0, n:n + 1], scale=scale,
                  accum_out=sums[:, 1, n:n + 1], w=(t, w))
            b.free = [t]
            t2 = V(ve.reciprocal, sums[:, 1, n:n + 1], sums[:, 1, n:n + 1], w=(t,))
            return t, t2

        for l in range(2):
            cL = colL[l]
            XL = arr(base + 4096, 8)
            t_XT = turn_halves(done, XL)
            w_kv = T["xa_w_kv_2"][l].rearrange("(k p) n -> p k n", p=128)
            w_q = T["xa_w_q_2"][l].rearrange("(k p) n -> p k n", p=128)
            cq = arena(2, 2, 256, reset=base)
            otk = AR[:, base:base + 1024].rearrange("p (a b) -> p a b", a=2)
            cT = arena(2, 2, 256)
            pT = [AR[:, base + 1024 + 256 * i:base + 1280 + 256 * i] for i in range(3)]
            kx = arena(8, 256)
            assert ar["at"] == base + 4096
            qh = arena(8, 256, p=96)
            catH, catL = arr(base + 4096, 8), arr(base + 6144, 8)
            Kh = arena(8, 256, p=96)
            va = arena(2, 512)
            hp = arena(4, 286)
            yc = arena(4, 256)
            catB = arena(4, 256)
            tq_ = [arena(2, 256, p=96)]
            krw = AR[:, ar["at"]:ar["at"] + 768].rearrange("p (a b) -> p a b", a=8)
            pr = [arena(256) for _ in range(3)]
            sgc = arena(256)
            vx = gB
            M_ = lambda k: memT[:, k, :]
            kvt = {"k": []}

            def mem_key(hf, f):
                o = hf * 512 + f * 128
                if f % 2 == 0:
                    kvt["s"] = load((8, 256), [(lambda v: v, w_kv[:, :, o:o + 256])])
                s_ = kvt["s"]
                b = feature(lambda k: s_.v[:, k, (f % 2) * 128:(f % 2 + 1) * 128], M_, [s_.ready, t_mT])
                t = A(ae.activation, kx[:, hf * 4 + f, :], b.t[:, 0:256], ACT.Copy, w=(b.tk,))
                kvt["k"].append(t)
                b.free = [t]
                if f % 2:
                    s_.free = [b.tk]

            FILL += [lambda hf=hf, f=f: mem_key(hf, f) for hf in range(2) for f in range(4)]
            rowm = load_rows([row(T["mix_b_in_2"][l], 0, 512)])
            tkz = G(ge.memset, krw, 0.0, w=(t_XT,))
            t_kr = small([(krw[:, :, 64:96], w_mix[l][:, :, 512:544])], w=(tkz,), q=G)
            def conv_in():
                for f2 in range(2):
                    s = load((2, 8, 256), [(lambda v, a=a: v[:, a], w_mix[l][:, :, 544 + 512 * a + 256 * f2:
                                                                     800 + 512 * a + 256 * f2]) for a in range(2)])
                    for c in range(2):
                        b = halves(s.v[:, :, :, c * 128:(c + 1) * 128], s.ready)
                        if c:
                            s.free = [b.tk]
                        yield b

            cin = Feed(conv_in())
            t_h = []
            tsg = None
            tcq = []
            pair = [first.take(), first.take()]
            for tt in range(2):
                b = bank()
                if tt:
                    cin.ahead()
                for c in range(2):
                    tk = part3(b, XH, XL, pair[c], tt, c, t_XT)
                    if tt:
                        pair[c].free = [tk]
                t = V(ve.tensor_tensor, cq[:, tt, :, :].rearrange("p a b -> p (a b)"), b.t[:, :], rowm.t[:, 0:512],
                      ALU.add, w=(b.tk, rowm.ready))
                b.free = [t]
                for a in range(2):
                    tcq.append(A(ae.activation, sgc, cq[:, tt, a, :], ACT.Square,
                                 accum_out=rq[:, tt * 2 + a:tt * 2 + a + 1], w=(t, tcq[-1] if tcq else None)))
            rowm.free = [t]
            t = V(ve.tensor_scalar, rq[:, 0:4], rq[:, 0:4], 1.0 / 256, 1e-6, ALU.mult, ALU.add, w=(tcq,))
            t = G(ge.tensor_tensor, rq[:, 0:4], rq[:, 0:4], C("nhalf")[:, 0:4], ALU.pow, w=(t,))
            for tt in range(2):
                for a in range(2):
                    t2 = V(ve.tensor_scalar, cq[:, tt, a, :], cq[:, tt, a, :], rq[:, tt * 2 + a:tt * 2 + a + 1],
                           None, ALU.mult, w=(t,))
            b = bank()
            for k in range(8):
                mm(b.t[0:96, 0:256], krw[:, k, :], XH[:, k, :].bitcast(F32), k == 0, False, w=(b.w, t_kr, t_XT))
                b.tk = mm(b.t[0:96, 0:256], krw[:, k, :], XL[:, k, :].bitcast(F32), False, k == 7, inc=(k == 7))
            krr = tq_[0]
            t = A(ae.activation, krr[:, 0, :], b.t[0:96, 0:256], ACT.Identity, bias=krb[:, l:l + 1], scale=1.0,
                  w=(b.tk, t_krb))
            b.free = [t]
            b = bank()
            tk = mm(b.t[0:96, 0:256], C("rot", 96), krr[:, 0, :], True, True, w=(b.w, t), inc=True)
            t2 = V(ve.tensor_tensor, krr[:, 1, :], b.t[0:96, 0:256], RS, ALU.mult, w=(tk, t_rs))
            b.free = [t2]
            t3 = V(ve.tensor_tensor, krr[:, 0, :], krr[:, 0, :], RC, ALU.mult, w=(tk, t_rc))
            t3 = V(ve.tensor_tensor, krr[:, 0, :], krr[:, 0, :], krr[:, 1, :], ALU.add, w=(t3, t2))
            for h in range(8):
                t_kh = G(ge.tensor_copy, Kh[64:96, h, :], krr[64:96, 0, :], w=(t3,))
            t_hz = G(ge.memset, hp[:, :, 0:30], 0.0, w=(t_XT,))

            for f in range(4):
                hb = cin.take()
                if f < 3:
                    cin.ahead()
                ba, bg = bank(), bank()
                for b, a in ((ba, 0), (bg, 1)):
                    for k in range(8):
                        b.tk = three(b.t[:, 0:256], hb.H[:, a, k, :], hb.L[:, a, k, :], XH[:, k, :], XL[:, k, :],
                                     k == 0, k == 7, w=(b.w, hb.tk), inc=(k == 7))
                hb.free = [bg.tk]
                t = A(ae.activation, sgc, bg.t[:, 0:256], ACT.Sigmoid, bias=cL[:, 128 + f:129 + f], scale=1.0,
                      w=(bg.tk, tsg, t_cL[l], tcq))
                bg.free = [t]
                t = V(ve.scalar_tensor_tensor, hp[:, f, 30:286], ba.t[:, 0:256], cL[:, 124 + f:125 + f], sgc,
                      ALU.add, ALU.mult, w=(t, ba.tk))
                ba.free = [t]
                tsg = t
                t_h.append(t)
            t_cT = []
            for a in range(2):
                t_cT += turn(cT[:, a], cq[:, :, a, :], [t2], cL[:, 132 + 2 * a:134 + 2 * a], None, chunks=2)
            tcv = [None] * 4

            def tap(j, f):
                if j == 0:
                    tcv[f] = V(ve.tensor_scalar, yc[:, f, :], hp[:, f, 0:256], cL[:, f:f + 1], cL[:, 136 + f:137 + f],
                               ALU.mult, ALU.add, w=(t_h, t_hz))
                else:
                    tcv[f] = V(ve.scalar_tensor_tensor, yc[:, f, :], hp[:, f, j:j + 256],
                               cL[:, 4 * j + f:4 * j + f + 1], yc[:, f, :], ALU.mult, ALU.add, w=(tcv[f],))

            CV = [(j, f) for j in range(31) for f in range(4)]

            def conv_steps(n):
                for _ in range(min(n, len(CV))):
                    tap(*CV.pop(0))

            su = load((3584,), [(lambda v: v[:, 0:1536].rearrange("p (k n) -> p k n", k=2),
                                 T["mla_w_uq_2"][l].rearrange("(k p) n -> p k n", p=128)),
                                (lambda v: v[:, 1536:3584].rearrange("p (k n) -> p k n", k=2),
                                 T["mla_w_ukv_2"][l].rearrange("(k p) n -> p k n", p=128))])
            wuq = su.v[:, 0:1536].rearrange("p (k n) -> p k n", k=2)
            wukv = su.v[:, 1536:3584].rearrange("p (k h n) -> p k h n", k=2, h=8)
            for hh in range(4):
                b = bank()
                for i in range(2):
                    h = 2 * hh + i
                    for k in range(2):
                        tk = mm(b.t[0:64, i * 256:(i + 1) * 256], wukv[:, k, h, 0:64], cT[:, 1, k, :], k == 0,
                                k == 1, w=(b.w, su.ready, t_cT), inc=(i == 1 and k == 1))
                conv_steps(3)
                t_kh2 = A(ae.activation, Kh[0:64, 2 * hh:2 * hh + 2, :],
                          b.t[0:64, :].rearrange("p (a b) -> p a b", a=2), ACT.Copy, w=(tk,))
                b.free = [t_kh2]
            for tt in range(2):
                b = bank()
                for k in range(2):
                    tk = mm(b.t[:, :].rearrange("p (h n) -> p h n", h=8), cT[:, 1, k, tt * 128:(tt + 1) * 128],
                            wukv[:, k, :, 64:128], k == 0, k == 1, w=(b.w, su.ready, t_cT), inc=(k == 1))
                conv_steps(4)
                t_va = A(ae.activation, va[:, tt, :], b.t[:, :], ACT.Copy, w=(tk,))
                b.free = [t_va]
            t_q = t3
            for hh in range(4):
                b = bank()
                for i in range(2):
                    h = 2 * hh + i
                    for k in range(2):
                        tk = mm(b.t[0:96, i * 256:(i + 1) * 256], wuq[:, k, h * 96:(h + 1) * 96], cT[:, 0, k, :],
                                k == 0, k == 1, w=(b.w, su.ready, t_cT), inc=(i == 1 and k == 1))
                conv_steps(4)
                qv = qh[:, 2 * hh:2 * hh + 2, :]
                t = A(ae.activation, qv, b.t[0:96, :].rearrange("p (a b) -> p a b", a=2), ACT.Copy, w=(tk,))
                b.free = [t]
                b = bank()
                tk = mm(b.t[0:96, :], C("rot", 96), qv.rearrange("p a b -> p (a b)"), True, True, w=(b.w, t),
                        inc=True)
                for i in range(2):
                    t2 = V(ve.tensor_tensor, tq_[0][:, i, :], b.t[0:96, i * 256:(i + 1) * 256], RS, ALU.mult,
                           w=(tk, t_rs, t_q, t_kh))
                    t3 = V(ve.tensor_tensor, qv[:, i, :], qv[:, i, :], RC, ALU.mult, w=(tk, t_rc))
                b.free = [t2]
                t_q = V(ve.tensor_tensor, qv, qv, tq_[0], ALU.add, w=(t3, t2))
            su.free = [tk]
            SCL = 96.0 ** -0.5
            t_o = []
            n_ = 0
            prf = [None] * 3
            ptf = [None] * 3
            for j in range(2):
                kn = 128 * (j + 1)
                bo_ = bank()
                bo_.pin = True
                pend = {}
                for step in range(8 + 2):
                    if step < 8:
                        h = step
                        i = n_ % 3
                        b = bank()
                        mm(b.t[:, 0:kn], qh[:, h, j * 128:(j + 1) * 128], Kh[:, h, 0:kn], True, False,
                           w=(b.w, t_q, t_kh, t_kh2))
                        zo = CONST["zero"][0] + 128 * (1 - j)
                        b.tk = mm(b.t[:, 0:kn], C("ident"), cst[:, zo:zo + kn], False, True, inc=True)
                        te, tr_ = softmax(b, j * 8 + h, kn, pr[i][:, 0:kn], SCL, [prf[i]])
                        pend[h] = (i, te, tr_)
                        n_ += 1
                    if 1 <= step < 9:
                        h = step - 1
                        i, te, tr_ = pend[h]
                        b = bank()
                        for m in range(j + 1):
                            tk = tr(b.t[:, m * 128:(m + 1) * 128], pr[i][:, m * 128:(m + 1) * 128], w=(b.w, te),
                                    inc=(m == j))
                        prf[i] = tk
                        t = A(ae.activation, pT[i][:, 0:kn], b.t[:, 0:kn], ACT.Copy, w=(tk, ptf[i]))
                        b.free = [t]
                        pend[h] = (i, t, tr_)
                    if step >= 2:
                        h = step - 2
                        i, t, tr_ = pend[h]
                        for m in range(j + 1):
                            tk = mm(bo_.t[:, h * 64:(h + 1) * 64], pT[i][:, m * 128:(m + 1) * 128],
                                    va[:, m, h * 64:(h + 1) * 64], m == 0, m == j, w=(bo_.w, t, t_va), inc=(m == j))
                        ptf[i] = tk
                    conv_steps(5)
                    if step % 2 and len(FILL) > 2:
                        fill()
                for h in range(8):
                    t = V(ve.tensor_scalar, otk[:, j, h * 64:(h + 1) * 64], bo_.t[:, h * 64:(h + 1) * 64],
                          sums[:, 1, j * 8 + h:j * 8 + h + 1], None, ALU.mult, w=(tk, pend[7][2]))
                bo_.free = [t]
                bo_.pin = False
                t_o.append(t)
            t_cat = []
            for k0 in (0, 2):
                b = bank()
                for k in (k0, k0 + 1):
                    for tt in range(2):
                        i = (k - k0) * 2 + tt
                        tk = tr(b.t[:, i * 128:(i + 1) * 128], otk[:, tt, k * 128:(k + 1) * 128], w=(b.w, t_o),
                                inc=(i == 3))
                src = b.t[:, :].rearrange("p (a b) -> p a b", a=2)
                t = A(ae.activation, catH[:, k0:k0 + 2, :], src, ACT.Copy, w=(tk,))
                t = V(ve.tensor_tensor, catL[:, k0:k0 + 2, :], src, catH[:, k0:k0 + 2, :].bitcast(F32), ALU.subtract,
                      w=(t,))
                b.free = [t]
                t_cat.append(t)
            w_o = T["mix_w_o_2"][l].rearrange("(k p) n -> p k n", p=128)
            f_o = Feed(quarters_of(w_o))
            f_o.ahead()
            f_o.ahead()
            conv_steps(len(CV))
            f_q = Feed(columns_of([w_q[:, :, hf * 512:(hf + 1) * 512] for hf in range(2)]))
            b = bank()
            for f in range(4):
                tk = mm(b.t[:, 0:256], C("mean"), yc[:, f, :], f == 0, f == 3, w=(b.w, tcv[f]), inc=(f == 3))
            tsq = []
            for f in range(4):
                t = V(ve.tensor_tensor, yc[:, f, :], yc[:, f, :], b.t[:, 0:256], ALU.subtract, w=(tk,))
                tsq.append(A(ae.activation, catB[:, f, :], yc[:, f, :], ACT.Square, w=(t,)))
            b.free = [t]
            b = bank()
            for f in range(4):
                tk = mm(b.t[:, 0:256], C("mean"), catB[:, f, :], f == 0, f == 3, w=(b.w, tsq[f]), inc=(f == 3))
            t = V(ve.tensor_scalar, sgc, b.t[:, 0:256], 1e-5, None, ALU.add, w=(tk,))
            b.free = [t]
            t = A(ae.activation, sgc, sgc, ACT.Sqrt, w=(t,))
            t = V(ve.reciprocal, sgc, sgc, w=(t,))
            for f in range(4):
                t2 = V(ve.tensor_tensor, yc[:, f, :], yc[:, f, :], sgc, ALU.mult, w=(t,))
                t_cv = A(ae.activation, catB[:, f, :], yc[:, f, :], ACT.Silu, bias=cL[:, 144 + f:145 + f],
                         scale=cL[:, 140 + f:141 + f], w=(t2, tk))
                t_cv = A(ae.activation, catH[:, 4 + f, :], catB[:, f, :], ACT.Copy, w=(t_cv,))
                t_cv = V(ve.tensor_tensor, catL[:, 4 + f, :], catB[:, f, :], catH[:, 4 + f, :].bitcast(F32),
                         ALU.subtract, w=(t_cv,))
            done = close(ALPHA2, None, None, T["ln1_g_2"][l], T["ln1_b_2"][l],
                         token3(catH, catL, f_o, t_cat, t_cv, f_q.ahead))
            fill(len(FILL))

            qx = arena(8, 256, reset=base + 4096)
            oxH, oxL = arr(base + 6144, 8), arr(base + 8192, 8)
            pr = [arena(256, reset=base + 10240)] + [arena(256) for _ in range(3)]
            pT = [arena(2, 256) for _ in range(2)]
            t_kx, t_vx = kvt["k"], vtok[l]
            XL = arr(base + 12288, 8)
            t_XT = turn_halves(done, XL)
            w_o = T["xa_w_o_2"][l].rearrange("(k p) n -> p k n", p=128)
            f_o = Feed(quarters_of(w_o))
            f_q.ahead()
            for i in range(4):
                hb = f_q.take()
                if i < 2:
                    f_q.ahead()
                else:
                    f_o.ahead()
                for f in range(2):
                    b = feature3(hb, f, XL, t_XT)
                    t_qx = A(ae.activation, qx[:, 2 * i + f, :], b.t[:, 0:256], ACT.Copy, w=(b.tk,))
                    b.free = [t_qx]
                hb.free = [b.tk]
            t_oxs = []
            if l == 0:
                load_values(1, 0)
            prf = [None] * 4
            ptf = [None] * 2
            pend = {}
            for step in range(4 + 2):
                if step < 4:
                    h = step
                    for j in range(2):
                        i = (2 * h + j) % 4
                        b = bank()
                        for c in range(2):
                            b.tk = mm(b.t[:, 0:256], qx[:, 2 * h + c, j * 128:(j + 1) * 128], kx[:, 2 * h + c, :],
                                      c == 0, c == 1, w=(b.w, t_qx, t_kx), inc=(c == 1))
                        te, tr_ = softmax(b, 16 + 2 * h + j, 256, pr[i], 1.0 / 16, [prf[i]])
                        pend[(h, j)] = V(ve.tensor_scalar, pr[i], pr[i],
                                         sums[:, 1, 16 + 2 * h + j:17 + 2 * h + j], None, ALU.mult, w=(te, tr_))
                if 1 <= step < 5:
                    h = step - 1
                    b = bank()
                    for j in range(2):
                        i = (2 * h + j) % 4
                        for m in range(2):
                            tk = tr(b.t[:, m * 256 + j * 128:m * 256 + (j + 1) * 128],
                                    pr[i][:, m * 128:(m + 1) * 128], w=(b.w, pend[(h, j)]), inc=(m == 1))
                        prf[i] = tk
                    t = V(ve.tensor_copy, pT[h % 2].rearrange("p a b -> p (a b)"), b.t[:, :], w=(tk, ptf[h % 2]))
                    b.free = [t]
                    pend[h] = t
                if step >= 2:
                    h = step - 2
                    for d in range(2):
                        b = bank()
                        o0 = h * 256 + d * 128
                        for m in range(2):
                            tk = mm(b.t[:, 0:256], vx[:, m, o0:o0 + 128], pT[h % 2][:, m, :], m == 0, m == 1,
                                    w=(b.w, t_vx, pend[h]), inc=(m == 1))
                        t_ox = A(ae.activation, oxH[:, 2 * h + d, :], b.t[:, 0:256], ACT.Copy, w=(tk,))
                        t_ox = V(ve.tensor_tensor, oxL[:, 2 * h + d, :], b.t[:, 0:256],
                                 oxH[:, 2 * h + d, :].bitcast(F32), ALU.subtract, w=(t_ox,))
                        b.free = [t_ox]
                        t_oxs.append(t_ox)
                    ptf[h % 2] = tk
            w_f = T["ffn_w_in_2"][l].rearrange("(k p) n -> p k n", p=128)
            w_d = T["ffn_w_down_2"][l].rearrange("(k p) n -> p k n", p=128)

            def ff_boxes(w_f, w_d):
                for q in range(11):
                    s = load((2, 8, 256), [(lambda v, a=a: v[:, a], w_f[:, :, 2816 * a + q * 256:
                                                                        2816 * a + (q + 1) * 256]) for a in range(2)])
                    for g2 in range(2):
                        b = halves(s.v[:, :, :, g2 * 128:(g2 + 1) * 128], s.ready)
                        if g2:
                            s.free = [b.tk]
                        yield b
                for q in range(6):
                    kn = 4 if q < 5 else 2
                    s = load((kn, 1024), [(lambda v: v, w_d[:, 4 * q:4 * q + kn, :])])
                    for c in range(kn // 2):
                        b = halves(s.v[:, 2 * c:2 * c + 2, :], s.ready)
                        if 2 * c + 2 == kn:
                            s.free = [b.tk]
                        yield b

            ff = Feed(ff_boxes(w_f, w_d))
            done = close(ALPHA2, None, None, T["ln2_g_2"][l], T["ln2_b_2"][l],
                         token3(oxH, oxL, f_o, t_oxs[3], t_oxs[7], ff.ahead))
            if l == 0:
                for tt in range(2):
                    values(1, 0, tt)

            ffH, ffL, XL = arr(base, 22), arr(base + 5632, 22), arr(base + 11264, 8)
            t_XT = turn_halves(done, XL)
            arena(1, reset=base + 13312)
            sl = [arena(256) for _ in range(2)]
            fp_ = [arena(256) for _ in range(2)]
            slf, fpf = [None] * 2, [None] * 2
            for f in range(22):
                hb = ff.take()
                ff.ahead()
                i = f % 2
                bg, bu = bank(), bank()
                for b, a in ((bg, 0), (bu, 1)):
                    for k in range(8):
                        b.tk = three(b.t[:, 0:256], hb.H[:, a, k, :], hb.L[:, a, k, :], XH[:, k, :], XL[:, k, :],
                                     k == 0, k == 7, w=(b.w, hb.tk, t_XT), inc=(k == 7))
                hb.free = [bu.tk]
                t = A(ae.activation, sl[i], bg.t[:, 0:256], ACT.Silu, w=(bg.tk, slf[i]))
                bg.free = [t]
                t = V(ve.tensor_tensor, fp_[i], bu.t[:, 0:256], sl[i], ALU.mult, w=(t, bu.tk, fpf[i]))
                bu.free = [t]
                slf[i] = t
                t = A(ae.activation, ffH[:, f, :], fp_[i], ACT.Copy, w=(t,))
                t_f = V(ve.tensor_tensor, ffL[:, f, :], fp_[i], ffH[:, f, :].bitcast(F32), ALU.subtract, w=(t,))
                fpf[i] = t_f
            bb = {(tt, h): bank() for h in range(2) for tt in range(2)}
            def down_part(c, k, tt, h, hb, inc):
                kk, b = 2 * c + k, bb[(tt, h)]
                tc_, hc_ = slice(tt * 128, (tt + 1) * 128), slice(h * 512, (h + 1) * 512)
                b.tk = three(b.t[:, :], ffH[:, kk, tc_], ffL[:, kk, tc_], hb.H[:, k, hc_], hb.L[:, k, hc_],
                             kk == 0, kk == 21, w=(b.w, hb.tk, t_f), inc=inc)
                return b.tk

            for c in range(9):
                hb = ff.take()
                ff.ahead()
                for k in range(2):
                    for tt, h in keys:
                        tk = down_part(c, k, tt, h, hb, k == 1)
                hb.free = [tk]
            if l == 0:
                load_values(1, 1)
            two = [ff.take(), ff.take()]
            if l == 0:
                first = Feed(rows_of([w_mix[1][:, :, 0:512]]))
                first.ahead()
            for tt, h in keys:
                for c in (9, 10):
                    for k in range(2):
                        tk = down_part(c, k, tt, h, two[c - 9], k == 1)
                    two[c - 9].free = [tk]
            done = close(ALPHA2, None, None, T["ln3_g_2"][l], T["ln3_b_2"][l],
                         [(tt, h, bb[(tt, h)]) for tt, h in keys])
            if l == 0:
                for tt in range(2):
                    values(1, 1, tt)
        return finish(nc, ctx, PE, V, A, G, SP, out, xtok, sem)


def finish(nc, ctx, PE, V, A, G, SP, out, xtok, sem):
    s = sem("s_out")
    toks = [q.last() for q in (PE, V, A, G) if q.count]
    for tt in range(2):
        SP.items.append((toks, nc.sync.dma_start, (out[0, tt * 128:(tt + 1) * 128, :], xtok[:, tt, :]), {}, s, 16))
    SP.items.append(((( s, 32),), None, (), {}, None, 0))
    block = ctx.enter_context(nc.Block())

    @block.sync
    def _(eng):
        emit(eng, SP.items)

    @block.gpsimd
    def _(eng):
        emit(eng, G.items)

    @block.scalar
    def _(eng):
        emit(eng, A.items)

    @block.vector
    def _(eng):
        emit(eng, V.items)

    @block.tensor
    def _(eng):
        emit(eng, PE.items)


_INS = ["x", "c", "ctx", "c_ctx", "w_ada", "b_ada", "w_in", "b_in", "pool_w", "pool_scale", "qk_conv_w", "qk_conv_b",
        "mlstm_norm_g", "sgu_ln_g", "sgu_ln_b", "sgu_w", "sgu_b", "w_br_pool", "w_br_mlstm", "w_br_sgu", "w_out",
        "ln1_g", "ln1_b", "w_router", "b_router", "w_gate_up", "b_gate_up", "w_down", "b_down", "ln2_g", "ln2_b",
        "mem_2", "positions_2", "mix_w_in_2", "mix_b_in_2", "mla_q_norm_2", "mla_w_uq_2", "mla_kv_norm_2",
        "mla_w_ukv_2", "conv_dw_w_2", "conv_dw_b_2", "conv_norm_g_2", "conv_norm_b_2", "mix_w_o_2", "ln1_g_2",
        "ln1_b_2", "xa_w_q_2", "xa_w_kv_2", "xa_w_o_2", "ln2_g_2", "ln2_b_2", "ffn_w_in_2", "ffn_w_down_2",
        "ln3_g_2", "ln3_b_2"]


def kernel(**inputs):
    import concourse.bacc as bacc
    from concourse.bass_utils import run_bass_kernel_spmd

    nc = bacc.Bacc("TRN2", target_bir_lowering=False, num_devices=1)
    arrays, T = {}, {}
    for name in _INS:
        a = np.ascontiguousarray(inputs[name])
        arrays["in_" + name] = a
        T[name] = nc.dram_tensor("in_" + name, a.shape, mybir.dt.from_np(a.dtype), kind="ExternalInput").ap()
    arrays["in_const"] = constants()
    T["const"] = nc.dram_tensor("in_const", arrays["in_const"].shape, F32, kind="ExternalInput").ap()
    out = nc.dram_tensor("out_0", (1, 256, 1024), F32, kind="ExternalOutput").ap()
    build(nc, T, out)
    r = run_bass_kernel_spmd(nc, [arrays], core_ids=[0])
    return r.results[0]["out_0"]
```
